# Optimizing a Trainium2 kernel written in Bass

```python
import jax, jax.numpy as jnp
from jax import lax
import numpy as np

D_MODEL = 1024
BATCH = 1
SEQ = 1024
DEPTH = 1

GRID_W = 64
NA_HEAD_DIM = 64
NA_WIDTH = D_MODEL // 2
NA_HEADS = NA_WIDTH // NA_HEAD_DIM
NA_WIN_ROWS = 8
NA_WIN_COLS = 16
LRU_WIDTH = D_MODEL // 2
LRU_BLOCKS = 8
LRU_BLOCK_W = LRU_WIDTH // LRU_BLOCKS
LRU_C = 8.0
CONV_W = 4
FNET_WIDTH = D_MODEL // 2
FNET_GROUPS = 4
FNET_GROUP_W = FNET_WIDTH // FNET_GROUPS
N_BRANCH = 3
IN_COLS = 3 * NA_WIDTH + 2 * LRU_WIDTH + FNET_WIDTH
N_EXPERTS = 32
N_EXPERT_GROUPS = 8
EXPERTS_PER_GROUP = N_EXPERTS // N_EXPERT_GROUPS
TOP_K = 2
D_EXPERT = D_MODEL // 2
MOE_BLOCK = 128
EPS = 1e-6

kernel_name = "hybrid_na_rglru_fnet_moe_encoder"

def rmsnorm(x, g):
    xf = x.astype(jnp.float32)
    y = xf * lax.rsqrt(jnp.mean(xf * xf, axis=-1, keepdims=True) + EPS)
    return (y * g.astype(jnp.float32)).astype(x.dtype)

def modulate(h, shift, scale):
    return h * (1.0 + scale[:, None, :]) + shift[:, None, :]

def neighbourhood_attention(q, k, v, rpb):
    B, T, H, dh = q.shape
    rows = T // GRID_W
    kr = min(NA_WIN_ROWS, rows)
    kc = NA_WIN_COLS
    qg = q.reshape(B, rows, GRID_W, H, dh)
    kg = k.reshape(B, rows, GRID_W, H, dh)
    vg = v.reshape(B, rows, GRID_W, H, dh)
    cols = jnp.arange(GRID_W)
    col_start = jnp.clip(cols - kc // 2, 0, GRID_W - kc)
    col_idx = col_start[:, None] + jnp.arange(kc)[None, :]
    col_bias_idx = col_idx - cols[:, None] + (NA_WIN_COLS - 1)
    scale = dh ** -0.5

    def row_block(r):
        rs = jnp.clip(r - kr // 2, 0, rows - kr)
        q_r = lax.dynamic_index_in_dim(qg, r, axis=1, keepdims=False)
        k_band = lax.dynamic_slice_in_dim(kg, rs, kr, axis=1)
        v_band = lax.dynamic_slice_in_dim(vg, rs, kr, axis=1)
        k_win = k_band[:, :, col_idx]
        v_win = v_band[:, :, col_idx]
        row_bias_idx = rs + jnp.arange(kr) - r + (NA_WIN_ROWS - 1)
        bias = rpb[:, row_bias_idx[:, None, None], col_bias_idx[None, :, :]]
        bias = bias.transpose(0, 2, 1, 3).astype(jnp.float32)
        s = jnp.einsum('bwhd,brwjhd->bhwrj', q_r, k_win).astype(jnp.float32) * scale + bias[None]
        p = jax.nn.softmax(s.reshape(B, H, GRID_W, kr * kc), axis=-1).reshape(B, H, GRID_W, kr, kc)
        return jnp.einsum('bhwrj,brwjhd->bwhd', p.astype(v.dtype), v_win)

    out = lax.map(row_block, jnp.arange(rows))
    return out.transpose(1, 0, 2, 3, 4).reshape(B, T, H * dh)

def centred_dwconv(x, w, b):
    T = x.shape[1]
    left = CONV_W // 2
    right = CONV_W - 1 - left
    xp = jnp.pad(x, ((0, 0), (left, right), (0, 0)))
    y = xp[:, 0:T] * w[0]
    for j in range(1, CONV_W):
        y = y + xp[:, j:j + T] * w[j]
    return y + b

def block_diag(x, w, b):
    B, T, _ = x.shape
    xb = x.reshape(B, T, LRU_BLOCKS, LRU_BLOCK_W)
    return jnp.einsum('btni,nij->btnj', xb, w).reshape(B, T, LRU_WIDTH) + b

def rglru_scan(x, w_r, b_r, w_i, b_i, lam, reverse):
    xf = x.astype(jnp.float32)
    r = jax.nn.sigmoid(block_diag(x, w_r, b_r).astype(jnp.float32))
    i = jax.nn.sigmoid(block_diag(x, w_i, b_i).astype(jnp.float32))
    log_a = -LRU_C * r * jax.nn.softplus(-lam.astype(jnp.float32))
    a = jnp.exp(log_a)
    bx = jnp.sqrt(-jnp.expm1(2.0 * log_a)) * (i * xf)

    def combine(c1, c2):
        a1, b1 = c1
        a2, b2 = c2
        return a1 * a2, a2 * b1 + b2

    _, h = lax.associative_scan(combine, (a, bx), reverse=reverse, axis=1)
    return h

def fourier_mix(f):
    B, T, _ = f.shape
    fg = f.astype(jnp.float32).reshape(B, T, FNET_GROUPS, FNET_GROUP_W)
    y = jnp.fft.fft2(fg, axes=(1, 3), norm='ortho').real
    return y.reshape(B, T, FNET_WIDTH).astype(f.dtype)

def route(u, w_router, router_bias):
    N = u.shape[0]
    scores = jax.nn.sigmoid(jnp.dot(u.astype(jnp.float32), w_router.astype(jnp.float32)))
    sel = scores + router_bias.astype(jnp.float32)
    sel_g = sel.reshape(N, N_EXPERT_GROUPS, EXPERTS_PER_GROUP)
    group_score = lax.top_k(sel_g, TOP_K)[0].sum(axis=-1)
    _, g_idx = lax.top_k(group_score, 1)
    cand = jnp.take_along_axis(sel_g, g_idx[:, :, None], axis=1)[:, 0]
    _, local = lax.top_k(cand, TOP_K)
    e_idx = g_idx * EXPERTS_PER_GROUP + local
    w = jnp.take_along_axis(scores, e_idx, axis=1)
    w = w / jnp.sum(w, axis=-1, keepdims=True)
    return e_idx, w

def moe_ffn(u, w_router, router_bias, w_gate, w_up, w_down):
    B, T, D = u.shape
    N = B * T
    uf = u.reshape(N, D)
    e_idx, gw = route(uf, w_router, router_bias)
    A = N * TOP_K
    flat_e = e_idx.reshape(A)
    flat_tok = jnp.repeat(jnp.arange(N, dtype=jnp.int32), TOP_K)
    flat_w = gw.reshape(A)
    order = jnp.argsort(flat_e)
    sorted_e = flat_e[order]
    counts = jnp.bincount(flat_e, length=N_EXPERTS)
    starts = jnp.cumsum(counts) - counts
    padded = (counts + MOE_BLOCK - 1) // MOE_BLOCK * MOE_BLOCK
    padded_end = jnp.cumsum(padded)
    padded_start = padded_end - padded
    dest = padded_start[sorted_e] + (jnp.arange(A) - starts[sorted_e])
    n_blocks = -(-(A + N_EXPERTS * (MOE_BLOCK - 1)) // MOE_BLOCK)
    P = n_blocks * MOE_BLOCK
    buf_tok = jnp.zeros((P,), jnp.int32).at[dest].set(flat_tok[order])
    buf_w = jnp.zeros((P,), jnp.float32).at[dest].set(flat_w[order])
    block_e = jnp.minimum(
        jnp.searchsorted(padded_end, jnp.arange(n_blocks) * MOE_BLOCK, side='right'), N_EXPERTS - 1)
    xb = uf[buf_tok].reshape(n_blocks, MOE_BLOCK, D)

    def expert_block(args):
        xblk, e = args
        h = jax.nn.silu(xblk @ w_gate[e]) * (xblk @ w_up[e])
        return h @ w_down[e]

    yb = lax.map(expert_block, (xb, block_e)).reshape(P, D)
    y = jax.ops.segment_sum(yb * buf_w[:, None].astype(yb.dtype), buf_tok, num_segments=N)
    return y.reshape(B, T, D)

def setup_inputs(seed: int = 0) -> dict:
    key = jax.random.key(seed)
    ks = jax.random.split(key, 32)
    L, D = DEPTH, D_MODEL
    f32 = jnp.float32

    def nrm(k, shape, fan_in, s=1.0):
        return jax.random.normal(k, shape, f32) * (s * fan_in ** -0.5)

    def small(k, shape, s=0.02):
        return jax.random.normal(k, shape, f32) * s

    u_lam = jax.random.uniform(ks[16], (L, 2, LRU_WIDTH), f32, minval=0.9, maxval=0.999)
    a_lam = u_lam ** (1.0 / LRU_C)
    lru_lambda = jnp.log(a_lam) - jnp.log1p(-a_lam)
    return {
        "x": jax.random.normal(ks[0], (BATCH, SEQ, D), f32),
        "c": jax.random.normal(ks[1], (BATCH, D), f32),
        "ada_w": nrm(ks[2], (L, D, 6 * D), D, 0.5),
        "ada_b": small(ks[3], (L, 6 * D)),
        "norm_mix_g": 1.0 + small(ks[4], (L, D), 0.05),
        "norm_ffn_g": 1.0 + small(ks[5], (L, D), 0.05),
        "w_in": nrm(ks[6], (L, D, IN_COLS), D),
        "w_branch_gate": nrm(ks[7], (L, D, N_BRANCH * D), D),
        "b_branch_gate": small(ks[8], (L, N_BRANCH * D)),
        "na_rpb": small(ks[9], (L, NA_HEADS, 2 * NA_WIN_ROWS - 1, 2 * NA_WIN_COLS - 1), 0.1),
        "lru_conv_w": nrm(ks[10], (L, CONV_W, LRU_WIDTH), CONV_W),
        "lru_conv_b": small(ks[11], (L, LRU_WIDTH)),
        "lru_w_r": nrm(ks[12], (L, 2, LRU_BLOCKS, LRU_BLOCK_W, LRU_BLOCK_W), LRU_BLOCK_W),
        "lru_b_r": small(ks[13], (L, 2, LRU_WIDTH)),
        "lru_w_i": nrm(ks[14], (L, 2, LRU_BLOCKS, LRU_BLOCK_W, LRU_BLOCK_W), LRU_BLOCK_W),
        "lru_b_i": small(ks[15], (L, 2, LRU_WIDTH)),
        "lru_lambda": lru_lambda,
        "w_proj_na": nrm(ks[17], (L, NA_WIDTH, D), NA_WIDTH),
        "w_proj_lru": nrm(ks[18], (L, LRU_WIDTH, D), LRU_WIDTH),
        "w_proj_fnet": nrm(ks[19], (L, FNET_WIDTH, D), FNET_WIDTH),
        "w_out": nrm(ks[20], (L, D, D), D),
        "w_router": nrm(ks[21], (D, N_EXPERTS), D),
        "router_bias": small(ks[22], (N_EXPERTS,), 0.01),
        "w_exp_gate": nrm(ks[23], (L, N_EXPERTS, D, D_EXPERT), D),
        "w_exp_up": nrm(ks[24], (L, N_EXPERTS, D, D_EXPERT), D),
        "w_exp_down": nrm(ks[25], (L, N_EXPERTS, D_EXPERT, D), D_EXPERT),
        "final_g": 1.0 + small(ks[26], (D,), 0.05),
    }

def reference(x, c, ada_w, ada_b, norm_mix_g, norm_ffn_g, w_in, w_branch_gate, b_branch_gate,
              na_rpb, lru_conv_w, lru_conv_b, lru_w_r, lru_b_r, lru_w_i, lru_b_i, lru_lambda,
              w_proj_na, w_proj_lru, w_proj_fnet, w_out, w_router, router_bias,
              w_exp_gate, w_exp_up, w_exp_down, final_g):
    B, T, D = x.shape
    c_act = jax.nn.silu(c)
    splits = [NA_WIDTH, 2 * NA_WIDTH, 3 * NA_WIDTH, 3 * NA_WIDTH + LRU_WIDTH, 3 * NA_WIDTH + 2 * LRU_WIDTH]
    for l in range(DEPTH):
        mod = c_act @ ada_w[l] + ada_b[l]
        sh_mix, sc_mix, gt_mix, sh_ffn, sc_ffn, gt_ffn = jnp.split(mod, 6, axis=-1)

        u = modulate(rmsnorm(x, norm_mix_g[l]), sh_mix, sc_mix)
        proj = u @ w_in[l]
        q, k, v, xr, yr, fr = jnp.split(proj, splits, axis=-1)

        hs = (B, T, NA_HEADS, NA_HEAD_DIM)
        y_na = neighbourhood_attention(q.reshape(hs), k.reshape(hs), v.reshape(hs), na_rpb[l])

        xc = centred_dwconv(xr, lru_conv_w[l], lru_conv_b[l])
        h = (rglru_scan(xc, lru_w_r[l, 0], lru_b_r[l, 0], lru_w_i[l, 0], lru_b_i[l, 0], lru_lambda[l, 0], False)
             + rglru_scan(xc, lru_w_r[l, 1], lru_b_r[l, 1], lru_w_i[l, 1], lru_b_i[l, 1], lru_lambda[l, 1], True))
        y_lru = (h * jax.nn.gelu(yr.astype(jnp.float32))).astype(x.dtype)

        y_f = fourier_mix(fr)

        gates = jax.nn.sigmoid(u @ w_branch_gate[l] + b_branch_gate[l])
        g_na, g_lru, g_f = jnp.split(gates, N_BRANCH, axis=-1)
        merged = (g_na * (y_na @ w_proj_na[l])
                  + g_lru * (y_lru @ w_proj_lru[l])
                  + g_f * (y_f @ w_proj_fnet[l]))
        x = x + gt_mix[:, None, :] * (merged @ w_out[l])

        u2 = modulate(rmsnorm(x, norm_ffn_g[l]), sh_ffn, sc_ffn)
        x = x + gt_ffn[:, None, :] * moe_ffn(u2, w_router, router_bias, w_exp_gate[l], w_exp_up[l], w_exp_down[l])
    return rmsnorm(x, final_g)


_drawn_inputs = setup_inputs


def setup_inputs(seed=0):
    import zlib

    import numpy as np

    out = dict(_drawn_inputs(seed))
    spreads = {}
    factors = {'b_branch_gate': 5.615, 'na_rpb': 7.632, 'lru_b_r': 29.321, 'lru_b_i': 8.0}
    for name, (base, spread) in spreads.items():
        noise = np.random.default_rng([zlib.crc32(name.encode()), seed]).standard_normal(out[name].shape)
        drawn = base * np.exp(spread * noise) if base else spread * noise
        out[name] = __import__('jax').numpy.asarray(drawn.astype(out[name].dtype))
    for name, factor in factors.items():
        out[name] = (out[name] * factor).astype(out[name].dtype)
    return out
```

```python
import concourse.bass as bass
from concourse import mybir
from contextlib import ExitStack
import numpy as np

D = 1024
T = 1024
P = 128
TT = T // P
KC = D // P
HALF = 512
GRID_W, ROWS = 64, 16
DH = 64
HEADS = 8
PAIRS = HEADS // 2
WIN_R, WIN_C = 8, 16
NREL = 2 * WIN_R - 1
RELC = 2 * WIN_C - 1
RPAD = 128
BW = 512
BC = BW // P
GROUPS = 4
NE, NG, EPG = 32, 8, 4
FE = 512
FC = FE // P
CAP = 128
NBLK = 2048 // CAP + NE
LIST = NBLK + 1
EPS = 1e-6
NEG = -1e30
PRIME = 2


def done(n):
    return n + 1 + PRIME


class Chain:

    def __init__(self, eng, sem):
        self.eng, self.sem, self.n, self.dyn = eng, sem, 0, None

    def mark(self, ins):
        ins.then_inc(self.sem, 1)
        self.n += 1

    def sync(self):
        self.eng.wait_ge(self.sem, self.n if self.dyn is None else self.dyn + self.n)

    def __call__(self, ins):
        self.mark(ins)
        self.sync()

    def enter(self, turn, per):
        self.base, self.per, self.dyn = self.n, per, turn * per

    def leave(self, turns):
        assert self.n - self.base == self.per, (self.n - self.base, self.per)
        self.n, self.dyn = self.base + self.per * turns, None


def band(r):
    return min(max(r - WIN_R // 2, 0), ROWS - WIN_R)


def build(nc, x, c, ada_w, ada_b, norm_mix_g, norm_ffn_g, w_in, w_branch_gate, b_branch_gate,
          na_rpb, lru_conv_w, lru_conv_b, lru_w_r, lru_b_r, lru_w_i, lru_b_i, lru_lambda,
          w_proj_na, w_proj_lru, w_proj_fnet, w_out, w_router, router_bias,
          w_exp_gate, w_exp_up, w_exp_down, final_g,
          k_ident, k_window, k_before, k_chan, k_cos, k_sin, k_nyq, out):
    f32, f32r, i32, bf16 = mybir.dt.float32, mybir.dt.float32r, mybir.dt.int32, mybir.dt.bfloat16
    ALU, ACT, AX = mybir.AluOpType, mybir.ActivationFunctionType, mybir.AxisListType
    ADD, SUB, MUL = ALU.add, ALU.subtract, ALU.mult

    ctx = ExitStack()
    with ctx:
        ctx.enter_context(nc.allow_non_contiguous_dma("small parameter vectors are laid channel-major"))
        base = (nc.sbuf_base + 63) // 64 * 64

        def at(name, kb, shape, dt=f32):
            return nc.alloc_sbuf_tensor_at(name, shape, dt, offset=base + int(kb * 1024))

        def sem(name):
            return ctx.enter_context(nc.semaphore(name))

        xn = at("xn", 96, [P, TT, D])
        ada = [at(f"ada{i}", kb, [P, KC, HALF]) for i, kb in enumerate((128, 144, 80))]
        junk = at("junk", 64, [P, D])
        modtmp = at("modtmp", 68, [P, D])
        crep = at("crep", 72, [P, KC, P])
        mrow = at("mrow", 195, [1, 2, D])
        u_hi = at("u_hi", 0, [P, KC, T], f32r)
        u_lo = at("u_lo", 32, [P, KC, T], f32r)
        u_full = [at(f"u_full{i}", 76 + 2 * i, [P, HALF]) for i in range(2)]
        y_na = at("y_na", 64, [P, BC, T])
        lx = at("lx", 80, [P, 3, BC, T])
        qT = at("qT", 128, [P, 2, T])
        kT = at("kT", 136, [P, 2, T])
        vT = at("vT", 144, [P, T])
        vtok = at("vtok", 148, [P, 2, 15, P])
        bias = at("bias", 163, [P, 2, NREL * GRID_W])
        window = at("window", 170.5, [P, GRID_W])
        w_raw = [at(f"w_raw{i}", 171 + 4 * i, [P, KC, P]) for i in range(2)]
        w_hi = [at(f"w_hi{i}", 179 + 4 * i, [P, KC, P], f32r) for i in range(2)]
        w_lo = [at(f"w_lo{i}", 187 + 4 * i, [P, KC, P], f32r) for i in range(2)]
        prob = [at(f"prob{i}", 195 + 2 * i, [P, HALF]) for i in range(2)]
        probT = [at(f"probT{i}", 199 + 2 * i, [P, 4, P]) for i in range(2)]
        q_bd = [at(f"q_bd{i}", 203 + 0.5 * i, [P, P]) for i in range(2)]
        o_bd = [at(f"o_bd{i}", 204 + 0.5 * i, [P, P]) for i in range(2)]
        rpb_pad = at("rpb_pad", 195, [HEADS * NREL, RPAD])
        t_cos = at("t_cos", 128, [P, TT, HALF])
        t_sin = at("t_sin", 144, [P, TT, HALF])
        z = at("z", 160, [P, TT, 2 * P])
        chan = at("chan", 168, [P, 2 * P])
        t_nyq = at("t_nyq", 169, [P, TT])
        sin_part = at("sin_part", 198, [P, HALF])
        xc = at("xc", 170, [P, T])
        lt = [at(f"lt{i}", 174 + 4 * i, [P, T]) for i in range(4)]
        bd = at("bd", 190, [P, 16, P])
        zero_row = at("zero_row", 203, [P, HALF])
        merged = at("merged", 128, [P, KC, T])
        w_pr = [at(f"w_pr{i}", 160 + 2 * i, [P, BC, P]) for i in range(3)]
        gate = [at(f"gate{i}", 166 + 2 * i, [P, HALF]) for i in range(2)]
        part = at("part", 195, [P, HALF])
        x1 = at("x1", 0, [P, TT, D])
        xn2 = at("xn2", 32, [P, TT, D])
        wo = at("wo", 160, [P, 2, KC, HALF])
        gmix = at("gmix", 192, [P, D])
        u2T = at("u2T", 196, [P, KC, P])
        mixed = at("mixed", 200, [P, HALF])
        wr = at("wr", 202, [P, KC, NE])
        wg = [at(f"wg{i}", 64 + 48 * i, [P, KC, FE]) for i in range(2)]
        wu = [at(f"wu{i}", 80 + 48 * i, [P, KC, FE]) for i in range(2)]
        wd = [at(f"wd{i}", 96 + 48 * i, [P, FC, D]) for i in range(2)]
        xg = at("xg", 160, [P, D])
        xgT = at("xgT", 168, [P, KC, P])
        act = at("act", 172, [P, FE])
        actT = at("actT", 174, [P, FC, P])
        yb = at("yb", 176, [P, D])
        y0 = [at(f"y0_{i}", 64 + 8 * i, [P, D]) for i in range(2)]
        y1 = [at(f"y1_{i}", 68 + 8 * i, [P, D]) for i in range(2)]
        gffn = at("gffn", 80, [P, D])
        fing = at("fing", 84, [P, D])
        res = [at(f"res{i}", 88 + 4 * i, [P, D]) for i in range(2)]
        junk2 = at("junk2", 96, [P, D])

        NM = ["score", "sel", "hit", "wgt", "rank", "slot", "ta", "tb"]
        dd = {n: at("r_" + n, 128 + i, [P, TT, NE]) for i, n in enumerate(NM)}
        hit_b = at("hit_b", 136, [P, TT, NE], bf16)
        before_b = at("before_b", 137, [P, P], bf16)
        ones_b = at("ones_b", 137.5, [P, P], bf16)
        before = at("before", 138, [P, P])
        rbias = at("rbias", 138.5, [P, NE])
        cnt = at("cnt", 138.75, [P, 4, NE + 1])
        pairt = at("pairt", 139.5, [P, 8, TT, NG])
        slot_f = at("slot_f", 141.5, [P, 2, TT])
        slot_t = at("slot_t", 141.75, [P, 2, TT], i32)
        slot_u = at("slot_u", 142, [P, 2, TT], i32)
        gidx = at("gidx", 142.25, [P, NG])

        cur = [205.0]

        def small(name, shape, dt=f32):
            n = 1
            for s in shape[1:]:
                n *= s
            t = at(name, cur[0], shape, dt)
            cur[0] += (n * 4 + 31) // 32 * 32 / 1024
            assert base + cur[0] * 1024 <= nc.sbuf_usable_end, name
            return t

        ident = small("ident", [P, P])
        cvec = small("cvec", [P, KC])
        cact = small("cact", [P, KC])
        ms = small("ms", [P, TT])
        rstd = small("rstd", [P, TT])
        mod_b = small("mod_b", [P, 6, KC])
        norm_g = small("norm_g", [P, 2, KC])
        modv = small("modv", [P, 6, KC])
        u_scale = small("u_scale", [P, 2, KC])
        nmax = small("nmax", [P, 2])
        rsum = small("rsum", [P, 2])
        rinv = small("rinv", [P, 2])
        conv_w = small("conv_w", [P, 4, BC])
        conv_b = small("conv_b", [P, BC])
        lru_b = small("lru_b", [P, 4, BC])
        lam = small("lam", [P, 2, BC])
        lam_t = small("lam_t", [P, 4, 2, BC])
        decay = small("decay", [P, 2, BC])
        bg = small("bg", [P, 3 * KC])
        ms2 = small("ms2", [P, TT])
        rstd2 = small("rstd2", [P, TT])
        tok_cur = small("tok_cur", [P, 1], i32)
        tok = small("tok", [P, TT], i32)
        tokl = small("tokl", [P, LIST], i32)
        pair_w = small("pair_w", [P, 2, TT])
        pair_s = small("pair_s", [P, 2, TT], i32)
        starts = small("starts", [1, NE + 1], i32)
        zero_i = small("zero_i", [P, LIST], i32)

        ps = ctx.enter_context(nc.psum_tensor("ps", [P, 8, HALF], f32))

        d_rpb = nc.dram_tensor("d_rpb", (HEADS * NREL, RPAD), f32, kind="Internal")
        d_gt = nc.dram_tensor("d_gt", (2, D), f32, kind="Internal").ap()
        d_xn2 = nc.dram_tensor("d_xn2", (T, D), f32, kind="Internal").ap()
        d_list = nc.dram_tensor("d_list", (P * LIST, 1), i32, kind="Internal").ap()
        d_y = nc.dram_tensor("d_y", (NBLK * CAP, D), f32, kind="Internal").ap()

        held = sem("held")
        ch_dve, ch_act, ch_pool = sem("ch_dve"), sem("ch_act"), sem("ch_pool")
        ld_const, ld_small = sem("ld_const"), sem("ld_small")
        ld_x = [sem(f"ld_x{t}") for t in range(TT)]
        ld_ada = [sem(f"ld_ada{i}") for i in range(3)]
        ada_used = sem("ada_used")
        cact_ready, crep_ready, ms_ready, root_ready, xn_ready = (sem(n) for n in ("cact_ready", "crep_ready", "ms_ready", "root_ready", "xn_ready"))
        mod_ps, mod_read, gt_saved = (sem(n) for n in ("mod_ps", "mod_read", "gt_saved"))
        xt_ps, xt_full, u_hi_ready, u_ready = (sem(n) for n in ("xt_ps", "xt_full", "u_hi_ready", "u_ready"))
        ld_w = [sem(f"ld_w{i}") for i in range(2)]
        w_split, job_half, job_evac = sem("w_split"), sem("job_half"), sem("job_evac")
        vt_ps, vt_evac = sem("vt_ps"), sem("vt_evac")
        q_staged, s_ps, s_biased, p_ready, pt_ps, pt_ready, o_ps, o_ready, ot_ps, y_ready = (sem("at_" + n) for n in (
            "q_staged", "s_ps", "s_biased", "p_ready", "pt_ps", "pt_ready", "o_ps", "o_ready", "ot_ps", "y_ready"))
        rpb_set, rpb_in, rpb_out, bias_ready = (sem(n) for n in ("rpb_set", "rpb_in", "rpb_out", "bias_ready"))
        ld_bias = sem("ld_bias")
        bd_zero, ld_bd, ld_dft = sem("bd_zero"), sem("ld_bd"), sem("ld_dft")
        lam_exp, lam_ln, lam_in, decay_ready = (sem(n) for n in ("lam_exp", "lam_ln", "lam_in", "decay_ready"))
        gelu_ready, xc_ready, lru_ps, lru_read, lru_free, lru_act, lru_rad, lru_root, lru_done = (sem(n) for n in (
            "gelu_ready", "xc_ready", "lru_ps", "lru_read", "lru_free", "lru_act", "lru_rad", "lru_root", "lru_done"))
        z_ps, z_ready, f_ps, f_sin, f_done = (sem(n) for n in ("z_ps", "z_ready", "f_ps", "f_sin", "f_done"))
        ld_pr = [sem(f"ld_pr{i}") for i in range(3)]
        pr_ps, gated = sem("pr_ps"), sem("gated")
        ld_wo = [sem(f"ld_wo{i}") for i in range(2)]
        ld_x1 = [sem(f"ld_x1{t}") for t in range(TT)]
        ld_out = sem("ld_out")
        mo_ps, x1_half, ms2_ready, root2, xn2_ready, x2t_ps, u2_ready, ro_ps = (sem(n) for n in (
            "mo_ps", "x1_half", "ms2_ready", "root2", "xn2_ready", "x2t_ps", "u2_ready", "ro_ps"))
        st_xn2, st_zero = sem("st_xn2"), sem("st_zero")
        consts_up, ld_rt, score_ready, hit_ready, rank_ps, slots_ready, starts_ready, st_list, ld_list, tok_ready = (sem(n) for n in (
            "consts_up", "ld_rt", "score_ready", "hit_ready", "rank_ps", "slots_ready", "starts_ready", "st_list", "ld_list", "tok_ready"))
        ld_g = [sem(f"ld_g{i}") for i in range(2)]
        ld_u = [sem(f"ld_u{i}") for i in range(2)]
        ld_d = [sem(f"ld_d{i}") for i in range(2)]
        exp_used = sem("exp_used")
        ld_xg, xg_ps, xg_ready, g_ps, h_ps, silu_ready, h_ready, ht_ps, ht_ready, y_ps, y_evac, st_y, gath = (sem("e_" + n) for n in (
            "ld_xg", "xg_ps", "xg_ready", "g_ps", "h_ps", "silu", "h_ready", "ht_ps", "ht_ready", "y_ps", "y_evac", "st_y", "gath"))
        zero_set, st_pad = sem("zero_set"), sem("st_pad")
        ld_end, fin_ms, fin_root, fin_ready, fin_ready_x, ch_end = (sem(n) for n in ("ld_end", "fin_ms", "fin_root", "fin_ready", "fin_ready_x", "ch_end"))
        ld_y = [sem(f"ld_y{i}") for i in range(2)]
        st_out = [sem(f"st_out{i}") for i in range(2)]

        chan_major = lambda v: v.rearrange("(p c) -> p c", c=KC)
        chunked = lambda v: v.rearrange("(c p) -> p c", p=P)
        ada_v = ada_w[0].rearrange("(p c) n -> p c n", c=KC)
        w_in_v = w_in[0].rearrange("(p c) n -> p c n", c=KC)
        w_bg_v = w_branch_gate[0].rearrange("(p c) n -> p c n", c=KC)
        x_v = x[0].rearrange("(t p) d -> p t d", p=P)
        out_v = out[0].rearrange("(t p) d -> p t d", p=P)
        proj_v = [w[0].rearrange("(c p) n -> p c n", p=P) for w in (w_proj_na, w_proj_fnet, w_proj_lru)]
        wo_v = w_out[0].rearrange("(c p) n -> p c n", p=P)
        wr_v = w_router.rearrange("(p c) n -> p c n", c=KC)
        wg_v = w_exp_gate[0].rearrange("e (p c) n -> e p c n", c=KC)
        wu_v = w_exp_up[0].rearrange("e (p c) n -> e p c n", c=KC)
        wd_v = w_exp_down[0].rearrange("e (p c) n -> e p c n", c=FC)
        xn2_d = d_xn2.rearrange("(t p) d -> p t d", p=P)

        PRO, PER, LAST = 3, 6, 3
        KIND0 = [0, BW, 2 * BW]
        KIND1 = [3 * BW, 4 * BW, 5 * BW]
        GATE0 = PRO + PER * (PAIRS - 1) + LAST
        BRANCH = [0, 2 * D, D]
        VT0 = 9
        MM = 24
        HF = [slice(0, HALF), slice(HALF, T)]
        BACK = [slice(63, None, -1), slice(127, 63, -1)]

        def finish_unit(n_jobs, i, h):
            return (MM * (2 * i + h + 1) - 1) // (n_jobs * 2 * MM // ROWS)

        GATED_ALL = 6 * KC + PRIME
        PR_PRIME = 6
        ATT_ALL = done(PAIRS * ROWS - 1)

        def load_expert(q, e, s):
            q.dma_start(wg[s][:], wg_v[e]).then_inc(ld_g[s], 16)
            q.dma_start(wu[s][:], wu_v[e]).then_inc(ld_u[s], 16)
            q.dma_start(wd[s][:], wd_v[e]).then_inc(ld_d[s], 16)

        def hold(eng):
            eng.sem_inc(held, 1)

        block = ctx.enter_context(nc.Block())

        @block.sync
        def _(sp):
            def load_w(k, par, cols):
                sp.wait_ge(w_split, k - 1)
                sp.dma_start(w_raw[par][:], cols).then_inc(ld_w[par], 16)

            for dst, src in ((cvec[:], c[0].rearrange("(p c) -> p c", c=KC)), (ident[:], k_ident), (window[:], k_window),
                             (mod_b[:], ada_b[0].rearrange("(v p c) -> p v c", v=6, c=KC)),
                             (norm_g[:, 0, :], chan_major(norm_mix_g[0])), (norm_g[:, 1, :], chan_major(norm_ffn_g[0])),
                             (mrow[:, 0, :], ada_b[0:1, 2 * D:3 * D]), (mrow[:, 1, :], ada_b[0:1, 5 * D:6 * D])):
                sp.dma_start(dst, src).then_inc(ld_const, 16)
            for t in range(TT):
                sp.dma_start(xn[:, t, :], x_v[:, t, :]).then_inc(ld_x[t], 16)
            for b in range(12):
                if b >= 3:
                    sp.wait_ge(ada_used, b - 2)
                sp.dma_start(ada[b % 3][:], ada_v[:, :, b * HALF:(b + 1) * HALF]).then_inc(ld_ada[b % 3], 16)
            for i in range(PRO):
                cols = w_in_v[:, :, KIND0[i]:KIND0[i] + P]
                if i < 2:
                    sp.dma_start(w_raw[i % 2][:], cols).then_inc(ld_w[i % 2], 16)
                else:
                    load_w(i, i % 2, cols)
            sp.wait_ge(mod_read, 6)
            sp.dma_start(d_gt.rearrange("(o a) n -> o a n", o=1), mrow[:]).then_inc(gt_saved, 16)
            sp.wait_ge(gt_saved, 16)
            sp.wait_ge(rpb_set, 1)
            sp.dma_start(rpb_pad[:, 48:48 + RELC], na_rpb[0].rearrange("h r c -> (h r) c")).then_inc(rpb_in, 16)
            sp.wait_ge(rpb_in, 16)
            sp.dma_start(d_rpb.ap(), rpb_pad[:]).then_inc(rpb_out, 16)

            def load_bias(hp):
                for side in range(2):
                    src = bass.AP(d_rpb, ((2 * hp + side) * NREL) * RPAD, [[1, GRID_W], [RPAD, NREL], [1, GRID_W]])
                    dst = bias[64 * side:64 * side + 64, hp % 2, :].rearrange("p (r c) -> p r c", r=NREL)
                    sp.dma_start(dst, src).then_inc(ld_bias, 16)


            sp.wait_ge(rpb_out, 16)
            load_bias(0)
            for hp in range(PAIRS):
                kinds = ([(o, hp + 1) for o in KIND0] if hp < PAIRS - 1 else []) + [(o, hp) for o in KIND1]
                for i, (off, ch) in enumerate(kinds):
                    k = PRO + PER * hp + i
                    load_w(k, k % 2, w_in_v[:, :, off + ch * P:off + (ch + 1) * P])
                if hp < PAIRS - 1:
                    sp.wait_ge(bias_ready, hp + 1)
                    if hp:
                        sp.wait_ge(s_biased, done(ROWS * hp - 1))
                    load_bias(hp + 1)
            sp.wait_ge(y_ready, ATT_ALL)
            sp.dma_start(t_cos[:], k_cos.rearrange("(t p) n -> p t n", p=P)).then_inc(ld_dft, 16)
            sp.dma_start(t_sin[:], k_sin.rearrange("(t p) n -> p t n", p=P)).then_inc(ld_dft, 16)
            sp.dma_start(chan[:], k_chan).then_inc(ld_dft, 16)
            sp.dma_start(t_nyq[:], k_nyq).then_inc(ld_dft, 16)
            sp.wait_ge(bd_zero, 1)
            for g, w in enumerate((lru_w_r, lru_w_i)):
                for d in range(2):
                    for side in range(2):
                        src = w[0, d].rearrange("(c s) i j -> s i c j", s=2)[side]
                        dst = bd[64 * side:64 * side + 64, (2 * g + d) * BC:(2 * g + d + 1) * BC, 64 * side:64 * side + 64]
                        sp.dma_start(dst, src).then_inc(ld_bd, 16)
            sp.wait_ge(lru_done, 4)
            sp.wait_ge(f_done, 4)
            with sp.Fori(0, KC // 2) as two:
                dc = two * 2
                for s in range(2):
                    for b in range(3):
                        k = GATE0 + 3 * (dc + s) + b
                        par = (GATE0 + 3 * s + b) % 2
                        sp.wait_ge(pr_ps, 2 * (3 * (dc + s) + b) + 2)
                        sp.dma_start(w_pr[b][:], proj_v[b][:, :, bass.ds((dc + s) * P, P)]).then_inc(ld_pr[b], 16)
                        load_w(k, par, w_bg_v[:, :, bass.ds((dc + s) * P + BRANCH[b], P)])
            sp.wait_ge(gated, GATED_ALL)
            sp.dma_start(gmix[:], d_gt[0].partition_broadcast(P)).then_inc(ld_out, 16)
            for h in range(2):
                sp.dma_start(wo[:, h], wo_v[:, :, HF[h]]).then_inc(ld_wo[h], 16)
            sp.dma_start(wr[:], wr_v).then_inc(ld_out, 16)
            for t in range(TT):
                sp.dma_start(x1[:, t, :], x_v[:, t, :]).then_inc(ld_x1[t], 16)
            load_expert(sp, 0, 0)
            for t in range(TT):
                sp.wait_ge(xn2_ready, t + 1)
                sp.dma_start(xn2_d[:, t, :], xn2[:, t, :]).then_inc(st_xn2, 16)
            sp.wait_ge(mo_ps, 2 * TT)
            sp.dma_start(before[:], k_before).then_inc(ld_rt, 16)
            sp.dma_start(rbias[:], router_bias.partition_broadcast(P)).then_inc(ld_rt, 16)
            sp.wait_ge(st_list, 16 * 2 * TT)
            sp.dma_start(tokl[:], d_list.rearrange("(p l) o -> p (l o)", p=P)).then_inc(ld_list, 16)
            load_expert(sp, 1, 1)
            with sp.Fori(1, NE // 2) as two:
                e = two * 2
                for s in range(2):
                    free_at = sp.value_load(starts[0:1, bass.ds(e + s - 1, 1)], min_val=1, max_val=NBLK)
                    sp.wait_ge(y_ps, free_at)
                    load_expert(sp, e + s, s)
            nb = sp.value_load(starts[0:1, NE:NE + 1], min_val=NE, max_val=NBLK)
            sp.wait_ge(st_y, nb * 16 + 16)
            sp.dma_start(gffn[:], d_gt[1].partition_broadcast(P)).then_inc(ld_end, 16)
            sp.dma_start(fing[:], final_g.partition_broadcast(P)).then_inc(ld_end, 16)
            for t in range(TT):
                sp.wait_ge(fin_ready, t + 1)
                sp.dma_start(out_v[:, t, :], res[t % 2][:]).then_inc(st_out[t % 2], 16)
            for i in range(2):
                sp.wait_ge(st_out[i], 16 * TT // 2)
            sp.wait_ge(st_xn2, 16 * TT)


        @block.gpsimd
        def _(pool):
            ch = Chain(pool, ch_pool)
            for dst, src in [(conv_w[:, j, :], chunked(lru_conv_w[0, j])) for j in range(4)] + [
                    (conv_b[:], chunked(lru_conv_b[0])), (bg[:], chunked(b_branch_gate[0]))] + [
                    (lru_b[:, 2 * g + d, :], chunked(v[0, d])) for g, v in enumerate((lru_b_r, lru_b_i)) for d in range(2)] + [
                    (lam[:, d, :], chunked(lru_lambda[0, d])) for d in range(2)]:
                pool.dma_start(dst, src).then_inc(ld_small, 16)
            ch.mark(pool.memset(zero_i[:], 0))
            ch(pool.iota(tok[:], [[P, TT]], base=0, channel_multiplier=1))
            pool.dma_start(d_list.rearrange("(p l) o -> p (l o)", p=P), zero_i[:]).then_inc(st_zero, 16)

            def split(k, par, need, wait_half):
                pool.wait_ge(ld_w[par], need)
                if wait_half is not None:
                    pool.wait_ge(job_half, wait_half)
                hold(pool)
                ch(pool.tensor_copy(w_hi[par][:], w_raw[par][:]))
                pool.tensor_tensor(w_lo[par][:], w_raw[par][:], w_hi[par][:].bitcast(f32), SUB).then_inc(w_split, 1)

            split(0, 0, 16, None)
            split(1, 1, 16, None)
            pool.wait_ge(gt_saved, 16)
            pool.memset(rpb_pad[:], 0.0).then_inc(rpb_set, 1)

            def mask_bias(sl, need):
                pool.wait_ge(ld_bias, need)
                b3 = bias[:, sl, :].rearrange("p (r c) -> p r c", c=GRID_W)
                win = window[:].unsqueeze(1).to_broadcast([P, NREL, GRID_W])
                pool.tensor_tensor(b3, b3, win, ADD).then_inc(bias_ready, 1)

            pool.wait_ge(ld_const, 16 * 8)
            split(2, 0, 32, 2)
            mask_bias(0, 32)

            def pair(hp, n):
                for i in range(n):
                    k = PER * hp + PRO + i
                    split(k, (PRO + i) % 2, hp * (PER * 8) + 16 * ((PRO + i) // 2 + 1), 2 * k - 2)

            with pool.Fori(0, PAIRS - 1) as hp:
                ch.enter(hp, PER)
                pair(hp, PER)
                ch.leave(PAIRS - 1)
                mask_bias((hp + 1) % 2, hp * 32 + 64)
            pair(PAIRS - 1, LAST)

            pool.wait_ge(y_ready, ATT_ALL)
            pool.memset(bd[:], 0.0).then_inc(bd_zero, 1)
            pool.memset(zero_row[:], 0.0).then_inc(zero_set, 1)
            pool.wait_ge(zero_set, 1)
            spare = NBLK - NE
            pool.dma_start(d_y[NE * CAP:, :].rearrange("(p k) (a n) -> p (k a) n", p=P, n=HALF),
                           zero_row[:].unsqueeze(1).to_broadcast([P, spare * CAP * D // P // HALF, HALF])).then_inc(st_pad, 16)

            with pool.Fori(0, KC // 2) as two:
                dc = two * 2
                ch.enter(two, 6)
                for i in range(6):
                    k = dc * 3 + (GATE0 + i)
                    split(k, (GATE0 + i) % 2, dc * 24 + 16 * ((GATE0 + i) // 2 + 1), 2 * k - 2)
                ch.leave(KC // 2)

            pool.wait_ge(slots_ready, 1)
            pool.wait_ge(st_zero, 16)
            for k in range(2):
                for t in range(TT):
                    pool.indirect_dma_start(out=d_list, out_offset=bass.IndirectOffsetOnAxis(ap=slot_t[:, k, t:t + 1], axis=0),
                                            in_=tok[:, t:t + 1], in_offset=None).then_inc(st_list, 16)

            nb = pool.value_load(starts[0:1, NE:NE + 1], min_val=NE, max_val=NBLK)
            pool.wait_ge(st_xn2, 16 * TT)
            pool.wait_ge(ld_list, 16)
            pool.tensor_copy(tok_cur[:], tokl[:, 0:1]).then_inc(tok_ready, 1)
            pool.wait_ge(tok_ready, 1)
            pool.indirect_dma_start(out=xg[:], out_offset=None, in_=d_xn2,
                                    in_offset=bass.IndirectOffsetOnAxis(ap=tok_cur[:], axis=0)).then_inc(ld_xg, 16)
            with pool.Fori(0, nb) as j:
                pool.wait_ge(xg_ps, j + 1)
                hold(pool)
                pool.tensor_copy(tok_cur[:], tokl[:, bass.ds(j + 1, 1)]).then_inc(tok_ready, 1)
                pool.wait_ge(tok_ready, j + 2)
                hold(pool)
                pool.indirect_dma_start(out=xg[:], out_offset=None, in_=d_xn2,
                                        in_offset=bass.IndirectOffsetOnAxis(ap=tok_cur[:], axis=0)).then_inc(ld_xg, 16)

            pool.wait_ge(st_y, nb * 16 + 16)
            hold(pool)
            pool.wait_ge(st_pad, 16)
            for t in range(TT):
                if t >= 2:
                    pool.wait_ge(gath, t - 1)
                for k, y in enumerate((y0, y1)):
                    pool.indirect_dma_start(out=y[t % 2][:], out_offset=None, in_=d_y,
                                            in_offset=bass.IndirectOffsetOnAxis(ap=pair_s[:, k, t:t + 1], axis=0)).then_inc(ld_y[t % 2], 16)

        @block.tensor
        def _(pe):
            for s_, n_ in ((s_ps, PRIME), (pt_ps, PRIME), (o_ps, PRIME), (ot_ps, PRIME), (pr_ps, PR_PRIME)):
                pe.sem_inc(s_, n_)

            def mod_vector(v):
                if v >= 2:
                    pe.wait_ge(mod_read, v - 1)
                for h in range(2):
                    b = 2 * v + h
                    pe.wait_ge(ld_ada[b % 3], 16 * (b // 3 + 1))
                    for kc in range(KC):
                        last = pe.matmul(ps[:, b % 4, :], crep[:, kc, :], ada[b % 3][:, kc, :], start=(kc == 0), stop=(kc == KC - 1))
                    last.then_inc(ada_used, 1)

            pe.wait_ge(crep_ready, 1)
            mod_vector(0)
            mod_vector(1)
            pe.wait_ge(ld_const, 16 * 8)
            for n in range(2 * KC):
                kc, th = n // 2, n % 2
                if n < 2:
                    pe.wait_ge(xn_ready, 4 * (th + 1))
                if n >= 4:
                    pe.wait_ge(xt_full, n - 3)
                for i in range(4):
                    src = xn[:, 4 * th + i, :].rearrange("p (q c) -> p c q", c=KC)[:, kc, :]
                    last = pe.transpose(ps[:, 4 + n % 4, i * P:(i + 1) * P], src, ident[:])
                last.then_inc(xt_ps, 1)
            for v in range(2, 6):
                mod_vector(v)

            def job_half_mms(k, par, h, need_split, need_evac, split_wait=True):
                def gen():
                    if h == 0:
                        pe.wait_ge(w_split, need_split)
                    if need_evac is not None:
                        pe.wait_ge(job_evac, need_evac)
                    n = 0
                    for kc in range(KC):
                        for a, b in ((w_hi, u_hi), (w_hi, u_lo), (w_lo, u_hi)):
                            n += 1
                            ins = pe.matmul(ps[:, 5 + h, :], a[par][:, kc, :], b[:, kc, HF[h]], start=(n == 1), stop=(n == MM))
                            if n == MM:
                                ins.then_inc(job_half, 1)
                            yield
                return gen()

            def run(gen, n=10 ** 9):
                for _ in range(n):
                    if next(gen, "end") == "end":
                        return

            def transpose_v(g):
                for i in range(4 * g, min(4 * g + 4, 15)):
                    t0 = i * P if i < 8 else (i - 8) * P + GRID_W
                    last = pe.transpose(ps[:, 1, (i % 4) * P:(i % 4 + 1) * P], vT[:, t0:t0 + P], ident[:])
                last.then_inc(vt_ps, 1)

            pe.wait_ge(u_ready, 2 * KC)
            for k in range(PRO):
                for h in range(2):
                    run(job_half_mms(k, k % 2, h, k + 1, 2 * k + h - 1 if k else None))
            pe.wait_ge(job_evac, 2 * PRO)
            for g in range(4):
                if g:
                    pe.wait_ge(vt_evac, g)
                transpose_v(g)

            def scores(hp_k, r, u):
                pe.wait_ge(q_staged, done(u))
                pe.wait_ge(s_biased, done(u - 1))
                rs = band(r) * GRID_W
                rhs = kT[:, hp_k, rs:rs + HALF]
                pe.matmul(ps[:, 0, :], q_bd[r % 2][:], rhs, start=True, stop=True).then_inc(s_ps, 1)

            scores(0, 0, 0)

            def pair(hp, n):
                par = hp % 2
                nxt = (hp + 1) % 2
                share = 2 * MM * n // ROWS

                def fill():
                    for i in range(n):
                        k = hp * PER + PRO + i
                        for h in range(2):
                            yield from job_half_mms(k, (PRO + i) % 2, h, k + 1, 2 * k + h - 1)
                fg = fill()
                for r in range(ROWS):
                    u = hp * ROWS + r
                    if r < ROWS - 1:
                        scores(par, r + 1, u + 1)
                    elif n == PER:
                        scores(nxt, 0, u + 1)
                    pe.wait_ge(p_ready, done(u))
                    pe.wait_ge(pt_ready, done(u - 2))
                    for i in range(4):
                        last = pe.transpose(ps[:, 2 + 5 * (r % 2), i * P:(i + 1) * P], prob[r % 2][:, i * P:(i + 1) * P], ident[:])
                    last.then_inc(pt_ps, 1)
                    run(fg, share // 2)
                    pe.wait_ge(pt_ready, done(u))
                    pe.wait_ge(o_ready, done(u - 1))
                    t0 = band(r) // 2 if band(r) % 2 == 0 else 8 + band(r) // 2
                    for i in range(4):
                        rhs = vtok[:, par, t0 + i, :]
                        last = pe.matmul(ps[:, 3, 0:P], probT[r % 2][:, i, :], rhs, start=(i == 0), stop=(i == 3))
                    last.then_inc(o_ps, 1)
                    run(fg, share - share // 2)
                    pe.wait_ge(o_ready, done(u))
                    pe.wait_ge(y_ready, done(u - 1))
                    pe.transpose(ps[:, 4, 0:P], o_bd[r % 2][:], ident[:]).then_inc(ot_ps, 1)
                    if n == PER and VT0 <= r < VT0 + 4:
                        g = r - VT0
                        pe.wait_ge(vt_evac, hp * 4 + 4 + g)
                        if g == 0:
                            pe.wait_ge(job_evac, hp * (2 * PER) + 2 * PRO + 6)
                        transpose_v(g)
                run(fg)

            with pe.Fori(0, PAIRS - 1) as hp:
                pair(hp, PER)
            pair(PAIRS - 1, LAST)

            pe.wait_ge(ld_bd, 16 * 8)
            pe.wait_ge(job_evac, 2 * GATE0)

            def lru_gates(n):
                cc, d = n // 2, n % 2
                pe.wait_ge(xc_ready, cc + 1)
                if n:
                    pe.wait_ge(lru_read, n)
                for g in range(2):
                    for h in range(2):
                        last = pe.matmul(ps[:, 2 * g + h, :], bd[:, (2 * g + d) * BC + cc, :], xc[:, HF[h]], start=True, stop=True)
                last.then_inc(lru_ps, 1)

            def channel_dft(g):
                if g:
                    pe.wait_ge(f_done, g)
                for t in range(TT):
                    last = pe.matmul(ps[:, 4 + t // 2, (t % 2) * 2 * P:(t % 2 + 1) * 2 * P], lx[:, 2, g, t * P:(t + 1) * P], chan[:],
                                     start=True, stop=True)
                last.then_inc(z_ps, 1)

            def position_dft(g):
                pe.wait_ge(z_ready, g + 1)
                for bank, tab, off in ((4, t_cos, 0), (5, t_sin, P)):
                    for t in range(TT):
                        pe.matmul(ps[:, bank, :], z[:, t, off:off + P], tab[:, t, :], start=(t == 0), stop=(t == TT - 1))
                for t in range(TT):
                    last = pe.matmul(ps[:, 6, 0:1], z[:, t, 0:P], t_nyq[:, t:t + 1], start=(t == 0), stop=(t == TT - 1))
                last.then_inc(f_ps, 1)

            for g in range(GROUPS):
                lru_gates(2 * g)
                if g == 0:
                    pe.wait_ge(ld_dft, 16 * 4)
                channel_dft(g)
                lru_gates(2 * g + 1)
                position_dft(g)

            branch = [y_na, lx[:, 2], lx[:, 1]]
            pe.wait_ge(lru_done, 4)
            pe.wait_ge(f_done, 4)
            with pe.Fori(0, KC // 2) as two:
                dc = two * 2
                for s in range(2):
                    for b in range(3):
                        m = dc * 3 + (3 * s + b)
                        k = m + GATE0
                        pe.wait_ge(ld_pr[b], dc * 16 + 16 * (s + 1))
                        for h in range(2):
                            pe.wait_ge(gated, 2 * m + (h + 1))
                            for kc in range(BC):
                                last = pe.matmul(ps[:, h, :], w_pr[b][:, kc, :], branch[b][:, kc, HF[h]], start=(kc == 0), stop=(kc == BC - 1))
                            last.then_inc(pr_ps, 1)
                        for h in range(2):
                            run(job_half_mms(k, (GATE0 + 3 * s + b) % 2, h, k + 1, 2 * k + (h - 1)))

            pe.wait_ge(gated, GATED_ALL)
            for t in range(TT + 2):
                if t < TT:
                    for h in range(2):
                        q = 2 * t + h
                        if t == 0:
                            pe.wait_ge(ld_wo[h], 16)
                        if q >= 4:
                            pe.wait_ge(x1_half, q - 3)
                        for kc in range(KC):
                            last = pe.matmul(ps[:, q % 4, :], merged[:, kc, t * P:(t + 1) * P], wo[:, h, kc, :], start=(kc == 0), stop=(kc == KC - 1))
                        last.then_inc(mo_ps, 1)
                if 2 <= t:
                    pe.wait_ge(u2_ready, t - 1)
                    if t == 2:
                        pe.wait_ge(ld_out, 32)
                    for kc in range(KC):
                        last = pe.matmul(ps[:, 6, (t - 2) * NE:(t - 1) * NE], u2T[:, kc, :], wr[:, kc, :], start=(kc == 0), stop=(kc == KC - 1))
                    last.then_inc(ro_ps, 1)
                if 1 <= t <= TT:
                    pe.wait_ge(xn2_ready, t)
                    v = xn2[:, t - 1, :].rearrange("p (q c) -> p c q", c=KC)
                    for kc in range(KC):
                        last = pe.transpose(ps[:, 4 + kc // 4, (kc % 4) * P:(kc % 4 + 1) * P], v[:, kc, :], ident[:])
                    last.then_inc(x2t_ps, 1)

            pe.wait_ge(hit_ready, 1)
            for t in range(TT):
                for t2 in range(t + 1):
                    pe.matmul(ps[:, 7, t * NE:(t + 1) * NE], (before_b if t2 == t else ones_b)[:], hit_b[:, t2, :], start=(t2 == 0), stop=(t2 == t))
            for t in range(TT):
                last = pe.matmul(ps[:, 7, TT * NE:(TT + 1) * NE], ones_b[:], hit_b[:, t, :], start=(t == 0), stop=(t == TT - 1))
            last.then_inc(rank_ps, 1)

            def rows_to_features():
                v = xg[:].rearrange("p (q c) -> p c q", c=KC)
                for kc in range(KC):
                    last = pe.transpose(ps[:, kc // 4, (kc % 4) * P:(kc % 4 + 1) * P], v[:, kc, :], ident[:])
                last.then_inc(xg_ps, 1)

            pe.wait_ge(starts_ready, 1)
            pe.wait_ge(ld_xg, 16)
            rows_to_features()
            hv = act[:].rearrange("p (q c) -> p c q", c=FC)
            with pe.Fori(0, NE // 2) as two:
                e = two * 2
                for s in range(2):
                    first = pe.value_load(starts[0:1, bass.ds(e + s, 1)], min_val=0, max_val=NBLK)
                    end = pe.value_load(starts[0:1, bass.ds(e + (s + 1), 1)], min_val=1, max_val=NBLK)
                    pe.wait_ge(ld_g[s], e * 8 + 16)
                    pe.wait_ge(ld_u[s], e * 8 + 16)
                    pe.wait_ge(ld_d[s], e * 8 + 16)
                    hold(pe)
                    with pe.Fori(first, end) as j:
                        pe.wait_ge(xg_ready, j + 1)
                        for bank, w, sg in ((2, wg, g_ps), (3, wu, h_ps)):
                            for kc in range(KC):
                                last = pe.matmul(ps[:, bank, :], xgT[:, kc, :], w[s][:, kc, :], start=(kc == 0), stop=(kc == KC - 1))
                            last.then_inc(sg, 1)
                        pe.wait_ge(ld_xg, j * 16 + 32)
                        rows_to_features()
                        pe.wait_ge(h_ready, j + 1)
                        for fc in range(FC):
                            last = pe.transpose(ps[:, 4, fc * P:(fc + 1) * P], hv[:, fc, :], ident[:])
                        last.then_inc(ht_ps, 1)
                        pe.wait_ge(ht_ready, j + 1)
                        pe.wait_ge(y_evac, j + 1)
                        for h in range(2):
                            for fc in range(FC):
                                last = pe.matmul(ps[:, 5 + h, :], actT[:, fc, :], wd[s][:, fc, HF[h]], start=(fc == 0), stop=(fc == FC - 1))
                        last.then_inc(y_ps, 1)

        @block.scalar
        def _(sc):
            ch = Chain(sc, ch_act)
            for s_, n_ in ((p_ready, PRIME), (pt_ready, PRIME), (y_ready, PRIME), (y_evac, 1), (st_y, 16)):
                sc.sem_inc(s_, n_)
            sc.wait_ge(ld_const, 16 * 8)
            sc.activation(cact[:], cvec[:], ACT.Silu).then_inc(cact_ready, 1)
            sc.wait_ge(lam_in, 1)
            sc.activation(lam_t[:, 1], lam_t[:, 0], ACT.Exp, scale=-1.0).then_inc(lam_exp, 1)
            sc.wait_ge(lam_in, 2)
            sc.activation(lam_t[:, 3], lam_t[:, 2], ACT.Ln).then_inc(lam_ln, 1)
            for t in range(TT):
                sc.wait_ge(ld_x[t], 16)
                ch(sc.activation(junk[:], xn[:, t, :], ACT.Square, accum_out=ms[:, t:t + 1]))
            sc.activation(rstd[:], ms[:], ACT.Copy).then_inc(ms_ready, 1)
            sc.wait_ge(ms_ready, 2)
            sc.activation(ms[:], rstd[:], ACT.Sqrt).then_inc(root_ready, 1)
            for n in range(2 * KC):
                kc, th = n // 2, n % 2
                sc.wait_ge(xt_full, n + 1)
                sc.activation(u_hi[:, kc, HF[th]], u_full[n % 2][:], ACT.Copy).then_inc(u_hi_ready, 1)

            def evac(k, h, dst, scale=1.0):
                sc.wait_ge(job_half, 2 * k + (h + 1))
                hold(sc)
                sc.activation(dst, ps[:, 5 + h, :], ACT.Copy, scale=scale).then_inc(job_evac, 1)

            for k in range(PRO):
                for h in range(2):
                    evac(k, h, (qT[:, 0, HF[h]], kT[:, 0, HF[h]], vT[:, HF[h]])[k], DH ** -0.5 if k == 0 else 1.0)

            def exps(r, u):
                sc.wait_ge(s_biased, done(u))
                sc.wait_ge(o_ready, done(u - 2))
                sc.activation(prob[r % 2][:], prob[r % 2][:], ACT.Exp, bias=nmax[:, r % 2:r % 2 + 1],
                              accum_out=rsum[:, r % 2:r % 2 + 1]).then_inc(p_ready, 1)

            exps(0, 0)

            def pair(hp, n):
                nxt = (hp + 1) % 2
                for r in range(ROWS):
                    u = hp * ROWS + r
                    sc.wait_ge(pt_ps, done(u))
                    sc.wait_ge(o_ps, done(u - 2))
                    sc.activation(probT[r % 2][:].rearrange("p a b -> p (a b)"), ps[:, 2 + 5 * (r % 2), :], ACT.Copy).then_inc(pt_ready, 1)
                    if r < ROWS - 1:
                        exps(r + 1, u + 1)
                    elif n == PER:
                        exps(0, u + 1)
                    for i in range(n):
                        for h in range(2):
                            if finish_unit(n, i, h) == r:
                                k = hp * PER + PRO + i
                                if n == PER and i < 3:
                                    dst = (qT[:, nxt, HF[h]], kT[:, nxt, HF[h]], vT[:, HF[h]])[i]
                                else:
                                    ii = i - 3 if n == PER else i
                                    dst = lx[:, ii, hp, HF[h]]
                                evac(k, h, dst, DH ** -0.5 if n == PER and i == 0 else 1.0)
                    sc.wait_ge(ot_ps, done(u))
                    hold(sc)
                    for side in range(2):
                        sl = slice(64 * side, 64 * side + 64)
                        dst = y_na[sl, hp, r * GRID_W:(r + 1) * GRID_W]
                        ins = sc.activation(dst, ps[sl, 4, BACK[side]], ACT.Copy)
                        if side:
                            ins.then_inc(y_ready, 1)

            with sc.Fori(0, PAIRS - 1) as hp:
                pair(hp, PER)
            pair(PAIRS - 1, LAST)

            sc.wait_ge(job_evac, 2 * GATE0)
            sc.activation(lx[:, 1], lx[:, 1], ACT.Gelu_apprx_tanh).then_inc(gelu_ready, 1)
            sc.wait_ge(decay_ready, 1)

            def lru_step(n):
                cc, d = n // 2, n % 2
                dec = decay[:, d, cc:cc + 1]
                sc.wait_ge(lru_ps, n + 1)
                if n:
                    sc.wait_ge(lru_free, n)
                ch.mark(sc.activation(lt[0][:], ps[:, 0:2, :].rearrange("p a b -> p (a b)"), ACT.Tanh, scale=0.5, bias=lru_b[:, d, cc:cc + 1]))
                sc.activation(lt[1][:], ps[:, 2:4, :].rearrange("p a b -> p (a b)"), ACT.Tanh, scale=0.5, bias=lru_b[:, 2 + d, cc:cc + 1]).then_inc(lru_read, 1)
                ch.sync()
                ch(sc.activation(lt[2][:], lt[0][:], ACT.Exp, scale=dec, bias=dec))
                sc.activation(lt[0][:], lt[0][:], ACT.Tanh, scale=dec, bias=dec).then_inc(lru_act, 1)
                sc.wait_ge(lru_rad, n + 1)
                sc.activation(lt[0][:], lt[0][:], ACT.Sqrt, scale=-1.0).then_inc(lru_root, 1)

            for g in range(GROUPS):
                lru_step(2 * g)
                sc.wait_ge(z_ps, g + 1)
                for b in range(4):
                    ins = sc.activation(z[:, 2 * b:2 * b + 2, :].rearrange("p a b -> p (a b)"), ps[:, 4 + b, :], ACT.Copy)
                ins.then_inc(z_ready, 1)
                lru_step(2 * g + 1)
                sc.wait_ge(f_ps, g + 1)
                if g:
                    sc.wait_ge(f_done, g)
                sc.activation(sin_part[:], ps[:, 5, :], ACT.Copy).then_inc(f_sin, 1)

            with sc.Fori(0, KC // 2) as two:
                dc = two * 2
                for s in range(2):
                    for b in range(3):
                        m = dc * 3 + (3 * s + b)
                        for h in range(2):
                            sc.wait_ge(job_half, 2 * (m + GATE0) + (h + 1))
                            sc.wait_ge(gated, 2 * m + (h + 1))
                            hold(sc)
                            sc.activation(gate[h][:], ps[:, 5 + h, :], ACT.Sigmoid,
                                          bias=bg[:, bass.ds(dc + (s + BRANCH[b] // P), 1)]).then_inc(job_evac, 1)

            for t in range(TT):
                sc.wait_ge(x1_half, 2 * t + 2)
                sc.activation(xn2[:, t, :], x1[:, t, :], ACT.Square, accum_out=ms2[:, t:t + 1]).then_inc(ms2_ready, 1)
                sc.wait_ge(root2, 2 * t + 1)
                sc.activation(ms2[:, t:t + 1], rstd2[:, t:t + 1], ACT.Sqrt).then_inc(root2, 1)
            sc.wait_ge(ro_ps, TT)
            sc.activation(dd["score"][:].rearrange("p a b -> p (a b)"), ps[:, 6, 0:TT * NE], ACT.Sigmoid).then_inc(score_ready, 1)

            sc.wait_ge(starts_ready, 1)
            nb = sc.value_load(starts[0:1, NE:NE + 1], min_val=NE, max_val=NBLK)
            with sc.Fori(0, nb) as j:
                sc.wait_ge(g_ps, j + 1)
                sc.activation(act[:], ps[:, 2, :], ACT.Silu).then_inc(silu_ready, 1)
                sc.wait_ge(ht_ps, j + 1)
                sc.activation(actT[:].rearrange("p a b -> p (a b)"), ps[:, 4, :], ACT.Copy).then_inc(ht_ready, 1)
                sc.wait_ge(y_ps, j + 1)
                sc.wait_ge(st_y, j * 16 + 16)
                sc.activation(yb[:], ps[:, 5:7, :].rearrange("p a b -> p (a b)"), ACT.Copy).then_inc(y_evac, 1)
                sc.wait_ge(y_evac, j + 2)
                hold(sc)
                sc.wait_ge(st_pad, 16)
                sc.dma_start(d_y[bass.ds(j * CAP, CAP), :], yb[:]).then_inc(st_y, 16)

            for t in range(TT):
                sc.wait_ge(fin_ready_x, t + 1)
                sc.activation(junk2[:], x1[:, t, :], ACT.Square, accum_out=ms2[:, t:t + 1]).then_inc(fin_ms, 1)
                sc.wait_ge(fin_root, 2 * t + 1)
                sc.activation(ms2[:, t:t + 1], rstd2[:, t:t + 1], ACT.Sqrt).then_inc(fin_root, 1)

        @block.vector
        def _(dve):
            ch = Chain(dve, ch_dve)
            for s_, n_ in ((s_biased, PRIME), (o_ready, PRIME), (gated, PRIME), (q_staged, PRIME)):
                dve.sem_inc(s_, n_)
            dve.wait_ge(cact_ready, 1)
            dve.tensor_copy(crep[:], cact[:].unsqueeze(2).to_broadcast([P, KC, P])).then_inc(crep_ready, 1)
            dve.wait_ge(ld_small, 16 * 12)
            ch(dve.tensor_scalar(decay[:], lam[:], -1.0, None, MUL))
            dve.tensor_tensor(lam_t[:, 0], decay[:], lam[:], ALU.max).then_inc(lam_in, 1)
            dve.wait_ge(lam_exp, 1)
            dve.tensor_scalar(lam_t[:, 2], lam_t[:, 1], 1.0, None, ADD).then_inc(lam_in, 1)
            dve.wait_ge(lam_ln, 1)
            dve.wait_ge(lam_in, 2)
            ch(dve.tensor_scalar(lam_t[:, 2], lam_t[:, 2], 1.0, None, SUB))
            ch(dve.tensor_scalar(lam_t[:, 0], lam_t[:, 2], 0.0, None, ALU.is_equal))
            ch(dve.tensor_tensor(lam_t[:, 2], lam_t[:, 2], lam_t[:, 0], ADD))
            ch(dve.reciprocal(lam_t[:, 2], lam_t[:, 2]))
            ch(dve.tensor_tensor(lam_t[:, 3], lam_t[:, 3], lam_t[:, 2], MUL))
            ch(dve.tensor_tensor(lam_t[:, 3], lam_t[:, 3], lam_t[:, 0], ADD))
            ch(dve.tensor_tensor(lam_t[:, 3], lam_t[:, 3], lam_t[:, 1], MUL))
            ch(dve.scalar_tensor_tensor(decay[:], decay[:], 0.0, lam_t[:, 3], ALU.max, ADD))
            ch.mark(dve.tensor_scalar(lru_b[:], lru_b[:], 0.5, None, MUL))
            dve.tensor_scalar(decay[:], decay[:], -4.0, None, MUL).then_inc(decay_ready, 1)
            dve.wait_ge(ms_ready, 1)
            dve.tensor_scalar(rstd[:], rstd[:], 1.0 / D, EPS, MUL, ADD).then_inc(ms_ready, 1)
            dve.wait_ge(root_ready, 1)
            ch(dve.reciprocal(rstd[:], ms[:]))
            for t in range(TT):
                dve.tensor_scalar(xn[:, t, :], xn[:, t, :], rstd[:, t:t + 1], None, MUL).then_inc(xn_ready, 1)

            def mod_vector(v):
                dve.wait_ge(ada_used, 2 * v + 2)
                row = ps[:, 2 * (v % 2):2 * (v % 2) + 2, :].rearrange("p a b -> p (a b)")
                if v in (2, 5):
                    r = mrow[:, v // 3, :]
                    dve.tensor_tensor(r, row[0:1, :], r, ADD).then_inc(mod_read, 1)
                    return
                v3 = lambda a: a.rearrange("p (q c) -> p q c", c=KC)
                dve.tensor_tensor(v3(modtmp[:]), v3(row), ident[:].unsqueeze(2).to_broadcast([P, P, KC]), MUL).then_inc(mod_read, 1)
                dve.wait_ge(mod_read, v + 1)
                ch(dve.tensor_reduce(modv[:, v, :], modtmp[:].rearrange("p (q c) -> p c q", c=KC), AX.X, ADD))
                ch(dve.tensor_tensor(modv[:, v, :], modv[:, v, :], mod_b[:, v, :], ADD))
                if v in (1, 4):
                    ch(dve.scalar_tensor_tensor(u_scale[:, v // 3, :], modv[:, v, :], 1.0, norm_g[:, v // 3, :], ADD, MUL))

            dve.wait_ge(ld_const, 16 * 8)
            mod_vector(0)
            mod_vector(1)
            for n in range(2 * KC + 1):
                if n < 2 * KC:
                    kc = n // 2
                    dve.wait_ge(xt_ps, n + 1)
                    dve.tensor_scalar(u_full[n % 2][:], ps[:, 4 + n % 4, :], u_scale[:, 0, kc:kc + 1], modv[:, 0, kc:kc + 1], MUL, ADD).then_inc(xt_full, 1)
                if n:
                    m = n - 1
                    dve.wait_ge(u_hi_ready, m + 1)
                    dve.tensor_tensor(u_lo[:, m // 2, HF[m % 2]], u_full[m % 2][:], u_hi[:, m // 2, HF[m % 2]].bitcast(f32), SUB).then_inc(u_ready, 1)
                    dve.wait_ge(u_ready, m + 1)
            for v in range(2, 6):
                mod_vector(v)

            def v_tiles(g, par):
                n = min(4, 15 - 4 * g)
                dst = vtok[:, par, 4 * g:4 * g + n, :]
                dve.tensor_copy(dst, ps[:, 1, 0:n * P].rearrange("p (a b) -> p a b", b=P)).then_inc(vt_evac, 1)

            def stage_q(r, par):
                for side in range(2):
                    sl = slice(64 * side, 64 * side + 64)
                    ins = dve.tensor_copy(q_bd[r % 2][sl, BACK[side]], qT[sl, par, r * GRID_W:(r + 1) * GRID_W])
                    if side:
                        ins.then_inc(q_staged, 1)

            dve.wait_ge(gt_saved, 16)
            ch.mark(dve.memset(q_bd[0][:], 0.0))
            ch.mark(dve.memset(q_bd[1][:], 0.0))
            ch.mark(dve.memset(o_bd[0][:], 0.0))
            ch.mark(dve.memset(o_bd[1][:], 0.0))
            for g in range(4):
                dve.wait_ge(vt_ps, g + 1)
                v_tiles(g, 0)
            ch.sync()
            dve.wait_ge(job_evac, 2)
            stage_q(0, 0)
            stage_q(1, 0)
            dve.wait_ge(bias_ready, 1)

            def biased(r, u, par):
                dve.wait_ge(s_ps, done(u))
                dve.wait_ge(pt_ps, done(u - 2))
                d0 = (band(r) - r + WIN_R - 1) * GRID_W
                ch(dve.tensor_tensor(prob[r % 2][:], ps[:, 0, :], bias[:, par, d0:d0 + HALF], ADD))
                dve.tensor_reduce(nmax[:, r % 2:r % 2 + 1], prob[r % 2][:], AX.X, ALU.max, negate=True).then_inc(s_biased, 1)

            biased(0, 0, 0)

            def pair(hp, n):
                par = hp % 2
                nxt = (hp + 1) % 2
                for r in range(ROWS):
                    u = hp * ROWS + r
                    if r < ROWS - 1:
                        biased(r + 1, u + 1, par)
                    elif n == PER:
                        dve.wait_ge(bias_ready, hp + 2)
                        biased(0, u + 1, nxt)
                    if r < ROWS - 2:
                        stage_q(r + 2, par)
                    elif n == PER:
                        if r == ROWS - 2:
                            dve.wait_ge(job_evac, hp * (2 * PER) + 2 * PRO + 2)
                        stage_q(r + 2 - ROWS, nxt)
                    dve.wait_ge(o_ps, done(u))
                    dve.wait_ge(p_ready, done(u))
                    ch(dve.reciprocal(rinv[:, r % 2:r % 2 + 1], rsum[:, r % 2:r % 2 + 1]))
                    dve.wait_ge(ot_ps, done(u - 2))
                    for side in range(2):
                        sl = slice(64 * side, 64 * side + 64)
                        ins = dve.tensor_scalar(o_bd[r % 2][sl, sl], ps[sl, 3, sl], rinv[sl, r % 2:r % 2 + 1], None, MUL)
                        if side:
                            ins.then_inc(o_ready, 1)
                    if n == PER and VT0 <= r < VT0 + 4:
                        g = r - VT0
                        dve.wait_ge(vt_ps, hp * 4 + (g + 5))
                        v_tiles(g, nxt)

            with dve.Fori(0, PAIRS - 1) as hp:
                ch.enter(hp, 2 * ROWS)
                pair(hp, PER)
                ch.leave(PAIRS - 1)
            pair(PAIRS - 1, LAST)

            dve.wait_ge(y_ready, ATT_ALL)
            dve.wait_ge(job_evac, 2 * GATE0)
            for cc in range(BC):
                xr, yr = lx[:, 0, cc, :], lx[:, 1, cc, :]
                if cc:
                    dve.wait_ge(lru_ps, 2 * cc)
                ch(dve.tensor_scalar(xc[:], xr, conv_w[:, 2, cc:cc + 1], conv_b[:, cc:cc + 1], MUL, ADD))
                ch(dve.scalar_tensor_tensor(xc[:, 2:], xr[:, :T - 2], conv_w[:, 0, cc:cc + 1], xc[:, 2:], MUL, ADD))
                ch(dve.scalar_tensor_tensor(xc[:, 1:], xr[:, :T - 1], conv_w[:, 1, cc:cc + 1], xc[:, 1:], MUL, ADD))
                dve.scalar_tensor_tensor(xc[:, :T - 1], xr[:, 1:], conv_w[:, 3, cc:cc + 1], xc[:, :T - 1], MUL, ADD).then_inc(xc_ready, 1)
                dve.wait_ge(xc_ready, cc + 1)
                for d in range(2):
                    n = 2 * cc + d
                    dve.wait_ge(lru_act, n + 1)
                    ch(dve.tensor_tensor(lt[3][:], lt[2][:], lt[2][:], MUL))
                    dve.scalar_tensor_tensor(lt[0][:], lt[3][:], 1.0, lt[0][:], ADD, MUL).then_inc(lru_rad, 1)
                    ch.mark(dve.scalar_tensor_tensor(lt[1][:], lt[1][:], 1.0, xc[:], ADD, MUL))
                    ch.sync()
                    dve.wait_ge(lru_root, n + 1)
                    ch(dve.scalar_tensor_tensor(lt[0][:], lt[0][:], 0.5, lt[1][:], MUL, MUL))
                    if d == 0:
                        dve.tensor_tensor_scan(xr, lt[2][:], lt[0][:], 0.0, MUL, ADD).then_inc(lru_free, 1)
                    else:
                        dve.tensor_tensor_scan(lt[3][:, ::-1], lt[2][:, ::-1], lt[0][:, ::-1], 0.0, MUL, ADD).then_inc(lru_free, 1)
                dve.wait_ge(lru_free, 2 * cc + 2)
                ch(dve.tensor_tensor(xr, xr, lt[3][:], ADD))
                if cc == 0:
                    dve.wait_ge(gelu_ready, 1)
                dve.tensor_tensor(yr, xr, yr, MUL).then_inc(lru_done, 1)
                g = cc
                fy = lx[:, 2, g, :]
                dve.wait_ge(f_sin, g + 1)
                ch.mark(dve.tensor_tensor(fy[:, 0:HALF], ps[:, 4, :], sin_part[:], SUB))
                ch.mark(dve.tensor_tensor(fy[:, T - 1:HALF:-1], ps[:, 4, 1:HALF], sin_part[:, 1:HALF], ADD))
                dve.tensor_copy(fy[:, HALF:HALF + 1], ps[:, 6, 0:1]).then_inc(f_done, 1)

            with dve.Fori(0, KC // 2) as two:
                dc = two * 2
                ch.enter(two, 8)
                for s in range(2):
                    for b in range(3):
                        m = dc * 3 + (3 * s + b)
                        for h in range(2):
                            dve.wait_ge(job_evac, 2 * (m + GATE0) + (h + 1))
                            dve.wait_ge(pr_ps, 2 * m + (h + 1 + PR_PRIME))
                            dst = merged[:, dc + s, HF[h]]
                            if b == 0:
                                dve.tensor_tensor(dst, gate[h][:], ps[:, h, :], MUL).then_inc(gated, 1)
                            else:
                                ch(dve.tensor_tensor(part[:], gate[h][:], ps[:, h, :], MUL))
                                dve.wait_ge(gated, 2 * m + (h + 1))
                                dve.tensor_tensor(dst, dst, part[:], ADD).then_inc(gated, 1)
                                if h == 0:
                                    dve.wait_ge(gated, 2 * m + (h + 1 + PRIME))
                ch.leave(KC // 2)

            dve.wait_ge(ld_out, 32)
            for t in range(TT + 1):
                if t < TT:
                    dve.wait_ge(ld_x1[t], 16)
                    for h in range(2):
                        dve.wait_ge(mo_ps, 2 * t + h + 1)
                        ch(dve.tensor_tensor(mixed[:], ps[:, (2 * t + h) % 4, :], gmix[:, HF[h]], MUL))
                        dve.tensor_tensor(x1[:, t, HF[h]], x1[:, t, HF[h]], mixed[:], ADD).then_inc(x1_half, 1)
                        dve.wait_ge(x1_half, 2 * t + h + 1)
                if t:
                    m = t - 1
                    dve.wait_ge(ms2_ready, m + 1)
                    dve.tensor_scalar(rstd2[:, m:m + 1], ms2[:, m:m + 1], 1.0 / D, EPS, MUL, ADD).then_inc(root2, 1)
                    dve.wait_ge(root2, 2 * m + 2)
                    ch(dve.reciprocal(rstd2[:, m:m + 1], ms2[:, m:m + 1]))
                    dve.tensor_scalar(xn2[:, m, :], x1[:, m, :], rstd2[:, m:m + 1], None, MUL).then_inc(xn2_ready, 1)
                    dve.wait_ge(x2t_ps, m + 1)
                    for kc in range(KC):
                        ins = dve.tensor_scalar(u2T[:, kc, :], ps[:, 4 + kc // 4, (kc % 4) * P:(kc % 4 + 1) * P],
                                                u_scale[:, 1, kc:kc + 1], modv[:, 3, kc:kc + 1], MUL, ADD)
                    ins.then_inc(u2_ready, 1)

            t3 = lambda n: dd[n][:]
            g4 = lambda a: a.rearrange("p t (g e) -> p (t g) e", e=EPG)
            dve.wait_ge(mo_ps, 2 * TT)
            ch.mark(dve.memset(ones_b[:], 1.0))
            for g in range(NG):
                ch.mark(dve.memset(gidx[:, g:g + 1], float(g - NG)))
            dve.wait_ge(ld_rt, 32)
            ch(dve.tensor_copy(before_b[:], before[:]))
            dve.wait_ge(score_ready, 1)
            ch(dve.tensor_tensor(t3("sel"), t3("score"), rbias[:].unsqueeze(1).to_broadcast([P, TT, NE]), ADD))
            pt = [pairt[:, i].rearrange("p t g -> p (t g)") for i in range(8)]
            se = [g4(t3("sel"))[:, :, e] for e in range(EPG)]
            tt = lambda o, a, b, op: ch(dve.tensor_tensor(o, a, b, op))
            tt(pt[0], se[0], se[1], ALU.max)
            tt(pt[1], se[0], se[1], ALU.min)
            tt(pt[2], se[2], se[3], ALU.max)
            tt(pt[3], se[2], se[3], ALU.min)
            tt(pt[4], pt[0], pt[2], ALU.max)
            tt(pt[5], pt[0], pt[2], ALU.min)
            tt(pt[1], pt[1], pt[3], ALU.max)
            tt(pt[5], pt[5], pt[1], ALU.max)
            tt(pt[4], pt[4], pt[5], ADD)
            gs = pairt[:, 4]
            top = slot_f[:, 0, :]
            bc8 = lambda a: a.unsqueeze(2).to_broadcast([P, TT, NG])
            gi = gidx[:].unsqueeze(1).to_broadcast([P, TT, NG])
            ch(dve.tensor_reduce(top, gs, AX.X, ALU.max))
            tt(pairt[:, 6], gs, bc8(top), ALU.is_equal)
            tt(pairt[:, 6], pairt[:, 6], gi, MUL)
            ch(dve.tensor_reduce(top, pairt[:, 6], AX.X, ALU.min))
            tt(pairt[:, 7], gi, bc8(top), ALU.is_equal)
            rk = g4(t3("ta"))
            for e in range(EPG):
                ch(dve.memset(rk[:, :, e], float(EPG - 1 - e)))
            for a in range(EPG):
                for b in range(a + 1, EPG):
                    tt(pt[0], se[a], se[b], ALU.is_ge)
                    tt(rk[:, :, b], rk[:, :, b], pt[0], ADD)
                    tt(rk[:, :, a], rk[:, :, a], pt[0], SUB)
            ch(dve.scalar_tensor_tensor(g4(t3("hit")), rk, 1.5, pt[7].unsqueeze(2).to_broadcast([P, TT * NG, EPG]), ALU.is_lt, MUL))
            dve.tensor_copy(hit_b[:], t3("hit")).then_inc(hit_ready, 1)
            bc32 = lambda a: a.unsqueeze(2).to_broadcast([P, TT, NE])
            tt(t3("wgt"), t3("score"), t3("hit"), MUL)
            ch(dve.tensor_reduce(top, t3("wgt"), AX.X, ADD))
            ch(dve.reciprocal(top, top))
            tt(t3("wgt"), t3("wgt"), bc32(top), MUL)
            dve.wait_ge(rank_ps, 1)
            ch(dve.tensor_copy(cnt[:, 0, 0:NE], ps[:, 7, TT * NE:(TT + 1) * NE]))
            ch.mark(dve.memset(cnt[:, 1, :], 1.0))
            ch.mark(dve.memset(cnt[:, 3, :], 1.0))
            ch(dve.memset(cnt[:, 2, :], 0.0))
            for b in range(1, T // CAP):
                ch(dve.scalar_tensor_tensor(cnt[:, 1, 0:NE], cnt[:, 0, 0:NE], float(CAP * b), cnt[:, 1, 0:NE], ALU.is_gt, ADD))
            ch(dve.tensor_tensor_scan(cnt[:, 2, 1:NE + 1], cnt[:, 3, 0:NE], cnt[:, 1, 0:NE], 0.0, MUL, ADD))
            dve.tensor_copy(starts[:], cnt[0:1, 2, :]).then_inc(starts_ready, 1)
            ch(dve.tensor_scalar(cnt[:, 3, 0:NE], cnt[:, 2, 0:NE], float(CAP), 1.0, MUL, ADD))
            tt(t3("slot"), ps[:, 7, 0:TT * NE].rearrange("p (t e) -> p t e", e=NE), cnt[:, 3, 0:NE].unsqueeze(1).to_broadcast([P, TT, NE]), ADD)
            tt(t3("slot"), t3("slot"), t3("hit"), MUL)
            for k in range(2):
                top = slot_f[:, k, :]
                ch(dve.tensor_reduce(top, t3("slot"), AX.X, ALU.max))
                tt(t3("ta"), t3("slot"), bc32(top), ALU.is_equal)
                tt(t3("tb"), t3("ta"), t3("wgt"), MUL)
                ch(dve.tensor_reduce(pair_w[:, k, :], t3("tb"), AX.X, ADD))
                if k == 0:
                    tt(t3("ta"), t3("ta"), t3("slot"), MUL)
                    tt(t3("slot"), t3("slot"), t3("ta"), SUB)
            ch(dve.tensor_scalar(slot_f[:], slot_f[:], 1.0, None, SUB))
            ch(dve.tensor_copy(pair_s[:], slot_f[:]))
            ch(dve.tensor_single_scalar(slot_u[:], pair_s[:], CAP - 1, ALU.bitwise_and))
            ch(dve.tensor_single_scalar(slot_t[:], pair_s[:], 7, ALU.arith_shift_right))
            dve.scalar_tensor_tensor(slot_t[:], slot_u[:], float(LIST), slot_t[:], MUL, ADD).then_inc(slots_ready, 1)

            def features():
                for kc in range(KC):
                    ins = dve.tensor_scalar(xgT[:, kc, :], ps[:, kc // 4, (kc % 4) * P:(kc % 4 + 1) * P],
                                            u_scale[:, 1, kc:kc + 1], modv[:, 3, kc:kc + 1], MUL, ADD)
                ins.then_inc(xg_ready, 1)

            nb = dve.value_load(starts[0:1, NE:NE + 1], min_val=NE, max_val=NBLK)
            dve.wait_ge(xg_ps, 1)
            features()
            with dve.Fori(0, nb) as j:
                dve.wait_ge(silu_ready, j + 1)
                dve.wait_ge(h_ps, j + 1)
                dve.tensor_tensor(act[:], act[:], ps[:, 3, :], MUL).then_inc(h_ready, 1)
                dve.wait_ge(xg_ps, j + 2)
                features()

            ce = Chain(dve, ch_end)
            dve.wait_ge(ld_end, 32)
            for t in range(TT):
                dve.wait_ge(ld_y[t % 2], 32 * (t // 2 + 1))
                if t >= 2:
                    dve.wait_ge(st_out[t % 2], 16 * (t // 2))
                r = res[t % 2][:]
                ce(dve.tensor_scalar(r, y0[t % 2][:], pair_w[:, 0, t:t + 1], None, MUL))
                dve.scalar_tensor_tensor(r, y1[t % 2][:], pair_w[:, 1, t:t + 1], r, MUL, ADD).then_inc(gath, 1)
                dve.wait_ge(gath, t + 1)
                ce(dve.tensor_tensor(r, r, gffn[:], MUL))
                dve.tensor_tensor(x1[:, t, :], x1[:, t, :], r, ADD).then_inc(fin_ready_x, 1)
                dve.wait_ge(fin_ms, t + 1)
                dve.tensor_scalar(rstd2[:, t:t + 1], ms2[:, t:t + 1], 1.0 / D, EPS, MUL, ADD).then_inc(fin_root, 1)
                dve.wait_ge(fin_root, 2 * t + 2)
                ce(dve.reciprocal(rstd2[:, t:t + 1], ms2[:, t:t + 1]))
                dve.scalar_tensor_tensor(r, x1[:, t, :], rstd2[:, t:t + 1], fing[:], MUL, MUL).then_inc(fin_ready, 1)


_INS = ["x", "c", "ada_w", "ada_b", "norm_mix_g", "norm_ffn_g", "w_in", "w_branch_gate", "b_branch_gate",
        "na_rpb", "lru_conv_w", "lru_conv_b", "lru_w_r", "lru_b_r", "lru_w_i", "lru_b_i", "lru_lambda",
        "w_proj_na", "w_proj_lru", "w_proj_fnet", "w_out", "w_router", "router_bias",
        "w_exp_gate", "w_exp_up", "w_exp_down", "final_g"]


def constants():
    w, cc = np.arange(GRID_W)[:, None], np.arange(GRID_W)[None, :]
    start = np.clip(w - WIN_C // 2, 0, GRID_W - WIN_C)
    window = np.where((cc >= start) & (cc < start + WIN_C), 0.0, NEG)
    j = np.arange(P)
    chan = 2 * np.pi * (np.outer(j, j) % P) / P
    t, k = np.arange(T), np.arange(HALF)
    pos = 2 * np.pi * (np.outer(t, k) % T) / T
    f = lambda a: np.ascontiguousarray(a, dtype=np.float32)
    return {
        "k_ident": f(np.eye(P)),
        "k_window": f(np.concatenate([window[::-1], window[::-1]])),
        "k_before": f(np.triu(np.ones((P, P)), 1)),
        "k_chan": f(np.concatenate([np.cos(chan), np.sin(chan)], 1) / np.sqrt(P)),
        "k_cos": f(np.cos(pos) / np.sqrt(T)),
        "k_sin": f(np.sin(pos) / np.sqrt(T)),
        "k_nyq": f(np.broadcast_to(((-1.0) ** j)[:, None] / np.sqrt(T), (P, TT))),
    }


def kernel(**inputs):
    import numpy as _np
    import concourse.bacc as _bacc
    from concourse import mybir as _mybir
    from concourse.bass_utils import run_bass_kernel_spmd as _run

    nc = _bacc.Bacc("TRN2", target_bir_lowering=False, num_devices=1)
    arrays, args = {}, []
    consts = constants()
    for name in _INS + list(consts):
        a = _np.ascontiguousarray(consts[name] if name in consts else inputs[name])
        arrays[f"in_{name}"] = a
        args.append(nc.dram_tensor(f"in_{name}", a.shape, _mybir.dt.from_np(a.dtype), kind="ExternalInput").ap())
    args.append(nc.dram_tensor("out_0", (1, T, D), _mybir.dt.float32, kind="ExternalOutput").ap())
    build(nc, *args)
    r = _run(nc, [arrays], core_ids=[0])
    return r.results[0]["out_0"]
```

```python
import concourse.bass as bass
from concourse import mybir
from contextlib import ExitStack
import numpy as np

D = 1024
T = 1024
P = 128
TT = T // P
KC = D // P
HALF = 512
GRID_W, ROWS = 64, 16
DH = 64
HEADS = 8
PAIRS = HEADS // 2
WIN_R, WIN_C = 8, 16
NREL = 2 * WIN_R - 1
RELC = 2 * WIN_C - 1
RPAD = 128
BW = 512
BC = BW // P
GROUPS = 4
NE, NG, EPG = 32, 8, 4
FE = 512
FC = FE // P
CAP = 128
NBLK = 2048 // CAP + NE
LIST = NBLK + 1
EPS = 1e-6
NEG = -1e30
YBUF = 4
PRIME = 2


def done(n):
    return n + 1 + PRIME


class Chain:

    def __init__(self, eng, sem):
        self.eng, self.sem, self.n, self.dyn = eng, sem, 0, None

    def mark(self, ins):
        ins.then_inc(self.sem, 1)
        self.n += 1

    def sync(self):
        self.eng.wait_ge(self.sem, self.n if self.dyn is None else self.dyn + self.n)

    def __call__(self, ins):
        self.mark(ins)
        self.sync()

    def enter(self, turn, per):
        self.base, self.per, self.dyn = self.n, per, turn * per

    def leave(self, turns):
        assert self.n - self.base == self.per, (self.n - self.base, self.per)
        self.n, self.dyn = self.base + self.per * turns, None


def band(r):
    return min(max(r - WIN_R // 2, 0), ROWS - WIN_R)


def build(nc, x, c, ada_w, ada_b, norm_mix_g, norm_ffn_g, w_in, w_branch_gate, b_branch_gate,
          na_rpb, lru_conv_w, lru_conv_b, lru_w_r, lru_b_r, lru_w_i, lru_b_i, lru_lambda,
          w_proj_na, w_proj_lru, w_proj_fnet, w_out, w_router, router_bias,
          w_exp_gate, w_exp_up, w_exp_down, final_g,
          k_ident, k_window, k_before, k_chan, k_cos, k_sin, k_nyq, out):
    f32, f32r, i32, bf16 = mybir.dt.float32, mybir.dt.float32r, mybir.dt.int32, mybir.dt.bfloat16
    ALU, ACT, AX = mybir.AluOpType, mybir.ActivationFunctionType, mybir.AxisListType
    ADD, SUB, MUL = ALU.add, ALU.subtract, ALU.mult

    ctx = ExitStack()
    with ctx:
        ctx.enter_context(nc.allow_non_contiguous_dma("small parameter vectors are laid channel-major"))
        base = (nc.sbuf_base + 63) // 64 * 64

        def at(name, kb, shape, dt=f32):
            return nc.alloc_sbuf_tensor_at(name, shape, dt, offset=base + int(kb * 1024))

        def sem(name):
            return ctx.enter_context(nc.semaphore(name))

        xn = at("xn", 96, [P, TT, D])
        ada = [at(f"ada{i}", kb, [P, KC, HALF]) for i, kb in enumerate((128, 144, 80))]
        junk = at("junk", 64, [P, D])
        modtmp = at("modtmp", 68, [P, D])
        crep = at("crep", 72, [P, KC, P])
        u_hi = at("u_hi", 0, [P, KC, T], f32r)
        u_lo = at("u_lo", 32, [P, KC, T], f32r)
        u_full = [at(f"u_full{i}", kb, [P, HALF]) for i, kb in enumerate((64, 66, 76, 78))]
        y_na = at("y_na", 64, [P, BC, T])
        lx = at("lx", 80, [P, 3, BC, T])
        qT = at("qT", 128, [P, 2, T])
        kT = at("kT", 136, [P, 2, T])
        vT = at("vT", 144, [P, T])
        vtok = at("vtok", 148, [P, 2, 15, P])
        bias = at("bias", 163, [P, 2, NREL * GRID_W])
        window = at("window", 170.5, [P, GRID_W])
        w_raw = [at(f"w_raw{i}", 171 + 4 * i, [P, KC, P]) for i in range(2)]
        w_hi = [at(f"w_hi{i}", 179 + 4 * i, [P, KC, P], f32r) for i in range(2)]
        w_lo = [at(f"w_lo{i}", 187 + 4 * i, [P, KC, P], f32r) for i in range(2)]
        prob = [at(f"prob{i}", 195 + 2 * i, [P, HALF]) for i in range(2)]
        probT = [at(f"probT{i}", 199 + 2 * i, [P, 4, P]) for i in range(2)]
        q_bd = [at(f"q_bd{i}", 203 + 0.5 * i, [P, P]) for i in range(2)]
        o_bd = [at(f"o_bd{i}", 204 + 0.5 * i, [P, P]) for i in range(2)]
        rpb_pad = at("rpb_pad", 195, [HEADS * NREL, RPAD])
        t_cos = at("t_cos", 128, [P, TT // 2, HALF])
        t_sin = at("t_sin", 136, [P, TT // 2, HALF])
        bd = at("bd", 144, [P, 16, P])
        chan = at("chan", 152, [P, 2 * P])
        t_nyq = at("t_nyq", 153, [P, TT // 2])
        z_first = at("z_first", 154, [P, TT // 2, 2 * P])
        z = at("z", 158, [P, 2, TT // 2, 2 * P])
        sin_part = at("sin_part", 166, [P, HALF])
        xc = [at(f"xc{i}", 168 + 4 * i, [P, T]) for i in range(2)]
        t_a = [at(f"t_a{i}", 176 + 4 * i, [P, T]) for i in range(2)]
        t_b = [at(f"t_b{i}", 184 + 4 * i, [P, T]) for i in range(2)]
        t_c = [at(f"t_c{i}", 192 + 4 * i, [P, T]) for i in range(2)]
        t_d = at("t_d", 200, [P, T])
        zero_row = at("zero_row", 204, [P, 2 * P])
        merged = at("merged", 128, [P, KC, T])
        w_pr = [at(f"w_pr{i}", 160 + 2 * i, [P, BC, P]) for i in range(3)]
        gate = [at(f"gate{i}", 166 + 2 * i, [P, HALF]) for i in range(2)]
        part = at("part", 195, [P, HALF])
        ada_g = at("ada_g", 80, [P, KC, HALF])
        acc = at("acc", 199, [P, HALF])
        mrow = at("mrow", 197, [1, HALF])
        x1 = at("x1", 0, [P, TT, D])
        u2 = at("u2", 32, [P, TT, D])
        wo = at("wo", 160, [P, 2, KC, HALF])
        gmix = at("gmix", 192, [P, D])
        gmix_b = at("gmix_b", 112, [P, D])
        sc_row = at("sc_row", 116, [P, D])
        sh_row = at("sh_row", 120, [P, D])
        g_row = at("g_row", 124, [P, D])
        sc_b = at("sc_b", 56, [P, D])
        sh_b = at("sh_b", 60, [P, D])
        u2T = at("u2T", 196, [P, KC, P])
        mixed = at("mixed", 200, [P, HALF])
        wr = at("wr", 202, [P, KC, NE])
        raw_g, raw_u, raw_d = (at("raw_" + n, 64 + 16 * i, shp) for i, (n, shp) in enumerate((("g", [P, KC, FE]), ("u", [P, KC, FE]), ("d", [P, FC, D]))))
        wg_hi, wu_hi, wd_hi = (at(n + "_hi", kb, shp, f32r) for n, kb, shp in (("wg", 32, [P, KC, FE]), ("wu", 48, [P, KC, FE]), ("wd", 112, [P, FC, D])))
        wg_lo, wu_lo, wd_lo = (at(n + "_lo", kb, shp, f32r) for n, kb, shp in (("wg", 128, [P, KC, FE]), ("wu", 144, [P, KC, FE]), ("wd", 160, [P, FC, D])))
        xg = at("xg", 176, [P, D])
        xgT_hi = at("xgT_hi", 180, [P, KC, P], f32r)
        xgT_lo = at("xgT_lo", 184, [P, KC, P], f32r)
        act = at("act", 188, [P, FE])
        actT_hi = at("actT_hi", 190, [P, FC, P], f32r)
        actT_lo = at("actT_lo", 192, [P, FC, P], f32r)
        yb = at("yb", 194, [P, D])
        y0 = [at(f"y0_{i}", 64 + 4 * i, [P, D]) for i in range(YBUF)]
        y1 = [at(f"y1_{i}", 80 + 4 * i, [P, D]) for i in range(YBUF)]
        gffn = at("gffn", 96, [P, D])
        gffn_b = at("gffn_b", 100, [P, D])
        fing = at("fing", 104, [P, D])
        res = [at(f"res{i}", 112 + 4 * i, [P, D]) for i in range(2)]
        junk2 = at("junk2", 120, [P, D])

        NM = ["score", "sel", "hit", "wgt", "rank", "slot", "ta", "tb"]
        dd = {n: at("r_" + n, 176 + i, [P, TT, NE]) for i, n in enumerate(NM)}
        hit_b = at("hit_b", 184, [P, TT, NE], bf16)
        before_b = at("before_b", 185, [P, P], bf16)
        ones_b = at("ones_b", 185.5, [P, P], bf16)
        before = at("before", 186, [P, P])
        rbias = at("rbias", 186.5, [P, NE])
        cnt = at("cnt", 186.75, [P, 4, NE + 1])
        pairt = at("pairt", 187.5, [P, 8, TT, NG])
        slot_f = at("slot_f", 189.5, [P, 2, TT])
        slot_t = at("slot_t", 189.75, [P, 2, TT], i32)
        slot_u = at("slot_u", 190, [P, 2, TT], i32)
        gidx = at("gidx", 190.25, [P, NG])

        cur = [205.0]

        def small(name, shape, dt=f32):
            n = 1
            for s in shape[1:]:
                n *= s
            t = at(name, cur[0], shape, dt)
            cur[0] += (n * 4 + 31) // 32 * 32 / 1024
            assert base + cur[0] * 1024 <= nc.sbuf_usable_end, name
            return t

        ident = small("ident", [P, P])
        cvec = small("cvec", [P, KC])
        cact = small("cact", [P, KC])
        ms = small("ms", [P, TT])
        rstd = small("rstd", [P, TT])
        mod_b = small("mod_b", [P, 6, KC])
        norm_g = small("norm_g", [P, 2, KC])
        modv = small("modv", [P, 6, KC])
        u_scale = small("u_scale", [P, 2, KC])
        nmax = small("nmax", [P, 2])
        rsum = small("rsum", [P, 2])
        rinv = small("rinv", [P, 2])
        conv_w = small("conv_w", [P, 4, BC])
        conv_b = small("conv_b", [P, BC])
        lru_b = small("lru_b", [P, 4, BC])
        lam = small("lam", [P, 2, BC])
        lam_t = small("lam_t", [P, 4, 2, BC])
        decay = small("decay", [P, 2, BC])
        decay2 = small("decay2", [P, 2, BC])
        ones_f = small("ones_f", [P, 1])
        bg = small("bg", [P, 3 * KC])
        ms2 = small("ms2", [P, TT])
        rstd2 = small("rstd2", [P, TT])
        tok_cur = small("tok_cur", [P, 1], i32)
        tok = small("tok", [P, TT], i32)
        tokl = small("tokl", [P, LIST], i32)
        pair_w = small("pair_w", [P, 2, TT])
        pair_s = small("pair_s", [P, 2, TT], i32)
        starts = small("starts", [1, NE + 1], i32)
        zero_i = small("zero_i", [P, LIST], i32)

        ps = ctx.enter_context(nc.psum_tensor("ps", [P, 8, HALF], f32))

        d_rpb = nc.dram_tensor("d_rpb", (HEADS * NREL, RPAD), f32, kind="Internal")
        d_mod = nc.dram_tensor("d_mod", (4, D), f32, kind="Internal").ap()
        d_u2 = nc.dram_tensor("d_u2", (T, D), f32, kind="Internal").ap()
        d_list = nc.dram_tensor("d_list", (P * LIST, 1), i32, kind="Internal").ap()
        d_y = nc.dram_tensor("d_y", (NBLK * CAP, D), f32, kind="Internal").ap()

        held = sem("held")
        ch_dve, ch_act, ch_pool = sem("ch_dve"), sem("ch_act"), sem("ch_pool")
        ld_const, ld_small = sem("ld_const"), sem("ld_small")
        ld_x = [sem(f"ld_x{t}") for t in range(TT)]
        ld_ada = [sem(f"ld_ada{i}") for i in range(3)]
        ada_used = sem("ada_used")
        cact_ready, crep_ready, ms_ready, root_ready, xn_ready = (sem(n) for n in ("cact_ready", "crep_ready", "ms_ready", "root_ready", "xn_ready"))
        mod_read, ld_mod, acc_ready, acc_ps, mrow_ready, st_mod = (sem(n) for n in ("mod_read", "ld_mod", "acc_ready", "acc_ps", "mrow_ready", "st_mod"))
        xt_ps, xt_full, u_hi_ready, u_lo_even, u_lo_odd = (sem(n) for n in ("xt_ps", "xt_full", "u_hi_ready", "u_lo_even", "u_lo_odd"))
        ld_w = [sem(f"ld_w{i}") for i in range(2)]
        w_split, job_half, job_evac = sem("w_split"), sem("job_half"), sem("job_evac")
        vt_ps, vt_evac = sem("vt_ps"), sem("vt_evac")
        q_staged, s_ps, s_biased, p_ready, pt_ps, pt_ready, o_ps, o_ready, ot_ps, y_ready = (sem("at_" + n) for n in (
            "q_staged", "s_ps", "s_biased", "p_ready", "pt_ps", "pt_ready", "o_ps", "o_ready", "ot_ps", "y_ready"))
        rpb_set, rpb_in, rpb_out, bias_ready = (sem(n) for n in ("rpb_set", "rpb_in", "rpb_out", "bias_ready"))
        ld_bias = sem("ld_bias")
        bd_zero, ld_bd, ld_chan, ld_dft = sem("bd_zero"), sem("ld_bd"), sem("ld_chan"), sem("ld_dft")
        lam_exp, lam_ln, lam_in, decay_ready = (sem(n) for n in ("lam_exp", "lam_ln", "lam_in", "decay_ready"))
        gelu_ready, xc_ready, lru_ps, lru_read, lru_free, lru_sum, lru_act, lru_rad, lru_root, lru_done = (sem(n) for n in (
            "gelu_ready", "xc_ready", "lru_ps", "lru_read", "lru_free", "lru_sum", "lru_act", "lru_rad", "lru_root", "lru_done"))
        z_ps, z_copied, z_ready, f_ps, f_sin, f_done = (sem(n) for n in ("z_ps", "z_copied", "z_ready", "f_ps", "f_sin", "f_done"))
        ld_pr = [sem(f"ld_pr{i}") for i in range(3)]
        pr_ps, gated = sem("pr_ps"), sem("gated")
        ld_wo = [sem(f"ld_wo{i}") for i in range(2)]
        ld_x1 = [sem(f"ld_x1{t}") for t in range(TT)]
        ld_out, ld_rows = sem("ld_out"), sem("ld_rows")
        mo_ps, x1_half, ms2_ready, root2, u2_ready, x2t_ps, u2T_ready, ro_ps = (sem(n) for n in (
            "mo_ps", "x1_half", "ms2_ready", "root2", "u2_ready", "x2t_ps", "u2T_ready", "ro_ps"))
        st_u2, st_zero = sem("st_u2"), sem("st_zero")
        consts_up, ld_rt, score_ready, hit_ready, rank_ps, slots_ready, starts_ready, st_list, ld_list, tok_ready = (sem(n) for n in (
            "consts_up", "ld_rt", "score_ready", "hit_ready", "rank_ps", "slots_ready", "starts_ready", "st_list", "ld_list", "tok_ready"))
        ld_raw = {w: sem("e_ld_" + w) for w in "gud"}
        hi_ready = {w: sem("e_hi_" + w) for w in "gud"}
        lo_ready = {w: sem("e_lo_" + w) for w in "gud"}
        ld_xg, xg_ps, xgT_hi_ready, xgT_ready, g_ps, h_ps, silu_ready, h_ready, ht_ps, actT_hi_ready, actT_ready, y_ps, y_evac, st_y = (
            sem("e_" + n) for n in ("ld_xg", "xg_ps", "xgT_hi", "xgT", "g_ps", "h_ps", "silu", "h_ready", "ht_ps", "actT_hi", "actT", "y_ps", "y_evac", "st_y"))
        zero_set, st_pad = sem("zero_set"), sem("st_pad")
        ld_end, fin_ms, fin_root, fin_ready, fin_ready_x, ch_end = (sem(n) for n in ("ld_end", "fin_ms", "fin_root", "fin_ready", "fin_ready_x", "ch_end"))
        ld_y = [sem(f"ld_y{i}") for i in range(YBUF)]
        y_scaled = sem("y_scaled")
        st_out = [sem(f"st_out{i}") for i in range(2)]

        chan_major = lambda v: v.rearrange("(p c) -> p c", c=KC)
        chunked = lambda v: v.rearrange("(c p) -> p c", p=P)
        ada_v = ada_w[0].rearrange("(p c) n -> p c n", c=KC)
        w_in_v = w_in[0].rearrange("(p c) n -> p c n", c=KC)
        w_bg_v = w_branch_gate[0].rearrange("(p c) n -> p c n", c=KC)
        x_v = x[0].rearrange("(t p) d -> p t d", p=P)
        out_v = out[0].rearrange("(t p) d -> p t d", p=P)
        proj_v = [w[0].rearrange("(c p) n -> p c n", p=P) for w in (w_proj_na, w_proj_fnet, w_proj_lru)]
        wo_v = w_out[0].rearrange("(c p) n -> p c n", p=P)
        wr_v = w_router.rearrange("(p c) n -> p c n", c=KC)
        wg_v = w_exp_gate[0].rearrange("e (p c) n -> e p c n", c=KC)
        wu_v = w_exp_up[0].rearrange("e (p c) n -> e p c n", c=KC)
        wd_v = w_exp_down[0].rearrange("e (p c) n -> e p c n", c=FC)
        u2_d = d_u2.rearrange("(t p) d -> p t d", p=P)

        PRO, PER, LAST = 3, 6, 3
        KIND0 = [0, BW, 2 * BW]
        KIND1 = [3 * BW, 4 * BW, 5 * BW]
        GATE0 = PRO + PER * (PAIRS - 1) + LAST
        BRANCH = [0, 2 * D, D]
        VT0 = 9
        XBANK = [4, 7, 0, 1]
        MM = 24
        HF = [slice(0, HALF), slice(HALF, T)]
        BACK = [slice(63, None, -1), slice(127, 63, -1)]

        def finish_unit(n_jobs, i, h):
            return (MM * (2 * i + h + 1) - 1) // (n_jobs * 2 * MM // ROWS)

        GATED_PRIME = 4
        GATED_ALL = 6 * KC + GATED_PRIME
        PR_PRIME = 6
        ATT_ALL = done(PAIRS * ROWS - 1)

        WT = {"g": (raw_g, wg_hi, wg_lo, wg_v), "u": (raw_u, wu_hi, wu_lo, wu_v), "d": (raw_d, wd_hi, wd_lo, wd_v)}

        def half_of(a, half):
            n = a.shape[1] // 2
            return a[:, half * n:(half + 1) * n, :]

        def split_hi(w, half):
            raw, hi, _, _ = WT[w]
            nc.scalar.activation(half_of(hi, half), half_of(raw, half), ACT.Copy).then_inc(hi_ready[w], 1)

        def split_lo(eng, w, half):
            raw, hi, lo, _ = WT[w]
            eng.tensor_tensor(half_of(lo, half), half_of(raw, half), half_of(hi, half).bitcast(f32), SUB).then_inc(lo_ready[w], 1)

        def hold(eng):
            eng.sem_inc(held, 1)

        block = ctx.enter_context(nc.Block())

        @block.sync
        def _(sp):
            def load_w(k, par, cols):
                sp.wait_ge(w_split, k - 1)
                sp.dma_start(w_raw[par][:], cols).then_inc(ld_w[par], 16)

            for dst, src in ((cvec[:], c[0].rearrange("(p c) -> p c", c=KC)), (ident[:], k_ident), (window[:], k_window),
                             (mod_b[:], ada_b[0].rearrange("(v p c) -> p v c", v=6, c=KC)),
                             (norm_g[:, 0, :], chan_major(norm_mix_g[0])), (norm_g[:, 1, :], chan_major(norm_ffn_g[0]))):
                sp.dma_start(dst, src).then_inc(ld_const, 16)
            for t in range(TT):
                sp.dma_start(xn[:, t, :], x_v[:, t, :]).then_inc(ld_x[t], 16)
            for b in range(4):
                if b >= 3:
                    sp.wait_ge(ada_used, b - 2)
                sp.dma_start(ada[b % 3][:], ada_v[:, :, b * HALF:(b + 1) * HALF]).then_inc(ld_ada[b % 3], 16)
                if b == 1:
                    for i in range(2):
                        sp.dma_start(w_raw[i][:], w_in_v[:, :, KIND0[i]:KIND0[i] + P]).then_inc(ld_w[i], 16)
            load_w(2, 0, w_in_v[:, :, KIND0[2]:KIND0[2] + P])
            sp.wait_ge(rpb_set, 1)
            sp.dma_start(rpb_pad[:, 48:48 + RELC], na_rpb[0].rearrange("h r c -> (h r) c")).then_inc(rpb_in, 16)
            sp.wait_ge(rpb_in, 16)
            sp.dma_start(d_rpb.ap(), rpb_pad[:]).then_inc(rpb_out, 16)

            def load_bias(hp):
                for side in range(2):
                    src = bass.AP(d_rpb, ((2 * hp + side) * NREL) * RPAD, [[1, GRID_W], [RPAD, NREL], [1, GRID_W]])
                    dst = bias[64 * side:64 * side + 64, hp % 2, :].rearrange("p (r c) -> p r c", r=NREL)
                    sp.dma_start(dst, src).then_inc(ld_bias, 16)


            sp.wait_ge(rpb_out, 16)
            load_bias(0)
            for hp in range(PAIRS):
                kinds = ([(o, hp + 1) for o in KIND0] if hp < PAIRS - 1 else []) + [(o, hp) for o in KIND1]
                for i, (off, ch) in enumerate(kinds):
                    k = PRO + PER * hp + i
                    load_w(k, k % 2, w_in_v[:, :, off + ch * P:off + (ch + 1) * P])
                if hp < PAIRS - 1:
                    sp.wait_ge(bias_ready, hp + 1)
                    if hp:
                        sp.wait_ge(s_biased, done(ROWS * hp - 1))
                    load_bias(hp + 1)
            sp.wait_ge(bd_zero, 1)
            for g, w in enumerate((lru_w_r, lru_w_i)):
                for d in range(2):
                    for side in range(2):
                        src = w[0, d].rearrange("(c s) i j -> s i c j", s=2)[side]
                        dst = bd[64 * side:64 * side + 64, (2 * g + d) * BC:(2 * g + d + 1) * BC, 64 * side:64 * side + 64]
                        sp.dma_start(dst, src).then_inc(ld_bd, 16)
            sp.dma_start(chan[:], k_chan).then_inc(ld_chan, 16)
            sp.dma_start(t_nyq[:], k_nyq).then_inc(ld_chan, 16)
            sp.wait_ge(y_ready, ATT_ALL)
            sp.dma_start(t_cos[:], k_cos.rearrange("(t p) n -> p t n", p=P)).then_inc(ld_dft, 16)
            sp.dma_start(t_sin[:], k_sin.rearrange("(t p) n -> p t n", p=P)).then_inc(ld_dft, 16)
            sp.wait_ge(f_ps, 4)
            sp.wait_ge(f_done, 4)
            sp.wait_ge(lru_free, 7)
            with sp.Fori(0, KC // 2) as two:
                dc = two * 2
                for s in range(2):
                    for b in range(3):
                        k = GATE0 + 3 * (dc + s) + b
                        par = (GATE0 + 3 * s + b) % 2
                        sp.wait_ge(pr_ps, 2 * (3 * (dc + s) + b) + 2)
                        sp.dma_start(w_pr[b][:], proj_v[b][:, :, bass.ds((dc + s) * P, P)]).then_inc(ld_pr[b], 16)
                        load_w(k, par, w_bg_v[:, :, bass.ds((dc + s) * P + BRANCH[b], P)])
                        if b == 0:
                            sp.wait_ge(lru_done, 4)
                            sp.wait_ge(acc_ready, dc + (s + 1))
                            sp.dma_start(ada_g[:], ada_v[:, :, bass.ds((dc + s) * HALF + 2 * D, HALF)]).then_inc(ld_mod, 16)
            sp.wait_ge(gated, GATED_ALL)
            sp.wait_ge(st_mod, 16 * (KC + 1))
            sp.dma_start(gmix[:], d_mod[0].partition_broadcast(P)).then_inc(ld_out, 16)
            sp.dma_start(gmix_b[:], ada_b[0, 2 * D:3 * D].partition_broadcast(P)).then_inc(ld_out, 16)
            for h in range(2):
                sp.dma_start(wo[:, h], wo_v[:, :, HF[h]]).then_inc(ld_wo[h], 16)
            sp.dma_start(wr[:], wr_v).then_inc(ld_out, 16)
            for dst, src in ((sc_row, d_mod[2]), (sc_b, ada_b[0, 4 * D:5 * D]), (g_row, norm_ffn_g[0]), (sh_row, d_mod[1]), (sh_b, ada_b[0, 3 * D:4 * D])):
                sp.dma_start(dst[:], src.partition_broadcast(P)).then_inc(ld_rows, 16)
            for t in range(TT):
                sp.dma_start(x1[:, t, :], x_v[:, t, :]).then_inc(ld_x1[t], 16)
            for w in "gud":
                sp.dma_start(WT[w][0][:], WT[w][3][0]).then_inc(ld_raw[w], 16)
            for t in range(TT):
                sp.wait_ge(u2_ready, t + 1)
                sp.dma_start(u2_d[:, t, :], u2[:, t, :]).then_inc(st_u2, 16)
            sp.wait_ge(mo_ps, 2 * TT)
            sp.dma_start(before[:], k_before).then_inc(ld_rt, 16)
            sp.dma_start(rbias[:], router_bias.partition_broadcast(P)).then_inc(ld_rt, 16)
            def load_weights(e):
                for w in "gud":
                    sp.wait_ge(lo_ready[w], 2 * e)
                    sp.dma_start(WT[w][0][:], WT[w][3][e]).then_inc(ld_raw[w], 16)

            load_weights(1)
            sp.wait_ge(st_list, 16 * 2 * TT)
            sp.dma_start(tokl[:], d_list.rearrange("(p l) o -> p (l o)", p=P)).then_inc(ld_list, 16)
            with sp.Fori(2, NE) as e:
                load_weights(e)
            for w in "gud":
                sp.wait_ge(lo_ready[w], 2 * NE)
            sp.dma_start(gffn[:], d_mod[3].partition_broadcast(P)).then_inc(ld_end, 16)
            sp.dma_start(gffn_b[:], ada_b[0, 5 * D:6 * D].partition_broadcast(P)).then_inc(ld_end, 16)
            sp.dma_start(fing[:], final_g.partition_broadcast(P)).then_inc(ld_end, 16)
            for t in range(TT):
                sp.wait_ge(fin_ready, t + 1)
                sp.dma_start(out_v[:, t, :], res[t % 2][:]).then_inc(st_out[t % 2], 16)
            for i in range(2):
                sp.wait_ge(st_out[i], 16 * TT // 2)
            sp.wait_ge(st_u2, 16 * TT)


        @block.gpsimd
        def _(pool):
            ch = Chain(pool, ch_pool)
            for dst, src in [(conv_w[:, j, :], chunked(lru_conv_w[0, j])) for j in range(4)] + [
                    (conv_b[:], chunked(lru_conv_b[0])), (bg[:], chunked(b_branch_gate[0]))] + [
                    (lru_b[:, 2 * g + d, :], chunked(v[0, d])) for g, v in enumerate((lru_b_r, lru_b_i)) for d in range(2)] + [
                    (lam[:, d, :], chunked(lru_lambda[0, d])) for d in range(2)]:
                pool.dma_start(dst, src).then_inc(ld_small, 16)
            ch.mark(pool.memset(zero_i[:], 0))
            ch(pool.iota(tok[:], [[P, TT]], base=0, channel_multiplier=1))
            pool.dma_start(d_list.rearrange("(p l) o -> p (l o)", p=P), zero_i[:]).then_inc(st_zero, 16)

            def split(k, par, need, wait_half):
                pool.wait_ge(ld_w[par], need)
                if wait_half is not None:
                    pool.wait_ge(job_half, wait_half)
                hold(pool)
                ch(pool.tensor_copy(w_hi[par][:], w_raw[par][:]))
                pool.tensor_tensor(w_lo[par][:], w_raw[par][:], w_hi[par][:].bitcast(f32), SUB).then_inc(w_split, 1)

            pool.memset(rpb_pad[:], 0.0).then_inc(rpb_set, 1)
            split(0, 0, 16, None)
            split(1, 1, 16, None)

            for n in range(1, 2 * KC, 2):
                kc, th = n % KC, n // KC
                pool.wait_ge(u_hi_ready, n + 1)
                pool.tensor_tensor(u_lo[:, kc, HF[th]], u_full[n % 4][:], u_hi[:, kc, HF[th]].bitcast(f32), SUB).then_inc(u_lo_odd, 1)

            def mask_bias(sl, need):
                pool.wait_ge(ld_bias, need)
                b3 = bias[:, sl, :].rearrange("p (r c) -> p r c", c=GRID_W)
                win = window[:].unsqueeze(1).to_broadcast([P, NREL, GRID_W])
                pool.tensor_tensor(b3, b3, win, ADD).then_inc(bias_ready, 1)

            pool.wait_ge(ld_const, 16 * 6)
            split(2, 0, 32, 2)
            mask_bias(0, 32)

            def pair(hp, n):
                for i in range(n):
                    k = PER * hp + PRO + i
                    split(k, (PRO + i) % 2, hp * (PER * 8) + 16 * ((PRO + i) // 2 + 1), 2 * k - 2)

            with pool.Fori(0, PAIRS - 1) as hp:
                ch.enter(hp, PER)
                pair(hp, PER)
                ch.leave(PAIRS - 1)
                mask_bias((hp + 1) % 2, hp * 32 + 64)
            pair(PAIRS - 1, LAST)

            pool.wait_ge(y_ready, done((PAIRS - 1) * ROWS - 1))
            pool.memset(bd[:], 0.0).then_inc(bd_zero, 1)
            pool.wait_ge(y_ready, ATT_ALL)
            pool.memset(zero_row[:], 0.0).then_inc(zero_set, 1)
            pool.wait_ge(zero_set, 1)
            spare = NBLK - NE
            pool.dma_start(d_y[NE * CAP:, :].rearrange("(p k) (a n) -> p (k a) n", p=P, n=2 * P),
                           zero_row[:].unsqueeze(1).to_broadcast([P, spare * CAP * D // P // (2 * P), 2 * P])).then_inc(st_pad, 16)

            pool.wait_ge(gelu_ready, 1)
            for cc in range(BC):
                xr, yr = lx[:, 0, cc, :], lx[:, 1, cc, :]
                pool.wait_ge(lru_free, 2 * cc + 2)
                pool.tensor_tensor(xr, xr, t_b[1][:], ADD).then_inc(lru_sum, 1)
                pool.wait_ge(lru_sum, cc + 1)
                pool.tensor_tensor(yr, xr, yr, MUL).then_inc(lru_done, 1)

            with pool.Fori(0, KC // 2) as two:
                dc = two * 2
                ch.enter(two, 6)
                for i in range(6):
                    k = dc * 3 + (GATE0 + i)
                    split(k, (GATE0 + i) % 2, dc * 24 + 16 * ((GATE0 + i) // 2 + 1), 2 * k - 2)
                ch.leave(KC // 2)

            for w in "gud":
                for half in range(2):
                    pool.wait_ge(hi_ready[w], half + 1)
                    split_lo(pool, w, half)

            pool.wait_ge(slots_ready, 1)
            pool.wait_ge(st_zero, 16)
            for k in range(2):
                for t in range(TT):
                    pool.indirect_dma_start(out=d_list, out_offset=bass.IndirectOffsetOnAxis(ap=slot_t[:, k, t:t + 1], axis=0),
                                            in_=tok[:, t:t + 1], in_offset=None).then_inc(st_list, 16)

            nb = pool.value_load(starts[0:1, NE:NE + 1], min_val=NE, max_val=NBLK)
            pool.wait_ge(st_u2, 16 * TT)
            pool.wait_ge(ld_list, 16)
            pool.tensor_copy(tok_cur[:], tokl[:, 0:1]).then_inc(tok_ready, 1)
            pool.wait_ge(tok_ready, 1)
            pool.indirect_dma_start(out=xg[:], out_offset=None, in_=d_u2,
                                    in_offset=bass.IndirectOffsetOnAxis(ap=tok_cur[:], axis=0)).then_inc(ld_xg, 16)
            with pool.Fori(0, nb) as j:
                pool.wait_ge(xg_ps, j + 1)
                hold(pool)
                pool.tensor_copy(tok_cur[:], tokl[:, bass.ds(j + 1, 1)]).then_inc(tok_ready, 1)
                pool.wait_ge(tok_ready, j + 2)
                hold(pool)
                pool.indirect_dma_start(out=xg[:], out_offset=None, in_=d_u2,
                                        in_offset=bass.IndirectOffsetOnAxis(ap=tok_cur[:], axis=0)).then_inc(ld_xg, 16)

            pool.wait_ge(st_y, nb * 16 + 16)
            hold(pool)
            pool.wait_ge(st_pad, 16)
            for t in range(TT):
                if t >= YBUF:
                    pool.wait_ge(fin_ready_x, t - YBUF + 1)
                for k, y in enumerate((y0, y1)):
                    pool.indirect_dma_start(out=y[t % YBUF][:], out_offset=None, in_=d_y,
                                            in_offset=bass.IndirectOffsetOnAxis(ap=pair_s[:, k, t:t + 1], axis=0)).then_inc(ld_y[t % YBUF], 16)

        @block.tensor
        def _(pe):
            for s_, n_ in ((s_ps, PRIME), (pt_ps, PRIME), (o_ps, PRIME), (ot_ps, PRIME), (pr_ps, PR_PRIME)):
                pe.sem_inc(s_, n_)

            def mod_vector(v):
                for h in range(2):
                    b = 2 * v + h
                    pe.wait_ge(ld_ada[b % 3], 16 * (b // 3 + 1))
                    for kc in range(KC):
                        last = pe.matmul(ps[:, b % 4, :], crep[:, kc, :], ada[b % 3][:, kc, :], start=(kc == 0), stop=(kc == KC - 1))
                    last.then_inc(ada_used, 1)
            pe.wait_ge(crep_ready, 1)
            def x_features(n):
                kc, th = n % KC, n // KC
                pe.wait_ge(xn_ready, 4 * (th + 1))
                if n >= 4:
                    pe.wait_ge(xt_full, n - 3)
                for i in range(4):
                    src = xn[:, 4 * th + i, :].rearrange("p (q c) -> p c q", c=KC)[:, kc, :]
                    last = pe.transpose(ps[:, XBANK[n % 4], i * P:(i + 1) * P], src, ident[:])
                last.then_inc(xt_ps, 1)

            mod_vector(0)
            pe.wait_ge(ld_const, 16 * 6)
            x_features(0)
            x_features(1)
            mod_vector(1)
            pe.wait_ge(mod_read, 1)

            def job_half_mms(k, par, h, need_split, need_evac):
                def gen():
                    if h == 0:
                        pe.wait_ge(w_split, need_split)
                    if need_evac is not None:
                        pe.wait_ge(job_evac, need_evac)
                    n = 0
                    for kc in range(KC):
                        for a, b in ((w_hi, u_hi), (w_hi, u_lo), (w_lo, u_hi)):
                            n += 1
                            ins = pe.matmul(ps[:, 5 + h, :], a[par][:, kc, :], b[:, kc, HF[h]], start=(n == 1), stop=(n == MM))
                            if n == MM:
                                ins.then_inc(job_half, 1)
                            yield
                return gen()

            def run(gen, n=10 ** 9):
                for _ in range(n):
                    if next(gen, "end") == "end":
                        return

            def transpose_v(g):
                for i in range(4 * g, min(4 * g + 4, 15)):
                    t0 = i * P if i < 8 else (i - 8) * P + GRID_W
                    last = pe.transpose(ps[:, 1, (i % 4) * P:(i % 4 + 1) * P], vT[:, t0:t0 + P], ident[:])
                last.then_inc(vt_ps, 1)

            first_job = [job_half_mms(0, 0, h, 1, None) for h in range(2)]
            for n in range(2, 2 * KC + 6):
                if n < 2 * KC:
                    x_features(n)
                m = n - 6
                if m >= 0:
                    pe.wait_ge((u_lo_even, u_lo_odd)[m % 2], m // 2 + 1)
                    run(first_job[m // KC], 3)
            for k in range(1, PRO):
                for h in range(2):
                    run(job_half_mms(k, k % 2, h, k + 1, 2 * k + h - 1))
            pe.wait_ge(job_evac, 2 * PRO)
            for g in range(4):
                if g:
                    pe.wait_ge(vt_evac, g)
                transpose_v(g)

            def scores(hp_k, r, u):
                pe.wait_ge(q_staged, done(u))
                pe.wait_ge(s_biased, done(u - 1))
                rs = band(r) * GRID_W
                rhs = kT[:, hp_k, rs:rs + HALF]
                pe.matmul(ps[:, 0, :], q_bd[r % 2][:], rhs, start=True, stop=True).then_inc(s_ps, 1)

            scores(0, 0, 0)

            def pair(hp, n):
                par = hp % 2
                nxt = (hp + 1) % 2
                share = 2 * MM * n // ROWS

                def fill():
                    for i in range(n):
                        k = hp * PER + PRO + i
                        for h in range(2):
                            yield from job_half_mms(k, (PRO + i) % 2, h, k + 1, 2 * k + h - 1)
                fg = fill()
                for r in range(ROWS):
                    u = hp * ROWS + r
                    if r < ROWS - 1:
                        scores(par, r + 1, u + 1)
                    elif n == PER:
                        scores(nxt, 0, u + 1)
                    pe.wait_ge(p_ready, done(u))
                    pe.wait_ge(pt_ready, done(u - 2))
                    for i in range(4):
                        last = pe.transpose(ps[:, 2 + 5 * (r % 2), i * P:(i + 1) * P], prob[r % 2][:, i * P:(i + 1) * P], ident[:])
                    last.then_inc(pt_ps, 1)
                    run(fg, share // 2)
                    pe.wait_ge(pt_ready, done(u))
                    pe.wait_ge(o_ready, done(u - 1))
                    t0 = band(r) // 2 if band(r) % 2 == 0 else 8 + band(r) // 2
                    for i in range(4):
                        rhs = vtok[:, par, t0 + i, :]
                        last = pe.matmul(ps[:, 3, 0:P], probT[r % 2][:, i, :], rhs, start=(i == 0), stop=(i == 3))
                    last.then_inc(o_ps, 1)
                    run(fg, share - share // 2)
                    pe.wait_ge(o_ready, done(u))
                    pe.wait_ge(y_ready, done(u - 1))
                    pe.transpose(ps[:, 4, 0:P], o_bd[r % 2][:], ident[:]).then_inc(ot_ps, 1)
                    if n == PER and VT0 <= r < VT0 + 4:
                        g = r - VT0
                        pe.wait_ge(vt_evac, hp * 4 + 4 + g)
                        if g == 0:
                            pe.wait_ge(job_evac, hp * (2 * PER) + 2 * PRO + 6)
                        transpose_v(g)
                run(fg)

            with pe.Fori(0, PAIRS - 1) as hp:
                pair(hp, PER)
            pair(PAIRS - 1, LAST)

            pe.wait_ge(ld_bd, 16 * 8)
            pe.wait_ge(job_evac, 2 * GATE0)

            def lru_gates(n):
                cc, d = n // 2, n % 2
                pe.wait_ge(xc_ready, cc + 1)
                if n:
                    pe.wait_ge(lru_read, n)
                for g in range(2):
                    for h in range(2):
                        last = pe.matmul(ps[:, 2 * g + h, :], bd[:, (2 * g + d) * BC + cc, :], xc[cc % 2][:, HF[h]], start=True, stop=True)
                last.then_inc(lru_ps, 1)

            def channel_dft(g):
                if g:
                    pe.wait_ge(f_done, g)
                for t in range(TT):
                    last = pe.matmul(ps[:, 4 + t // 2, (t % 2) * 2 * P:(t % 2 + 1) * 2 * P], lx[:, 2, g, t * P:(t + 1) * P], chan[:],
                                     start=True, stop=True)
                last.then_inc(z_ps, 1)

            def position_dft(g):
                pe.wait_ge(z_ready, g + 1)
                for bank, tab, off in ((4, t_cos, 0), (5, t_sin, P)):
                    for odd in range(2):
                        fr = slice(2 * P * odd, 2 * P * (odd + 1))
                        for t in range(TT // 2):
                            pe.matmul(ps[:, bank, fr], z[:, odd, t, off:off + P], tab[:, t, fr], start=(t == 0), stop=(t == TT // 2 - 1))
                for t in range(TT // 2):
                    last = pe.matmul(ps[:, 6, 0:1], z[:, 0, t, 0:P], t_nyq[:, t:t + 1], start=(t == 0), stop=(t == TT // 2 - 1))
                last.then_inc(f_ps, 1)

            lru_gates(0)
            pe.wait_ge(ld_chan, 16 * 2)
            for g in range(GROUPS):
                channel_dft(g)
                lru_gates(2 * g + 1)
                if g == 0:
                    pe.wait_ge(ld_dft, 16 * 2)
                position_dft(g)
                if g < GROUPS - 1:
                    lru_gates(2 * g + 2)

            branch = [y_na, lx[:, 2], lx[:, 1]]
            pe.wait_ge(lru_read, 2 * BC)
            with pe.Fori(0, KC // 2) as two:
                dc = two * 2
                for s in range(2):
                    for b in range(3):
                        m = dc * 3 + (3 * s + b)
                        k = m + GATE0
                        pe.wait_ge(ld_pr[b], dc * 16 + 16 * (s + 1))
                        if b == 2:
                            pe.wait_ge(lru_done, 4)
                        for h in range(2):
                            pe.wait_ge(gated, 2 * m + (h + GATED_PRIME - 3))
                            for kc in range(BC):
                                last = pe.matmul(ps[:, 2 * ((3 * s + b) % 2) + h, :], w_pr[b][:, kc, :], branch[b][:, kc, HF[h]], start=(kc == 0), stop=(kc == BC - 1))
                            last.then_inc(pr_ps, 1)
                        if b == 0:
                            pe.wait_ge(f_done, 4)
                        for h in range(2):
                            run(job_half_mms(k, (GATE0 + 3 * s + b) % 2, h, k + 1, 2 * k + (h - 1)))
                    pe.wait_ge(acc_ready, dc + (s + 2))
                    pe.wait_ge(mrow_ready, dc + (s + 1))
                    pe.matmul(ps[0:1, 4, :], ones_f[:], acc[:], start=True, stop=True).then_inc(acc_ps, 1)

            pe.wait_ge(gated, GATED_ALL)
            for t in range(TT + 2):
                if t < TT:
                    for h in range(2):
                        q = 2 * t + h
                        if t == 0:
                            pe.wait_ge(ld_wo[h], 16)
                        if q >= 4:
                            pe.wait_ge(x1_half, q - 3)
                        for kc in range(KC):
                            last = pe.matmul(ps[:, q % 4, :], merged[:, kc, t * P:(t + 1) * P], wo[:, h, kc, :], start=(kc == 0), stop=(kc == KC - 1))
                        last.then_inc(mo_ps, 1)
                if 2 <= t:
                    pe.wait_ge(u2T_ready, t - 1)
                    if t == 2:
                        pe.wait_ge(ld_out, 16 * 3)
                    for kc in range(KC):
                        last = pe.matmul(ps[:, 6, (t - 2) * NE:(t - 1) * NE], u2T[:, kc, :], wr[:, kc, :], start=(kc == 0), stop=(kc == KC - 1))
                    last.then_inc(ro_ps, 1)
                if 1 <= t <= TT:
                    pe.wait_ge(u2_ready, t)
                    v = u2[:, t - 1, :].rearrange("p (q c) -> p c q", c=KC)
                    for kc in range(KC):
                        last = pe.transpose(ps[:, 4 + kc // 4, (kc % 4) * P:(kc % 4 + 1) * P], v[:, kc, :], ident[:])
                    last.then_inc(x2t_ps, 1)

            pe.wait_ge(hit_ready, 1)
            for t in range(TT):
                for t2 in range(t + 1):
                    pe.matmul(ps[:, 7, t * NE:(t + 1) * NE], (before_b if t2 == t else ones_b)[:], hit_b[:, t2, :], start=(t2 == 0), stop=(t2 == t))
            for t in range(TT):
                last = pe.matmul(ps[:, 7, TT * NE:(TT + 1) * NE], ones_b[:], hit_b[:, t, :], start=(t == 0), stop=(t == TT - 1))
            last.then_inc(rank_ps, 1)

            def rows_to_features(part):
                v = xg[:].rearrange("p (q c) -> p c q", c=KC)
                for kc in range(4 * part, 4 * part + 4):
                    last = pe.transpose(ps[:, kc // 4, (kc % 4) * P:(kc % 4 + 1) * P], v[:, kc, :], ident[:])
                if part:
                    last.then_inc(xg_ps, 1)

            def products(bank, w, e, x_hi, x_lo, cols, x_lo_wait=None):
                _, hi, lo, _ = WT[w]
                n = x_hi.shape[1]
                for kc in range(n):
                    if kc % (n // 2) == 0:
                        pe.wait_ge(lo_ready[w], e * 2 + (2 * kc // n + 1))
                    pe.matmul(ps[:, bank, :], x_hi[:, kc, :], hi[:, kc, cols], start=(kc == 0), stop=False)
                    pe.matmul(ps[:, bank, :], x_hi[:, kc, :], lo[:, kc, cols], start=False, stop=False)
                if x_lo_wait is not None:
                    pe.wait_ge(*x_lo_wait)
                for kc in range(n):
                    last = pe.matmul(ps[:, bank, :], x_lo[:, kc, :], hi[:, kc, cols], start=False, stop=(kc == n - 1))
                return last

            pe.wait_ge(starts_ready, 1)
            pe.wait_ge(ld_xg, 16)
            rows_to_features(0)
            rows_to_features(1)
            hv = act[:].rearrange("p (q c) -> p c q", c=FC)
            with pe.Fori(0, NE) as e:
                first = pe.value_load(starts[0:1, bass.ds(e, 1)], min_val=0, max_val=NBLK)
                end = pe.value_load(starts[0:1, bass.ds(e + 1, 1)], min_val=1, max_val=NBLK)
                with pe.Fori(first, end) as j:
                    pe.wait_ge(xgT_ready, j + 1)
                    products(2, "g", e, xgT_hi, xgT_lo, HF[0]).then_inc(g_ps, 1)
                    products(3, "u", e, xgT_hi, xgT_lo, HF[0]).then_inc(h_ps, 1)
                    pe.wait_ge(ld_xg, j * 16 + 32)
                    rows_to_features(0)
                    pe.wait_ge(h_ready, j + 1)
                    for fc in range(FC):
                        last = pe.transpose(ps[:, 4, fc * P:(fc + 1) * P], hv[:, fc, :], ident[:])
                    last.then_inc(ht_ps, 1)
                    rows_to_features(1)
                    pe.wait_ge(actT_hi_ready, j + 1)
                    pe.wait_ge(y_evac, j + 1)
                    products(5, "d", e, actT_hi, actT_lo, HF[0], (actT_ready, j + 1))
                    products(6, "d", e, actT_hi, actT_lo, HF[1]).then_inc(y_ps, 1)

        @block.scalar
        def _(sc):
            ch = Chain(sc, ch_act)
            for s_, n_ in ((p_ready, PRIME), (pt_ready, PRIME), (y_ready, PRIME), (y_evac, 1), (st_y, 16), (mrow_ready, 1), (st_mod, 16)):
                sc.sem_inc(s_, n_)
            sc.wait_ge(ld_const, 16 * 6)
            sc.activation(cact[:], cvec[:], ACT.Silu).then_inc(cact_ready, 1)
            for t in range(TT):
                sc.wait_ge(ld_x[t], 16)
                ch(sc.activation(junk[:], xn[:, t, :], ACT.Square, accum_out=ms[:, t:t + 1]))
            sc.activation(rstd[:], ms[:], ACT.Copy).then_inc(ms_ready, 1)
            sc.wait_ge(ms_ready, 2)
            sc.activation(ms[:], rstd[:], ACT.Sqrt).then_inc(root_ready, 1)
            sc.wait_ge(lam_in, 1)
            sc.activation(lam_t[:, 1], lam_t[:, 0], ACT.Exp, scale=-1.0).then_inc(lam_exp, 1)
            sc.wait_ge(lam_in, 2)
            sc.activation(lam_t[:, 3], lam_t[:, 2], ACT.Ln).then_inc(lam_ln, 1)
            for n in range(2 * KC):
                kc, th = n % KC, n // KC
                sc.wait_ge(xt_full, n + 1)
                sc.activation(u_hi[:, kc, HF[th]], u_full[n % 4][:], ACT.Copy).then_inc(u_hi_ready, 1)

            def evac(k, h, dst, scale=1.0):
                sc.wait_ge(job_half, 2 * k + (h + 1))
                hold(sc)
                sc.activation(dst, ps[:, 5 + h, :], ACT.Copy, scale=scale).then_inc(job_evac, 1)

            for k in range(PRO):
                for h in range(2):
                    evac(k, h, (qT[:, 0, HF[h]], kT[:, 0, HF[h]], vT[:, HF[h]])[k], DH ** -0.5 if k == 0 else 1.0)

            def exps(r, u):
                sc.wait_ge(s_biased, done(u))
                sc.wait_ge(o_ready, done(u - 2))
                sc.activation(prob[r % 2][:], prob[r % 2][:], ACT.Exp, bias=nmax[:, r % 2:r % 2 + 1],
                              accum_out=rsum[:, r % 2:r % 2 + 1]).then_inc(p_ready, 1)

            exps(0, 0)

            def pair(hp, n):
                nxt = (hp + 1) % 2
                for r in range(ROWS):
                    u = hp * ROWS + r
                    sc.wait_ge(pt_ps, done(u))
                    sc.wait_ge(o_ps, done(u - 2))
                    sc.activation(probT[r % 2][:].rearrange("p a b -> p (a b)"), ps[:, 2 + 5 * (r % 2), :], ACT.Copy).then_inc(pt_ready, 1)
                    if r < ROWS - 1:
                        exps(r + 1, u + 1)
                    elif n == PER:
                        exps(0, u + 1)
                    for i in range(n):
                        for h in range(2):
                            if finish_unit(n, i, h) == r:
                                k = hp * PER + PRO + i
                                if n == PER and i < 3:
                                    dst = (qT[:, nxt, HF[h]], kT[:, nxt, HF[h]], vT[:, HF[h]])[i]
                                else:
                                    ii = i - 3 if n == PER else i
                                    dst = lx[:, ii, hp, HF[h]]
                                evac(k, h, dst, DH ** -0.5 if n == PER and i == 0 else 1.0)
                    sc.wait_ge(ot_ps, done(u))
                    hold(sc)
                    for side in range(2):
                        sl = slice(64 * side, 64 * side + 64)
                        dst = y_na[sl, hp, r * GRID_W:(r + 1) * GRID_W]
                        ins = sc.activation(dst, ps[sl, 4, BACK[side]], ACT.Copy)
                        if side:
                            ins.then_inc(y_ready, 1)

            with sc.Fori(0, PAIRS - 1) as hp:
                pair(hp, PER)
            pair(PAIRS - 1, LAST)

            sc.wait_ge(job_evac, 2 * GATE0)
            sc.activation(lx[:, 1], lx[:, 1], ACT.Gelu_apprx_tanh).then_inc(gelu_ready, 1)
            sc.wait_ge(decay_ready, 1)

            flat = lambda a: a.rearrange("p a b -> p (a b)")
            for cc in range(BC):
                for d in range(2):
                    n = 2 * cc + d
                    sc.wait_ge(lru_ps, n + 1)
                    if cc:
                        sc.wait_ge(*((lru_free, n - 1) if d == 0 else (lru_sum, cc)))
                    ch.mark(sc.activation(t_a[d][:], flat(ps[:, 0:2, :]), ACT.Tanh, scale=0.5, bias=lru_b[:, d, cc:cc + 1]))
                    sc.activation(t_b[d][:], flat(ps[:, 2:4, :]), ACT.Tanh, scale=0.5, bias=lru_b[:, 2 + d, cc:cc + 1]).then_inc(lru_read, 1)
                    if d == 0:
                        sc.wait_ge(z_ps, cc + 1)
                        sc.activation(flat(z_first[:]), flat(ps[:, 4:6, :]), ACT.Copy).then_inc(z_copied, 1)
                    ch.sync()
                    dec, dec2 = decay[:, d, cc:cc + 1], decay2[:, d, cc:cc + 1]
                    ch.mark(sc.activation(t_c[d][:], t_a[d][:], ACT.Exp, scale=dec, bias=dec))
                    if n:
                        sc.wait_ge(lru_rad, n)
                    ch(sc.activation(t_d[:], t_a[d][:], ACT.Exp, scale=dec2, bias=dec2))
                    sc.activation(t_a[d][:], t_a[d][:], ACT.Tanh, scale=dec, bias=dec).then_inc(lru_act, 1)
                sc.wait_ge(f_ps, cc + 1)
                if cc:
                    sc.wait_ge(f_done, cc)
                sc.activation(sin_part[:], ps[:, 5, :], ACT.Copy).then_inc(f_sin, 1)
                for d in range(2):
                    sc.wait_ge(lru_rad, 2 * cc + d + 1)
                    sc.activation(t_a[d][:], t_a[d][:], ACT.Sqrt, scale=-1.0).then_inc(lru_root, 1)

            with sc.Fori(0, KC // 2) as two:
                dc = two * 2
                for s in range(2):
                    for b in range(3):
                        m = dc * 3 + (3 * s + b)
                        for h in range(2):
                            sc.wait_ge(job_half, 2 * (m + GATE0) + (h + 1))
                            sc.wait_ge(gated, 2 * m + (h + GATED_PRIME - 1))
                            hold(sc)
                            sc.activation(gate[h][:], ps[:, 5 + h, :], ACT.Sigmoid,
                                          bias=bg[:, bass.ds(dc + (s + BRANCH[b] // P), 1)]).then_inc(job_evac, 1)
                    sc.wait_ge(acc_ps, dc + (s + 1))
                    sc.wait_ge(st_mod, dc * 16 + 16 * (s + 1))
                    hold(sc)
                    sc.activation(mrow[:], ps[0:1, 4, :], ACT.Copy).then_inc(mrow_ready, 1)
                    sc.wait_ge(mrow_ready, dc + (s + 2))
                    sc.dma_start(d_mod.rearrange("v n -> (v n)").unsqueeze(0)[:, bass.ds((dc + s) * HALF, HALF)], mrow[:]).then_inc(st_mod, 16)

            for t in range(TT):
                sc.wait_ge(x1_half, 2 * t + 2)
                sc.activation(u2[:, t, :], x1[:, t, :], ACT.Square, accum_out=ms2[:, t:t + 1]).then_inc(ms2_ready, 1)
                sc.wait_ge(root2, 2 * t + 1)
                sc.activation(ms2[:, t:t + 1], rstd2[:, t:t + 1], ACT.Sqrt).then_inc(root2, 1)
            sc.wait_ge(ro_ps, TT)
            sc.activation(dd["score"][:].rearrange("p a b -> p (a b)"), ps[:, 6, 0:TT * NE], ACT.Sigmoid).then_inc(score_ready, 1)

            sc.wait_ge(st_u2, 16 * TT)
            for w in "gud":
                sc.wait_ge(ld_raw[w], 16)
                for half in range(2):
                    split_hi(w, half)

            def gate_half(j):
                sc.wait_ge(g_ps, j + 1)
                sc.activation(act[:], ps[:, 2, :], ACT.Silu).then_inc(silu_ready, 1)

            def transposed(j):
                sc.wait_ge(ht_ps, j + 1)
                sc.activation(actT_hi[:].rearrange("p a b -> p (a b)"), ps[:, 4, :], ACT.Copy).then_inc(actT_hi_ready, 1)
                next_rows(j + 1)

            def next_rows(j):
                sc.wait_ge(xg_ps, j + 1)
                sc.activation(xgT_hi[:].rearrange("p a b -> p (a b)"), ps[:, 0:2, :].rearrange("p a b -> p (a b)"), ACT.Copy).then_inc(xgT_hi_ready, 1)

            def output(j):
                sc.wait_ge(y_ps, j + 1)
                sc.wait_ge(st_y, j * 16 + 16)
                sc.activation(yb[:], ps[:, 5:7, :].rearrange("p a b -> p (a b)"), ACT.Copy).then_inc(y_evac, 1)
                sc.wait_ge(y_evac, j + 2)
                hold(sc)
                sc.dma_start(d_y[bass.ds(j * CAP, CAP), :], yb[:]).then_inc(st_y, 16)

            def next_hi(w, e, used, end):
                sc.wait_ge(used, end)
                sc.wait_ge(ld_raw[w], e * 16 + 32)
                hold(sc)
                for half in range(2):
                    split_hi(w, half)

            def expert_blocks(e):
                first = sc.value_load(starts[0:1, bass.ds(e, 1)], min_val=0, max_val=NBLK)
                end = sc.value_load(starts[0:1, bass.ds(e + 1, 1)], min_val=1, max_val=NBLK)
                with sc.If(first + 1 < end):
                    with sc.Fori(first, end - 1) as j:
                        gate_half(j)
                        transposed(j)
                        output(j)
                return end

            sc.wait_ge(st_pad, 16)
            sc.wait_ge(starts_ready, 1)
            next_rows(0)
            with sc.Fori(0, NE - 1) as e:
                end = expert_blocks(e)
                gate_half(end - 1)
                next_hi("g", e, g_ps, end)
                transposed(end - 1)
                next_hi("u", e, h_ps, end)
                output(end - 1)
                next_hi("d", e, y_ps, end)
            end = expert_blocks(NE - 1)
            gate_half(end - 1)
            transposed(end - 1)
            output(end - 1)

            for t in range(TT + 1):
                if t < TT:
                    y = y0[t % YBUF]
                    sc.wait_ge(ld_y[t % YBUF], 32 * (t // YBUF + 1))
                    sc.activation(y[:], y[:], ACT.Copy, scale=pair_w[:, 0, t:t + 1]).then_inc(y_scaled, 1)
                if t:
                    m = t - 1
                    sc.wait_ge(fin_ready_x, m + 1)
                    sc.activation(junk2[:], x1[:, m, :], ACT.Square, accum_out=ms2[:, m:m + 1]).then_inc(fin_ms, 1)
                    sc.wait_ge(fin_root, 2 * m + 1)
                    sc.activation(ms2[:, m:m + 1], rstd2[:, m:m + 1], ACT.Sqrt).then_inc(fin_root, 1)

        @block.vector
        def _(dve):
            ch = Chain(dve, ch_dve)
            for s_, n_ in ((s_biased, PRIME), (o_ready, PRIME), (gated, GATED_PRIME), (q_staged, PRIME), (acc_ready, 1)):
                dve.sem_inc(s_, n_)
            dve.wait_ge(cact_ready, 1)
            dve.tensor_copy(crep[:], cact[:].unsqueeze(2).to_broadcast([P, KC, P])).then_inc(crep_ready, 1)
            dve.wait_ge(ms_ready, 1)
            dve.tensor_scalar(rstd[:], rstd[:], 1.0 / D, EPS, MUL, ADD).then_inc(ms_ready, 1)
            dve.wait_ge(root_ready, 1)
            ch(dve.reciprocal(rstd[:], ms[:]))
            for t in range(TT):
                dve.tensor_scalar(xn[:, t, :], xn[:, t, :], rstd[:, t:t + 1], None, MUL).then_inc(xn_ready, 1)

            def mod_vector(v):
                dve.wait_ge(ada_used, 2 * v + 2)
                row = ps[:, 2 * (v % 2):2 * (v % 2) + 2, :].rearrange("p a b -> p (a b)")
                v3 = lambda a: a.rearrange("p (q c) -> p q c", c=KC)
                dve.tensor_tensor(v3(modtmp[:]), v3(row), ident[:].unsqueeze(2).to_broadcast([P, P, KC]), MUL).then_inc(mod_read, 1)
                dve.wait_ge(mod_read, v + 1)
                ch(dve.tensor_reduce(modv[:, v, :], modtmp[:].rearrange("p (q c) -> p c q", c=KC), AX.X, ADD))
                ch(dve.tensor_tensor(modv[:, v, :], modv[:, v, :], mod_b[:, v, :], ADD))
                if v == 1:
                    ch(dve.scalar_tensor_tensor(u_scale[:, 0, :], modv[:, v, :], 1.0, norm_g[:, 0, :], ADD, MUL))

            dve.wait_ge(ld_const, 16 * 6)
            mod_vector(0)
            dve.wait_ge(ld_small, 16 * 12)
            ch(dve.tensor_scalar(decay[:], lam[:], -1.0, None, MUL))
            dve.tensor_tensor(lam_t[:, 0], decay[:], lam[:], ALU.max).then_inc(lam_in, 1)
            dve.wait_ge(lam_exp, 1)
            dve.tensor_scalar(lam_t[:, 2], lam_t[:, 1], 1.0, None, ADD).then_inc(lam_in, 1)
            dve.wait_ge(lam_ln, 1)
            dve.wait_ge(lam_in, 2)
            ch(dve.tensor_scalar(lam_t[:, 2], lam_t[:, 2], 1.0, None, SUB))
            ch(dve.tensor_scalar(lam_t[:, 0], lam_t[:, 2], 0.0, None, ALU.is_equal))
            ch(dve.tensor_tensor(lam_t[:, 2], lam_t[:, 2], lam_t[:, 0], ADD))
            ch(dve.reciprocal(lam_t[:, 2], lam_t[:, 2]))
            ch(dve.tensor_tensor(lam_t[:, 3], lam_t[:, 3], lam_t[:, 2], MUL))
            ch(dve.tensor_tensor(lam_t[:, 3], lam_t[:, 3], lam_t[:, 0], ADD))
            ch(dve.tensor_tensor(lam_t[:, 3], lam_t[:, 3], lam_t[:, 1], MUL))
            ch(dve.scalar_tensor_tensor(decay[:], decay[:], 0.0, lam_t[:, 3], ALU.max, ADD))
            ch.mark(dve.tensor_scalar(lru_b[:], lru_b[:], 0.5, None, MUL))
            ch(dve.tensor_scalar(decay2[:], decay[:], -8.0, None, MUL))
            ch.mark(dve.memset(ones_f[:], 1.0))
            dve.tensor_scalar(decay[:], decay[:], -4.0, None, MUL).then_inc(decay_ready, 1)
            mod_vector(1)
            for n in range(2 * KC + 1):
                if n < 2 * KC:
                    kc = n % KC
                    dve.wait_ge(xt_ps, n + 1)
                    if n >= 4:
                        dve.wait_ge((u_lo_even, u_lo_odd)[n % 2], n // 2 - 1)
                    dve.tensor_scalar(u_full[n % 4][:], ps[:, XBANK[n % 4], :], u_scale[:, 0, kc:kc + 1], modv[:, 0, kc:kc + 1], MUL, ADD).then_inc(xt_full, 1)
                if n % 2:
                    m = n - 1
                    dst = slice(m // KC * HALF, (m // KC + 1) * HALF)
                    dve.wait_ge(u_hi_ready, m + 1)
                    dve.tensor_tensor(u_lo[:, m % KC, dst], u_full[m % 4][:], u_hi[:, m % KC, dst].bitcast(f32), SUB).then_inc(u_lo_even, 1)

            def v_tiles(g, par):
                n = min(4, 15 - 4 * g)
                dst = vtok[:, par, 4 * g:4 * g + n, :]
                dve.tensor_copy(dst, ps[:, 1, 0:n * P].rearrange("p (a b) -> p a b", b=P)).then_inc(vt_evac, 1)

            def stage_q(r, par):
                for side in range(2):
                    sl = slice(64 * side, 64 * side + 64)
                    ins = dve.tensor_copy(q_bd[r % 2][sl, BACK[side]], qT[sl, par, r * GRID_W:(r + 1) * GRID_W])
                    if side:
                        ins.then_inc(q_staged, 1)

            ch.mark(dve.memset(q_bd[0][:], 0.0))
            ch.mark(dve.memset(q_bd[1][:], 0.0))
            ch.mark(dve.memset(o_bd[0][:], 0.0))
            ch.mark(dve.memset(o_bd[1][:], 0.0))
            for g in range(4):
                dve.wait_ge(vt_ps, g + 1)
                v_tiles(g, 0)
            ch.sync()
            dve.wait_ge(job_evac, 2)
            stage_q(0, 0)
            stage_q(1, 0)
            dve.wait_ge(bias_ready, 1)

            def biased(r, u, par):
                dve.wait_ge(s_ps, done(u))
                dve.wait_ge(pt_ps, done(u - 2))
                d0 = (band(r) - r + WIN_R - 1) * GRID_W
                ch(dve.tensor_tensor(prob[r % 2][:], ps[:, 0, :], bias[:, par, d0:d0 + HALF], ADD))
                dve.tensor_reduce(nmax[:, r % 2:r % 2 + 1], prob[r % 2][:], AX.X, ALU.max, negate=True).then_inc(s_biased, 1)

            biased(0, 0, 0)

            def pair(hp, n):
                par = hp % 2
                nxt = (hp + 1) % 2
                for r in range(ROWS):
                    u = hp * ROWS + r
                    if r < ROWS - 1:
                        biased(r + 1, u + 1, par)
                    elif n == PER:
                        dve.wait_ge(bias_ready, hp + 2)
                        biased(0, u + 1, nxt)
                    if r < ROWS - 2:
                        stage_q(r + 2, par)
                    elif n == PER:
                        if r == ROWS - 2:
                            dve.wait_ge(job_evac, hp * (2 * PER) + 2 * PRO + 2)
                        stage_q(r + 2 - ROWS, nxt)
                    dve.wait_ge(o_ps, done(u))
                    dve.wait_ge(p_ready, done(u))
                    ch(dve.reciprocal(rinv[:, r % 2:r % 2 + 1], rsum[:, r % 2:r % 2 + 1]))
                    dve.wait_ge(ot_ps, done(u - 2))
                    for side in range(2):
                        sl = slice(64 * side, 64 * side + 64)
                        ins = dve.tensor_scalar(o_bd[r % 2][sl, sl], ps[sl, 3, sl], rinv[sl, r % 2:r % 2 + 1], None, MUL)
                        if side:
                            ins.then_inc(o_ready, 1)
                    if n == PER and VT0 <= r < VT0 + 4:
                        g = r - VT0
                        dve.wait_ge(vt_ps, hp * 4 + (g + 5))
                        v_tiles(g, nxt)

            with dve.Fori(0, PAIRS - 1) as hp:
                ch.enter(hp, 2 * ROWS)
                pair(hp, PER)
                ch.leave(PAIRS - 1)
            pair(PAIRS - 1, LAST)

            dve.wait_ge(y_ready, ATT_ALL)
            dve.wait_ge(job_evac, 2 * GATE0)

            def conv(cc):
                xr, o = lx[:, 0, cc, :], xc[cc % 2]
                if cc > 1:
                    dve.wait_ge(lru_ps, 2 * cc - 2)
                ch(dve.tensor_scalar(o[:], xr, conv_w[:, 2, cc:cc + 1], conv_b[:, cc:cc + 1], MUL, ADD))
                ch(dve.scalar_tensor_tensor(o[:, 2:], xr[:, :T - 2], conv_w[:, 0, cc:cc + 1], o[:, 2:], MUL, ADD))
                ch(dve.scalar_tensor_tensor(o[:, 1:], xr[:, :T - 1], conv_w[:, 1, cc:cc + 1], o[:, 1:], MUL, ADD))
                dve.scalar_tensor_tensor(o[:, :T - 1], xr[:, 1:], conv_w[:, 3, cc:cc + 1], o[:, :T - 1], MUL, ADD).then_inc(xc_ready, 1)
                dve.wait_ge(xc_ready, cc + 1)

            conv(0)
            conv(1)
            for cc in range(BC):
                xr = lx[:, 0, cc, :]
                dve.wait_ge(z_copied, cc + 1)
                second = ps[:, 6:8, :].rearrange("p a b -> p (a b)")
                first = z_first[:].rearrange("p a b -> p (a b)")
                ch.mark(dve.tensor_tensor(z[:, 0].rearrange("p a b -> p (a b)"), first, second, ADD))
                dve.tensor_tensor(z[:, 1].rearrange("p a b -> p (a b)"), first, second, SUB).then_inc(z_ready, 1)
                for d in range(2):
                    dve.wait_ge(lru_act, 2 * cc + d + 1)
                    dve.scalar_tensor_tensor(t_a[d][:], t_d[:], 1.0, t_a[d][:], ADD, MUL).then_inc(lru_rad, 1)
                    ch.mark(dve.scalar_tensor_tensor(t_b[d][:], t_b[d][:], 1.0, xc[cc % 2][:], ADD, MUL))
                ch.sync()
                g = cc
                fy = lx[:, 2, g, :]
                dve.wait_ge(f_sin, g + 1)
                cos2, sin2 = ps[:, 4, :].rearrange("p (e m) -> p e m", e=2), sin_part[:].rearrange("p (e m) -> p e m", e=2)
                ch.mark(dve.tensor_tensor(fy[:, 0:HALF].rearrange("p (m e) -> p e m", e=2), cos2, sin2, SUB))
                ch.mark(dve.tensor_tensor(fy[:, T - 2:HALF:-2], cos2[:, 0, 1:], sin2[:, 0, 1:], ADD))
                ch.mark(dve.tensor_tensor(fy[:, T - 1:HALF:-2], cos2[:, 1, :], sin2[:, 1, :], ADD))
                dve.tensor_copy(fy[:, HALF:HALF + 1], ps[:, 6, 0:1]).then_inc(f_done, 1)
                for d in range(2):
                    dve.wait_ge(lru_root, 2 * cc + d + 1)
                    ch(dve.scalar_tensor_tensor(t_a[d][:], t_a[d][:], 0.5, t_b[d][:], MUL, MUL))
                    if d == 0:
                        dve.tensor_tensor_scan(xr, t_c[0][:], t_a[0][:], 0.0, MUL, ADD).then_inc(lru_free, 1)
                    else:
                        dve.tensor_tensor_scan(t_b[1][:, ::-1], t_c[1][:, ::-1], t_a[1][:, ::-1], 0.0, MUL, ADD).then_inc(lru_free, 1)
                if cc + 2 < BC:
                    conv(cc + 2)

            with dve.Fori(0, KC // 2) as two:
                dc = two * 2
                ch.enter(two, 8 + 2 * (KC - 1))
                for s in range(2):
                    for b in range(3):
                        m = dc * 3 + (3 * s + b)
                        for h in range(2):
                            dve.wait_ge(job_evac, 2 * (m + GATE0) + (h + 1))
                            dve.wait_ge(pr_ps, 2 * m + (h + 1 + PR_PRIME))
                            dst = merged[:, dc + s, HF[h]]
                            proj = ps[:, 2 * ((3 * s + b) % 2) + h, :]
                            if b == 0:
                                dve.tensor_tensor(dst, gate[h][:], proj, MUL).then_inc(gated, 1)
                            else:
                                ch(dve.tensor_tensor(part[:], gate[h][:], proj, MUL))
                                dve.wait_ge(gated, 2 * m + (h + GATED_PRIME - 1))
                                dve.tensor_tensor(dst, dst, part[:], ADD).then_inc(gated, 1)
                                dve.wait_ge(gated, 2 * m + (h + GATED_PRIME + 1))
                        if b == 0:
                            dve.wait_ge(ld_mod, dc * 16 + 16 * (s + 1))
                            for kc in range(KC):
                                if kc == 0:
                                    ins = dve.tensor_scalar(acc[:], ada_g[:, 0, :], cact[:, 0:1], None, MUL)
                                else:
                                    ins = dve.scalar_tensor_tensor(acc[:], ada_g[:, kc, :], cact[:, kc:kc + 1], acc[:], MUL, ADD)
                                if kc == KC - 1:
                                    ins.then_inc(acc_ready, 1)
                                else:
                                    ch(ins)
                ch.leave(KC // 2)

            dve.wait_ge(ld_out, 16 * 3)
            ch(dve.tensor_tensor(gmix[:], gmix[:], gmix_b[:], ADD))
            dve.wait_ge(ld_rows, 16 * 5)
            ch.mark(dve.tensor_tensor(sh_row[:], sh_row[:], sh_b[:], ADD))
            ch(dve.tensor_tensor(sc_row[:], sc_row[:], sc_b[:], ADD))
            ch(dve.scalar_tensor_tensor(sc_row[:], sc_row[:], 1.0, g_row[:], ADD, MUL))
            for t in range(TT + 1):
                if t < TT:
                    dve.wait_ge(ld_x1[t], 16)
                    for h in range(2):
                        dve.wait_ge(mo_ps, 2 * t + h + 1)
                        ch(dve.tensor_tensor(mixed[:], ps[:, (2 * t + h) % 4, :], gmix[:, HF[h]], MUL))
                        dve.tensor_tensor(x1[:, t, HF[h]], x1[:, t, HF[h]], mixed[:], ADD).then_inc(x1_half, 1)
                        dve.wait_ge(x1_half, 2 * t + h + 1)
                if t:
                    m = t - 1
                    dve.wait_ge(ms2_ready, m + 1)
                    dve.tensor_scalar(rstd2[:, m:m + 1], ms2[:, m:m + 1], 1.0 / D, EPS, MUL, ADD).then_inc(root2, 1)
                    dve.wait_ge(root2, 2 * m + 2)
                    ch(dve.reciprocal(rstd2[:, m:m + 1], ms2[:, m:m + 1]))
                    ch(dve.scalar_tensor_tensor(u2[:, m, :], x1[:, m, :], rstd2[:, m:m + 1], sc_row[:], MUL, MUL))
                    dve.tensor_tensor(u2[:, m, :], u2[:, m, :], sh_row[:], ADD).then_inc(u2_ready, 1)
                    dve.wait_ge(x2t_ps, m + 1)
                    dve.tensor_copy(u2T[:].rearrange("p a b -> p (a b)"), ps[:, 4:6, :].rearrange("p a b -> p (a b)")).then_inc(u2T_ready, 1)

            t3 = lambda n: dd[n][:]
            g4 = lambda a: a.rearrange("p t (g e) -> p (t g) e", e=EPG)
            dve.wait_ge(mo_ps, 2 * TT)
            ch.mark(dve.memset(ones_b[:], 1.0))
            for g in range(NG):
                ch.mark(dve.memset(gidx[:, g:g + 1], float(g - NG)))
            dve.wait_ge(ld_rt, 32)
            ch(dve.tensor_copy(before_b[:], before[:]))
            dve.wait_ge(score_ready, 1)
            ch(dve.tensor_tensor(t3("sel"), t3("score"), rbias[:].unsqueeze(1).to_broadcast([P, TT, NE]), ADD))
            pt = [pairt[:, i].rearrange("p t g -> p (t g)") for i in range(8)]
            se = [g4(t3("sel"))[:, :, e] for e in range(EPG)]
            tt = lambda o, a, b, op: ch(dve.tensor_tensor(o, a, b, op))
            tt(pt[0], se[0], se[1], ALU.max)
            tt(pt[1], se[0], se[1], ALU.min)
            tt(pt[2], se[2], se[3], ALU.max)
            tt(pt[3], se[2], se[3], ALU.min)
            tt(pt[4], pt[0], pt[2], ALU.max)
            tt(pt[5], pt[0], pt[2], ALU.min)
            tt(pt[1], pt[1], pt[3], ALU.max)
            tt(pt[5], pt[5], pt[1], ALU.max)
            tt(pt[4], pt[4], pt[5], ADD)
            gs = pairt[:, 4]
            top = slot_f[:, 0, :]
            bc8 = lambda a: a.unsqueeze(2).to_broadcast([P, TT, NG])
            gi = gidx[:].unsqueeze(1).to_broadcast([P, TT, NG])
            ch(dve.tensor_reduce(top, gs, AX.X, ALU.max))
            tt(pairt[:, 6], gs, bc8(top), ALU.is_equal)
            tt(pairt[:, 6], pairt[:, 6], gi, MUL)
            ch(dve.tensor_reduce(top, pairt[:, 6], AX.X, ALU.min))
            tt(pairt[:, 7], gi, bc8(top), ALU.is_equal)
            rk = g4(t3("ta"))
            for e in range(EPG):
                ch(dve.memset(rk[:, :, e], float(EPG - 1 - e)))
            for a in range(EPG):
                for b in range(a + 1, EPG):
                    tt(pt[0], se[a], se[b], ALU.is_ge)
                    tt(rk[:, :, b], rk[:, :, b], pt[0], ADD)
                    tt(rk[:, :, a], rk[:, :, a], pt[0], SUB)
            ch(dve.scalar_tensor_tensor(g4(t3("hit")), rk, 1.5, pt[7].unsqueeze(2).to_broadcast([P, TT * NG, EPG]), ALU.is_lt, MUL))
            dve.tensor_copy(hit_b[:], t3("hit")).then_inc(hit_ready, 1)
            bc32 = lambda a: a.unsqueeze(2).to_broadcast([P, TT, NE])
            tt(t3("wgt"), t3("score"), t3("hit"), MUL)
            ch(dve.tensor_reduce(top, t3("wgt"), AX.X, ADD))
            ch(dve.reciprocal(top, top))
            tt(t3("wgt"), t3("wgt"), bc32(top), MUL)
            dve.wait_ge(rank_ps, 1)
            ch(dve.tensor_copy(cnt[:, 0, 0:NE], ps[:, 7, TT * NE:(TT + 1) * NE]))
            ch.mark(dve.memset(cnt[:, 1, :], 1.0))
            ch.mark(dve.memset(cnt[:, 3, :], 1.0))
            ch(dve.memset(cnt[:, 2, :], 0.0))
            for b in range(1, T // CAP):
                ch(dve.scalar_tensor_tensor(cnt[:, 1, 0:NE], cnt[:, 0, 0:NE], float(CAP * b), cnt[:, 1, 0:NE], ALU.is_gt, ADD))
            ch(dve.tensor_tensor_scan(cnt[:, 2, 1:NE + 1], cnt[:, 3, 0:NE], cnt[:, 1, 0:NE], 0.0, MUL, ADD))
            dve.tensor_copy(starts[:], cnt[0:1, 2, :]).then_inc(starts_ready, 1)
            ch(dve.tensor_scalar(cnt[:, 3, 0:NE], cnt[:, 2, 0:NE], float(CAP), 1.0, MUL, ADD))
            tt(t3("slot"), ps[:, 7, 0:TT * NE].rearrange("p (t e) -> p t e", e=NE), cnt[:, 3, 0:NE].unsqueeze(1).to_broadcast([P, TT, NE]), ADD)
            tt(t3("slot"), t3("slot"), t3("hit"), MUL)
            for k in range(2):
                top = slot_f[:, k, :]
                ch(dve.tensor_reduce(top, t3("slot"), AX.X, ALU.max))
                tt(t3("ta"), t3("slot"), bc32(top), ALU.is_equal)
                tt(t3("tb"), t3("ta"), t3("wgt"), MUL)
                ch(dve.tensor_reduce(pair_w[:, k, :], t3("tb"), AX.X, ADD))
                if k == 0:
                    tt(t3("ta"), t3("ta"), t3("slot"), MUL)
                    tt(t3("slot"), t3("slot"), t3("ta"), SUB)
            ch(dve.tensor_scalar(slot_f[:], slot_f[:], 1.0, None, SUB))
            ch(dve.tensor_copy(pair_s[:], slot_f[:]))
            ch(dve.tensor_single_scalar(slot_u[:], pair_s[:], CAP - 1, ALU.bitwise_and))
            ch(dve.tensor_single_scalar(slot_t[:], pair_s[:], 7, ALU.arith_shift_right))
            dve.scalar_tensor_tensor(slot_t[:], slot_u[:], float(LIST), slot_t[:], MUL, ADD).then_inc(slots_ready, 1)

            def hidden(j):
                dve.wait_ge(silu_ready, j + 1)
                dve.wait_ge(h_ps, j + 1)
                dve.tensor_tensor(act[:], act[:], ps[:, 3, :], MUL).then_inc(h_ready, 1)

            def hidden_rest(j):
                dve.wait_ge(actT_hi_ready, j + 1)
                dve.tensor_tensor(actT_lo[:].rearrange("p a b -> p (a b)"), ps[:, 4, :], actT_hi[:].rearrange("p a b -> p (a b)").bitcast(f32), SUB).then_inc(actT_ready, 1)

            def next_rows(j):
                dve.wait_ge(xgT_hi_ready, j + 1)
                dve.tensor_tensor(xgT_lo[:].rearrange("p a b -> p (a b)"), ps[:, 0:2, :].rearrange("p a b -> p (a b)"),
                                  xgT_hi[:].rearrange("p a b -> p (a b)").bitcast(f32), SUB).then_inc(xgT_ready, 1)

            def next_lo(w, e, half):
                dve.wait_ge(hi_ready[w], e * 2 + (half + 3))
                hold(dve)
                split_lo(dve, w, half)

            def expert_blocks(e):
                first = dve.value_load(starts[0:1, bass.ds(e, 1)], min_val=0, max_val=NBLK)
                end = dve.value_load(starts[0:1, bass.ds(e + 1, 1)], min_val=1, max_val=NBLK)
                with dve.If(first + 1 < end):
                    with dve.Fori(first, end - 1) as j:
                        hidden(j)
                        hidden_rest(j)
                        next_rows(j + 1)
                return end

            dve.wait_ge(starts_ready, 1)
            next_rows(0)
            with dve.Fori(0, NE - 1) as e:
                end = expert_blocks(e)
                hidden(end - 1)
                next_lo("g", e, 0)
                hidden_rest(end - 1)
                next_lo("g", e, 1)
                next_rows(end)
                for w in "ud":
                    next_lo(w, e, 0)
                    next_lo(w, e, 1)
            end = expert_blocks(NE - 1)
            hidden(end - 1)
            hidden_rest(end - 1)
            next_rows(end)

            ce = Chain(dve, ch_end)
            dve.wait_ge(ld_end, 16 * 3)
            ce(dve.tensor_tensor(gffn[:], gffn[:], gffn_b[:], ADD))
            for t in range(TT + 1):
                if t < TT:
                    y = y0[t % YBUF][:]
                    dve.wait_ge(y_scaled, t + 1)
                    ce(dve.scalar_tensor_tensor(y, y1[t % YBUF][:], pair_w[:, 1, t:t + 1], y, MUL, ADD))
                    ce(dve.tensor_tensor(y, y, gffn[:], MUL))
                    dve.tensor_tensor(x1[:, t, :], x1[:, t, :], y, ADD).then_inc(fin_ready_x, 1)
                if t:
                    m = t - 1
                    dve.wait_ge(fin_ms, m + 1)
                    dve.tensor_scalar(rstd2[:, m:m + 1], ms2[:, m:m + 1], 1.0 / D, EPS, MUL, ADD).then_inc(fin_root, 1)
                    dve.wait_ge(fin_root, 2 * m + 2)
                    ce(dve.reciprocal(rstd2[:, m:m + 1], ms2[:, m:m + 1]))
                    if m >= 2:
                        dve.wait_ge(st_out[m % 2], 16 * (m // 2))
                    dve.scalar_tensor_tensor(res[m % 2][:], x1[:, m, :], rstd2[:, m:m + 1], fing[:], MUL, MUL).then_inc(fin_ready, 1)


_INS = ["x", "c", "ada_w", "ada_b", "norm_mix_g", "norm_ffn_g", "w_in", "w_branch_gate", "b_branch_gate",
        "na_rpb", "lru_conv_w", "lru_conv_b", "lru_w_r", "lru_b_r", "lru_w_i", "lru_b_i", "lru_lambda",
        "w_proj_na", "w_proj_lru", "w_proj_fnet", "w_out", "w_router", "router_bias",
        "w_exp_gate", "w_exp_up", "w_exp_down", "final_g"]


def constants():
    w, cc = np.arange(GRID_W)[:, None], np.arange(GRID_W)[None, :]
    start = np.clip(w - WIN_C // 2, 0, GRID_W - WIN_C)
    window = np.where((cc >= start) & (cc < start + WIN_C), 0.0, NEG)
    j = np.arange(P)
    chan = 2 * np.pi * (np.outer(j, j) % P) / P
    t, k = np.arange(T // 2), np.concatenate([np.arange(0, HALF, 2), np.arange(1, HALF, 2)])
    pos = 2 * np.pi * (np.outer(t, k) % T) / T
    f = lambda a: np.ascontiguousarray(a, dtype=np.float32)
    return {
        "k_ident": f(np.eye(P)),
        "k_window": f(np.concatenate([window[::-1], window[::-1]])),
        "k_before": f(np.triu(np.ones((P, P)), 1)),
        "k_chan": f(np.concatenate([np.cos(chan), np.sin(chan)], 1) / np.sqrt(P)),
        "k_cos": f(np.cos(pos) / np.sqrt(T)),
        "k_sin": f(np.sin(pos) / np.sqrt(T)),
        "k_nyq": f(np.broadcast_to(((-1.0) ** j)[:, None] / np.sqrt(T), (P, TT // 2))),
    }


def kernel(**inputs):
    import numpy as _np
    import concourse.bacc as _bacc
    from concourse import mybir as _mybir
    from concourse.bass_utils import run_bass_kernel_spmd as _run

    nc = _bacc.Bacc("TRN2", target_bir_lowering=False, num_devices=1)
    arrays, args = {}, []
    consts = constants()
    for name in _INS + list(consts):
        a = _np.ascontiguousarray(consts[name] if name in consts else inputs[name])
        arrays[f"in_{name}"] = a
        args.append(nc.dram_tensor(f"in_{name}", a.shape, _mybir.dt.from_np(a.dtype), kind="ExternalInput").ap())
    args.append(nc.dram_tensor("out_0", (1, T, D), _mybir.dt.float32, kind="ExternalOutput").ap())
    build(nc, *args)
    r = _run(nc, [arrays], core_ids=[0])
    return r.results[0]["out_0"]
```

```python
import concourse.bass as bass
from concourse import mybir
from contextlib import ExitStack
import numpy as np

D = 1024
T = 1024
P = 128
TT = T // P
KC = D // P
HALF = 512
GRID_W, ROWS = 64, 16
DH = 64
HEADS = 8
PAIRS = HEADS // 2
WIN_R, WIN_C = 8, 16
NREL = 2 * WIN_R - 1
RELC = 2 * WIN_C - 1
RPAD = 128
BW = 512
BC = BW // P
GROUPS = 4
NE, NG, EPG = 32, 8, 4
FE = 512
FC = FE // P
CAP = 128
NBLK = 2048 // CAP + NE
LIST = NBLK + 1
EPS = 1e-6
NEG = -1e30
YBUF = 4
PRIME = 2


def done(n):
    return n + 1 + PRIME


class Chain:

    def __init__(self, eng, sem):
        self.eng, self.sem, self.n, self.dyn = eng, sem, 0, None

    def mark(self, ins):
        ins.then_inc(self.sem, 1)
        self.n += 1

    def sync(self):
        self.eng.wait_ge(self.sem, self.n if self.dyn is None else self.dyn + self.n)

    def __call__(self, ins):
        self.mark(ins)
        self.sync()

    def enter(self, turn, per):
        self.base, self.per, self.dyn = self.n, per, turn * per

    def leave(self, turns):
        assert self.n - self.base == self.per, (self.n - self.base, self.per)
        self.n, self.dyn = self.base + self.per * turns, None


def band(r):
    return min(max(r - WIN_R // 2, 0), ROWS - WIN_R)


def build(nc, x, c, ada_w, ada_b, norm_mix_g, norm_ffn_g, w_in, w_branch_gate, b_branch_gate,
          na_rpb, lru_conv_w, lru_conv_b, lru_w_r, lru_b_r, lru_w_i, lru_b_i, lru_lambda,
          w_proj_na, w_proj_lru, w_proj_fnet, w_out, w_router, router_bias,
          w_exp_gate, w_exp_up, w_exp_down, final_g,
          k_ident, k_window, k_before, k_chan, k_cos, k_sin, k_nyq, out):
    f32, f32r, i32, bf16 = mybir.dt.float32, mybir.dt.float32r, mybir.dt.int32, mybir.dt.bfloat16
    ALU, ACT, AX = mybir.AluOpType, mybir.ActivationFunctionType, mybir.AxisListType
    ADD, SUB, MUL = ALU.add, ALU.subtract, ALU.mult

    ctx = ExitStack()
    with ctx:
        ctx.enter_context(nc.allow_non_contiguous_dma("small parameter vectors are laid channel-major"))
        base = (nc.sbuf_base + 63) // 64 * 64

        def at(name, kb, shape, dt=f32):
            return nc.alloc_sbuf_tensor_at(name, shape, dt, offset=base + int(kb * 1024))

        def sem(name):
            return ctx.enter_context(nc.semaphore(name))

        xn = at("xn", 96, [P, TT, D])
        ada = [at(f"ada{i}", kb, [P, KC, HALF]) for i, kb in enumerate((128, 144, 80))]
        junk = at("junk", 199, [P, D])
        modtmp = at("modtmp", 68, [P, D])
        crep = at("crep", 72, [P, KC, P])
        u_hi = at("u_hi", 0, [P, KC, T], f32r)
        u_lo = at("u_lo", 32, [P, KC, T], f32r)
        u_full = [at(f"u_full{i}", kb, [P, HALF]) for i, kb in enumerate((64, 66, 76, 78))]
        y_na = at("y_na", 64, [P, BC, T])
        lx = at("lx", 80, [P, 3, BC, T])
        qT = at("qT", 128, [P, 2, T])
        kT = at("kT", 136, [P, 2, T])
        vT = at("vT", 144, [P, T])
        vtok = at("vtok", 148, [P, 2, 15, P])
        bias = at("bias", 163, [P, 2, NREL * GRID_W])
        window = at("window", 170.5, [P, GRID_W])
        w_raw = [at(f"w_raw{i}", 171 + 4 * i, [P, KC, P]) for i in range(2)]
        w_hi = [at(f"w_hi{i}", 179 + 4 * i, [P, KC, P], f32r) for i in range(2)]
        w_lo = [at(f"w_lo{i}", 187 + 4 * i, [P, KC, P], f32r) for i in range(2)]
        prob = [at(f"prob{i}", 195 + 2 * i, [P, HALF]) for i in range(2)]
        probT = [at(f"probT{i}", 199 + 2 * i, [P, 4, P]) for i in range(2)]
        q_bd = [at(f"q_bd{i}", 203 + 0.5 * i, [P, P]) for i in range(2)]
        o_bd = [at(f"o_bd{i}", 204 + 0.5 * i, [P, P]) for i in range(2)]
        rpb_pad = at("rpb_pad", 195, [HEADS * NREL, RPAD])
        t_cos = at("t_cos", 128, [P, TT // 2, HALF])
        t_sin = at("t_sin", 136, [P, TT // 2, HALF])
        bd = at("bd", 144, [P, 16, P])
        chan = at("chan", 152, [P, 2 * P])
        t_nyq = at("t_nyq", 153, [P, TT // 2])
        z_first = at("z_first", 154, [P, TT // 2, 2 * P])
        z = at("z", 158, [P, 2, TT // 2, 2 * P])
        sin_part = at("sin_part", 166, [P, HALF])
        xc = [at(f"xc{i}", 168 + 4 * i, [P, T]) for i in range(2)]
        t_a = [at(f"t_a{i}", 176 + 4 * i, [P, T]) for i in range(2)]
        t_b = [at(f"t_b{i}", 184 + 4 * i, [P, T]) for i in range(2)]
        t_c = [at(f"t_c{i}", 192 + 4 * i, [P, T]) for i in range(2)]
        t_d = at("t_d", 200, [P, T])
        zero_row = at("zero_row", 204, [P, 2 * P])
        merged = at("merged", 128, [P, KC, T])
        w_pr = at("w_pr", 160, [P, BC, P])
        w_pr_hi = [at(f"w_pr_hi{i}", 162 + 2 * i, [P, BC, P], f32r) for i in range(2)]
        w_pr_lo = [at(f"w_pr_lo{i}", 166 + 2 * i, [P, BC, P], f32r) for i in range(2)]
        gate = [at(f"gate{i}", 175 + 2 * i, [P, HALF]) for i in range(2)]
        br_tmp = [at(f"br_tmp{i}", 175 + 2 * i, [P, HALF], f32r) for i in range(2)]
        part = at("part", 195, [P, HALF])
        mrow = at("mrow", 197, [1, HALF])
        acc = at("acc", 199, [P, HALF])
        ada_g = at("ada_g", 201, [P, 2, HALF])
        br_hi = [at(f"br_hi{i}", kb, [P, BC, T], f32r) for i, kb in enumerate((64, 112, 96))]
        br_lo = at("br_lo", 80, [P, BC, T], f32r)
        x1 = at("x1", 0, [P, TT, D])
        u2 = at("u2", 32, [P, TT, D])
        wo = [at(f"wo{h}", 64 + 48 * h, [P, KC, HALF]) for h in range(2)]
        wo_lo = [at(f"wo_lo{h}", 64 + 48 * h, [P, KC, HALF], f32r) for h in range(2)]
        wo_hi = [at(f"wo_hi{h}", 160 + 16 * h, [P, KC, HALF], f32r) for h in range(2)]
        m_hi = [at(f"m_hi{i}", 96 + 4 * i, [P, KC, P], f32r) for i in range(2)]
        m_lo = [at(f"m_lo{i}", 104 + 4 * i, [P, KC, P], f32r) for i in range(2)]
        gmix = at("gmix", 192, [P, D])
        gmix_b = at("gmix_b", 80, [P, D])
        sc_row = at("sc_row", 84, [P, D])
        sh_row = at("sh_row", 88, [P, D])
        g_row = at("g_row", 92, [P, D])
        sc_b = at("sc_b", 56, [P, D])
        sh_b = at("sh_b", 60, [P, D])
        u2T = at("u2T", 196, [P, KC, P])
        mixed = at("mixed", 200, [P, HALF])
        wr = at("wr", 202, [P, KC, NE])
        raw_g, raw_u, raw_d = (at("raw_" + n, 64 + 16 * i, shp) for i, (n, shp) in enumerate((("g", [P, KC, FE]), ("u", [P, KC, FE]), ("d", [P, FC, D]))))
        wg_hi, wu_hi, wd_hi = (at(n + "_hi", kb, shp, f32r) for n, kb, shp in (("wg", 32, [P, KC, FE]), ("wu", 48, [P, KC, FE]), ("wd", 112, [P, FC, D])))
        wg_lo, wu_lo, wd_lo = (at(n + "_lo", kb, shp, f32r) for n, kb, shp in (("wg", 128, [P, KC, FE]), ("wu", 144, [P, KC, FE]), ("wd", 160, [P, FC, D])))
        xg = at("xg", 176, [P, D])
        xgT_hi = at("xgT_hi", 180, [P, KC, P], f32r)
        xgT_lo = at("xgT_lo", 184, [P, KC, P], f32r)
        act = at("act", 188, [P, FE])
        actT_hi = at("actT_hi", 190, [P, FC, P], f32r)
        actT_lo = at("actT_lo", 192, [P, FC, P], f32r)
        yb = at("yb", 194, [P, D])
        y0 = [at(f"y0_{i}", 64 + 4 * i, [P, D]) for i in range(YBUF)]
        y1 = [at(f"y1_{i}", 80 + 4 * i, [P, D]) for i in range(YBUF)]
        gffn = at("gffn", 96, [P, D])
        gffn_b = at("gffn_b", 100, [P, D])
        fing = at("fing", 104, [P, D])
        res = [at(f"res{i}", 112 + 4 * i, [P, D]) for i in range(2)]
        junk2 = at("junk2", 120, [P, D])

        NM = ["score", "sel", "hit", "wgt", "rank", "slot", "ta", "tb"]
        dd = {n: at("r_" + n, 176 + i, [P, TT, NE]) for i, n in enumerate(NM)}
        hit_b = at("hit_b", 184, [P, TT, NE], bf16)
        before_b = at("before_b", 185, [P, P], bf16)
        ones_b = at("ones_b", 185.5, [P, P], bf16)
        before = at("before", 186, [P, P])
        rbias = at("rbias", 186.5, [P, NE])
        cnt = at("cnt", 186.75, [P, 4, NE + 1])
        pairt = at("pairt", 187.5, [P, 8, TT, NG])
        slot_f = at("slot_f", 189.5, [P, 2, TT])
        slot_t = at("slot_t", 189.75, [P, 2, TT], i32)
        slot_u = at("slot_u", 190, [P, 2, TT], i32)
        gidx = at("gidx", 190.25, [P, NG])

        cur = [205.0]

        def small(name, shape, dt=f32):
            n = 1
            for s in shape[1:]:
                n *= s
            t = at(name, cur[0], shape, dt)
            cur[0] += (n * 4 + 31) // 32 * 32 / 1024
            assert base + cur[0] * 1024 <= nc.sbuf_usable_end, name
            return t

        ident = small("ident", [P, P])
        cvec = small("cvec", [P, KC])
        cact = small("cact", [P, KC])
        ms = small("ms", [P, TT])
        rstd = small("rstd", [P, TT])
        mod_b = small("mod_b", [P, 2, KC])
        norm_g = small("norm_g", [P, KC])
        modv = small("modv", [P, 2, KC])
        u_scale = small("u_scale", [P, KC])
        nmax = small("nmax", [P, 2])
        rsum = small("rsum", [P, 2])
        rinv = small("rinv", [P, 2])
        conv_w = small("conv_w", [P, 4, BC])
        conv_b = small("conv_b", [P, BC])
        lru_b = small("lru_b", [P, 4, BC])
        lam = small("lam", [P, 2, BC])
        lam_t = small("lam_t", [P, 4, 2, BC])
        decay = small("decay", [P, 2, BC])
        decay2 = small("decay2", [P, 2, BC])
        ones_f = small("ones_f", [P, 1])
        bg = small("bg", [P, 3 * KC])
        ms2 = small("ms2", [P, TT])
        rstd2 = small("rstd2", [P, TT])
        tok_cur = small("tok_cur", [P, 1], i32)
        tok = small("tok", [P, TT], i32)
        tokl = small("tokl", [P, LIST], i32)
        pair_w = small("pair_w", [P, 2, TT])
        pair_s = small("pair_s", [P, 2, TT], i32)
        starts = small("starts", [1, NE + 1], i32)
        zero_i = small("zero_i", [P, LIST], i32)

        ps = ctx.enter_context(nc.psum_tensor("ps", [P, 8, HALF], f32))

        d_rpb = nc.dram_tensor("d_rpb", (HEADS * NREL, RPAD), f32, kind="Internal")
        d_mod = nc.dram_tensor("d_mod", (4, D), f32, kind="Internal").ap()
        d_u2 = nc.dram_tensor("d_u2", (T, D), f32, kind="Internal").ap()
        d_list = nc.dram_tensor("d_list", (P * LIST, 1), i32, kind="Internal").ap()
        d_y = nc.dram_tensor("d_y", (NBLK * CAP, D), f32, kind="Internal").ap()

        held = sem("held")
        ch_dve, ch_act, ch_pool = sem("ch_dve"), sem("ch_act"), sem("ch_pool")
        ld_const, ld_small = sem("ld_const"), sem("ld_small")
        ld_x = [sem(f"ld_x{t}") for t in range(TT)]
        ld_ada = [sem(f"ld_ada{i}") for i in range(3)]
        ada_used = sem("ada_used")
        cact_ready, crep_ready, ms_ready, root_ready, xn_ready = (sem(n) for n in ("cact_ready", "crep_ready", "ms_ready", "root_ready", "xn_ready"))
        mod_read, ld_mod, ada_done, acc_ps, mrow_ready, st_mod = (sem(n) for n in ("mod_read", "ld_mod", "ada_done", "acc_ps", "mrow_ready", "st_mod"))
        xt_ps, xt_full, u_hi_ready, u_lo_even, u_lo_odd = (sem(n) for n in ("xt_ps", "xt_full", "u_hi_ready", "u_lo_even", "u_lo_odd"))
        ld_w = [sem(f"ld_w{i}") for i in range(2)]
        w_split, job_half, job_evac = sem("w_split"), sem("job_half"), sem("job_evac")
        vt_ps, vt_evac = sem("vt_ps"), sem("vt_evac")
        q_staged, s_ps, s_biased, p_ready, pt_ps, pt_ready, o_ps, o_ready, ot_ps, y_ready = (sem("at_" + n) for n in (
            "q_staged", "s_ps", "s_biased", "p_ready", "pt_ps", "pt_ready", "o_ps", "o_ready", "ot_ps", "y_ready"))
        rpb_set, rpb_in, rpb_out, bias_ready = (sem(n) for n in ("rpb_set", "rpb_in", "rpb_out", "bias_ready"))
        ld_bias = sem("ld_bias")
        bd_zero, ld_bd, ld_chan, ld_dft = sem("bd_zero"), sem("ld_bd"), sem("ld_chan"), sem("ld_dft")
        lam_act, lam_in, decay_ready = (sem(n) for n in ("lam_act", "lam_in", "decay_ready"))
        gelu_ready, xc_ready, lru_ps, lru_read, lru_free, lru_sum, lru_act, lru_rad, lru_root, lru_done = (sem(n) for n in (
            "gelu_ready", "xc_ready", "lru_ps", "lru_read", "lru_free", "lru_sum", "lru_act", "lru_rad", "lru_root", "lru_done"))
        z_ps, z_copied, z_ready, f_ps, f_sin, f_done = (sem(n) for n in ("z_ps", "z_copied", "z_ready", "f_ps", "f_sin", "f_done"))
        ld_pr, pr_split, br_tmp_ready, br_ready = (sem(n) for n in ("ld_pr", "pr_split", "br_tmp_ready", "br_ready"))
        pr_ps, gated = sem("pr_ps"), sem("gated")
        ld_wo = [sem(f"ld_wo{h}") for h in range(2)]
        wo_hi_ready, wo_ready, m_hi_ready, m_ready = (sem(n) for n in ("wo_hi_ready", "wo_ready", "m_hi_ready", "m_ready"))
        ld_gmix = sem("ld_gmix")
        ld_rows = sem("ld_rows")
        mo_ps, x1_half, ms2_ready, root2, u2_ready, x2t_ps, u2T_ready, ro_ps = (sem(n) for n in (
            "mo_ps", "x1_half", "ms2_ready", "root2", "u2_ready", "x2t_ps", "u2T_ready", "ro_ps"))
        st_u2, st_zero = sem("st_u2"), sem("st_zero")
        ld_rt, score_ready, hit_ready, rank_ps, slots_ready, starts_ready, st_list, ld_list, tok_ready = (sem(n) for n in (
            "ld_rt", "score_ready", "hit_ready", "rank_ps", "slots_ready", "starts_ready", "st_list", "ld_list", "tok_ready"))
        ld_raw = {w: sem("e_ld_" + w) for w in "gud"}
        hi_ready = {w: sem("e_hi_" + w) for w in "gud"}
        lo_ready = {w: sem("e_lo_" + w) for w in "gud"}
        ld_xg, xg_ps, xgT_hi_ready, xgT_ready, g_ps, h_ps, silu_ready, h_ready, ht_ps, actT_hi_ready, actT_ready, y_ps, y_evac, st_y = (
            sem("e_" + n) for n in ("ld_xg", "xg_ps", "xgT_hi", "xgT", "g_ps", "h_ps", "silu", "h_ready", "ht_ps", "actT_hi", "actT", "y_ps", "y_evac", "st_y"))
        zero_set, st_pad = sem("zero_set"), sem("st_pad")
        ld_end, fin_ms, fin_root, fin_ready, fin_ready_x = (sem(n) for n in ("ld_end", "fin_ms", "fin_root", "fin_ready", "fin_ready_x"))
        ld_y = [sem(f"ld_y{i}") for i in range(YBUF)]
        y_scaled = sem("y_scaled")
        st_out = [sem(f"st_out{i}") for i in range(2)]

        chan_major = lambda v: v.rearrange("(p c) -> p c", c=KC)
        chunked = lambda v: v.rearrange("(c p) -> p c", p=P)
        ada_v = ada_w[0].rearrange("(p c) n -> p c n", c=KC)
        w_in_v = w_in[0].rearrange("(p c) n -> p c n", c=KC)
        w_bg_v = w_branch_gate[0].rearrange("(p c) n -> p c n", c=KC)
        x_v = x[0].rearrange("(t p) d -> p t d", p=P)
        out_v = out[0].rearrange("(t p) d -> p t d", p=P)
        proj_v = [w[0].rearrange("(c p) n -> p c n", p=P) for w in (w_proj_na, w_proj_fnet, w_proj_lru)]
        wo_v = w_out[0].rearrange("(c p) n -> p c n", p=P)
        wr_v = w_router.rearrange("(p c) n -> p c n", c=KC)
        wg_v = w_exp_gate[0].rearrange("e (p c) n -> e p c n", c=KC)
        wu_v = w_exp_up[0].rearrange("e (p c) n -> e p c n", c=KC)
        wd_v = w_exp_down[0].rearrange("e (p c) n -> e p c n", c=FC)
        u2_d = d_u2.rearrange("(t p) d -> p t d", p=P)

        PRO, PER, LAST = 3, 6, 3
        KIND0 = [0, BW, 2 * BW]
        KIND1 = [3 * BW, 4 * BW, 5 * BW]
        GATE0 = PRO + PER * (PAIRS - 1) + LAST
        BRANCH = [0, 2 * D, D]
        VT0 = 9
        XBANK = [4, 7, 0, 1]
        MM = 24
        HF = [slice(0, HALF), slice(HALF, T)]
        BACK = [slice(63, None, -1), slice(127, 63, -1)]

        def finish_unit(n_jobs, i, h):
            return (MM * (2 * i + h + 1) - 1) // (n_jobs * 2 * MM // ROWS)

        GATED_PRIME = 4
        GATED_ALL = 6 * KC + GATED_PRIME
        PR_PRIME = 4
        ATT_ALL = done(PAIRS * ROWS - 1)

        WT = {"g": (raw_g, wg_hi, wg_lo, wg_v), "u": (raw_u, wu_hi, wu_lo, wu_v), "d": (raw_d, wd_hi, wd_lo, wd_v)}

        def half_of(a, half):
            n = a.shape[1] // 2
            return a[:, half * n:(half + 1) * n, :]

        def split_hi(w, half):
            raw, hi, _, _ = WT[w]
            nc.scalar.activation(half_of(hi, half), half_of(raw, half), ACT.Copy).then_inc(hi_ready[w], 1)

        def split_lo(eng, w, half):
            raw, hi, lo, _ = WT[w]
            eng.tensor_tensor(half_of(lo, half), half_of(raw, half), half_of(hi, half).bitcast(f32), SUB).then_inc(lo_ready[w], 1)

        def hold(eng):
            eng.sem_inc(held, 1)

        block = ctx.enter_context(nc.Block())

        @block.sync
        def _(sp):
            def load_w(k, par, cols):
                sp.wait_ge(w_split, k - 1)
                sp.dma_start(w_raw[par][:], cols).then_inc(ld_w[par], 16)

            for dst, src in ((cvec[:], c[0].rearrange("(p c) -> p c", c=KC)), (ident[:], k_ident), (window[:], k_window),
                             (mod_b[:], ada_b[0, :2 * D].rearrange("(v p c) -> p v c", v=2, c=KC)),
                             (norm_g[:], chan_major(norm_mix_g[0]))):
                sp.dma_start(dst, src).then_inc(ld_const, 16)
            for b in range(4):
                if b == 3:
                    for i in range(2):
                        sp.dma_start(w_raw[i][:], w_in_v[:, :, KIND0[i]:KIND0[i] + P]).then_inc(ld_w[i], 16)
                    sp.wait_ge(ada_used, 1)
                sp.dma_start(ada[b % 3][:], ada_v[:, :, b * HALF:(b + 1) * HALF]).then_inc(ld_ada[b % 3], 16)
            for t in range(TT):
                sp.dma_start(xn[:, t, :], x_v[:, t, :]).then_inc(ld_x[t], 16)
            load_w(2, 0, w_in_v[:, :, KIND0[2]:KIND0[2] + P])
            sp.wait_ge(rpb_set, 1)
            sp.dma_start(rpb_pad[:, 48:48 + RELC], na_rpb[0].rearrange("h r c -> (h r) c")).then_inc(rpb_in, 16)
            sp.wait_ge(rpb_in, 16)
            sp.dma_start(d_rpb.ap(), rpb_pad[:]).then_inc(rpb_out, 16)

            def load_bias(hp):
                for side in range(2):
                    src = bass.AP(d_rpb, ((2 * hp + side) * NREL) * RPAD, [[1, GRID_W], [RPAD, NREL], [1, GRID_W]])
                    dst = bias[64 * side:64 * side + 64, hp % 2, :].rearrange("p (r c) -> p r c", r=NREL)
                    sp.dma_start(dst, src).then_inc(ld_bias, 16)


            sp.wait_ge(rpb_out, 16)
            load_bias(0)
            for hp in range(PAIRS):
                kinds = ([(o, hp + 1) for o in KIND0] if hp < PAIRS - 1 else []) + [(o, hp) for o in KIND1]
                for i, (off, ch) in enumerate(kinds):
                    k = PRO + PER * hp + i
                    load_w(k, k % 2, w_in_v[:, :, off + ch * P:off + (ch + 1) * P])
                if hp < PAIRS - 1:
                    sp.wait_ge(bias_ready, hp + 1)
                    if hp:
                        sp.wait_ge(s_biased, done(ROWS * hp - 1))
                    load_bias(hp + 1)
            sp.wait_ge(bd_zero, 1)
            for g, w in enumerate((lru_w_r, lru_w_i)):
                for d in range(2):
                    for side in range(2):
                        src = w[0, d].rearrange("(c s) i j -> s i c j", s=2)[side]
                        dst = bd[64 * side:64 * side + 64, (2 * g + d) * BC:(2 * g + d + 1) * BC, 64 * side:64 * side + 64]
                        sp.dma_start(dst, src).then_inc(ld_bd, 16)
            sp.dma_start(chan[:], k_chan).then_inc(ld_chan, 16)
            sp.dma_start(t_nyq[:], k_nyq).then_inc(ld_chan, 16)
            sp.wait_ge(y_ready, ATT_ALL)
            sp.dma_start(t_cos[:], k_cos.rearrange("(t p) n -> p t n", p=P)).then_inc(ld_dft, 16)
            sp.dma_start(t_sin[:], k_sin.rearrange("(t p) n -> p t n", p=P)).then_inc(ld_dft, 16)
            sp.wait_ge(f_ps, 4)
            sp.wait_ge(f_done, 4)
            sp.wait_ge(lru_free, 7)
            for b in range(3):
                if b == 2:
                    sp.wait_ge(pr_ps, 2 * KC + PR_PRIME)
                    sp.dma_start(wo[0][:], wo_v[:, :, HF[0]]).then_inc(ld_wo[0], 16)
                with sp.Fori(0, KC // 2) as two:
                    for s in range(2):
                        dc = two * 2 + s
                        it = dc + b * KC
                        sp.wait_ge(w_split, it + GATE0)
                        hold(sp)
                        sp.dma_start(w_raw[0][:], w_bg_v[:, :, bass.ds(dc * P + BRANCH[b], P)]).then_inc(ld_w[s], 16)
                        sp.wait_ge(pr_split, it + 1)
                        hold(sp)
                        sp.dma_start(w_pr[:], proj_v[b][:, :, bass.ds(dc * P, P)]).then_inc(ld_pr, 16)
            sp.wait_ge(pr_ps, 4 * KC + PR_PRIME)
            sp.dma_start(wo[1][:], wo_v[:, :, HF[1]]).then_inc(ld_wo[1], 16)
            sp.wait_ge(gated, GATED_ALL)
            sp.wait_ge(st_mod, 16 * (KC + 1))
            sp.dma_start(gmix[:], d_mod[0].partition_broadcast(P)).then_inc(ld_gmix, 16)
            sp.dma_start(gmix_b[:], ada_b[0, 2 * D:3 * D].partition_broadcast(P)).then_inc(ld_gmix, 16)
            for t in range(TT):
                sp.dma_start(x1[:, t, :], x_v[:, t, :]).then_inc(ld_x[t], 16)
                if t == 1:
                    for dst, src in ((sc_row, d_mod[2]), (sc_b, ada_b[0, 4 * D:5 * D]), (g_row, norm_ffn_g[0]), (sh_row, d_mod[1]), (sh_b, ada_b[0, 3 * D:4 * D])):
                        sp.dma_start(dst[:], src.partition_broadcast(P)).then_inc(ld_rows, 16)
            sp.dma_start(wr[:], wr_v).then_inc(ld_rows, 16)
            for t in range(TT):
                sp.wait_ge(u2_ready, t + 1)
                sp.dma_start(u2_d[:, t, :], u2[:, t, :]).then_inc(st_u2, 16)
            sp.wait_ge(mo_ps, 2 * TT)
            sp.dma_start(before[:], k_before).then_inc(ld_rt, 16)
            sp.dma_start(rbias[:], router_bias.partition_broadcast(P)).then_inc(ld_rt, 16)
            for w in "gud":
                sp.dma_start(WT[w][0][:], WT[w][3][0]).then_inc(ld_raw[w], 16)
            def load_weights(e):
                for w in "gud":
                    sp.wait_ge(lo_ready[w], 2 * e)
                    sp.dma_start(WT[w][0][:], WT[w][3][e]).then_inc(ld_raw[w], 16)

            load_weights(1)
            sp.wait_ge(st_list, 16 * 2 * TT)
            sp.dma_start(tokl[:], d_list.rearrange("(p l) o -> p (l o)", p=P)).then_inc(ld_list, 16)
            with sp.Fori(2, NE) as e:
                load_weights(e)
            for w in "gud":
                sp.wait_ge(lo_ready[w], 2 * NE)
            sp.dma_start(gffn[:], d_mod[3].partition_broadcast(P)).then_inc(ld_end, 16)
            sp.dma_start(gffn_b[:], ada_b[0, 5 * D:6 * D].partition_broadcast(P)).then_inc(ld_end, 16)
            sp.dma_start(fing[:], final_g.partition_broadcast(P)).then_inc(ld_end, 16)
            for t in range(TT):
                sp.wait_ge(fin_ready, t + 1)
                sp.dma_start(out_v[:, t, :], res[t % 2][:]).then_inc(st_out[t % 2], 16)
            for i in range(2):
                sp.wait_ge(st_out[i], 16 * TT // 2)
            sp.wait_ge(st_u2, 16 * TT)


        @block.gpsimd
        def _(pool):
            ch = Chain(pool, ch_pool)
            pool.sem_inc(pr_split, 1)
            for dst, src in [(conv_w[:, j, :], chunked(lru_conv_w[0, j])) for j in range(4)] + [
                    (conv_b[:], chunked(lru_conv_b[0])), (bg[:], chunked(b_branch_gate[0]))] + [
                    (lru_b[:, 2 * g + d, :], chunked(v[0, d])) for g, v in enumerate((lru_b_r, lru_b_i)) for d in range(2)] + [
                    (lam[:, d, :], chunked(lru_lambda[0, d])) for d in range(2)]:
                pool.dma_start(dst, src).then_inc(ld_small, 16)
            ch.mark(pool.memset(zero_i[:], 0))
            ch(pool.iota(tok[:], [[P, TT]], base=0, channel_multiplier=1))
            pool.dma_start(d_list.rearrange("(p l) o -> p (l o)", p=P), zero_i[:]).then_inc(st_zero, 16)

            def split(k, par, need, wait_half, raw=None):
                pool.wait_ge(ld_w[par], need)
                if wait_half is not None:
                    pool.wait_ge(job_half, wait_half)
                hold(pool)
                raw = w_raw[par] if raw is None else raw
                ch(pool.tensor_copy(w_hi[par][:], raw[:]))
                pool.tensor_tensor(w_lo[par][:], raw[:], w_hi[par][:].bitcast(f32), SUB).then_inc(w_split, 1)

            pool.memset(rpb_pad[:], 0.0).then_inc(rpb_set, 1)
            split(0, 0, 16, None)
            split(1, 1, 16, None)

            for n in range(1, 2 * KC, 2):
                kc, th = n % KC, n // KC
                pool.wait_ge(u_hi_ready, n + 1)
                pool.tensor_tensor(u_lo[:, kc, HF[th]], u_full[n % 4][:], u_hi[:, kc, HF[th]].bitcast(f32), SUB).then_inc(u_lo_odd, 1)

            def mask_bias(sl, need):
                pool.wait_ge(ld_bias, need)
                b3 = bias[:, sl, :].rearrange("p (r c) -> p r c", c=GRID_W)
                win = window[:].unsqueeze(1).to_broadcast([P, NREL, GRID_W])
                pool.tensor_tensor(b3, b3, win, ADD).then_inc(bias_ready, 1)

            pool.wait_ge(ld_const, 16 * 5)
            split(2, 0, 32, 2)
            mask_bias(0, 32)

            def pair(hp, n):
                for i in range(n):
                    k = PER * hp + PRO + i
                    split(k, (PRO + i) % 2, hp * (PER * 8) + 16 * ((PRO + i) // 2 + 1), 2 * k - 2)

            with pool.Fori(0, PAIRS - 1) as hp:
                ch.enter(hp, PER)
                pair(hp, PER)
                ch.leave(PAIRS - 1)
                mask_bias((hp + 1) % 2, hp * 32 + 64)
            pair(PAIRS - 1, LAST)

            pool.wait_ge(y_ready, done((PAIRS - 1) * ROWS - 1))
            pool.memset(bd[:], 0.0).then_inc(bd_zero, 1)
            pool.wait_ge(y_ready, ATT_ALL)
            pool.memset(zero_row[:], 0.0).then_inc(zero_set, 1)
            pool.wait_ge(zero_set, 1)
            spare = NBLK - NE
            pool.dma_start(d_y[NE * CAP:, :].rearrange("(p k) (a n) -> p (k a) n", p=P, n=2 * P),
                           zero_row[:].unsqueeze(1).to_broadcast([P, spare * CAP * D // P // (2 * P), 2 * P])).then_inc(st_pad, 16)

            pool.wait_ge(gelu_ready, 1)
            for cc in range(BC - 1):
                xr, yr = lx[:, 0, cc, :], lx[:, 1, cc, :]
                pool.wait_ge(lru_free, 2 * cc + 2)
                pool.tensor_tensor(xr, xr, t_b[1][:], ADD).then_inc(lru_sum, 1)
                pool.wait_ge(lru_sum, cc + 1)
                pool.tensor_tensor(yr, xr, yr, MUL).then_inc(lru_done, 1)

            pool.wait_ge(lru_sum, BC)
            for b in range(3):
                with pool.Fori(0, KC // 2) as two:
                    ch.enter(two, 4)
                    for s in range(2):
                        it = two * 2 + (b * KC + s)
                        k = it + GATE0
                        split(k, s, two * 16 + 16 * ((GATE0 + b * KC) // 2 + 1), 2 * k - 2, w_raw[0])
                        pool.wait_ge(ld_pr, it * 16 + 16)
                        pool.wait_ge(pr_ps, 2 * it + (PR_PRIME - 2))
                        hold(pool)
                        ch(pool.tensor_copy(w_pr_hi[s][:], w_pr[:]))
                        pool.tensor_tensor(w_pr_lo[s][:], w_pr[:], w_pr_hi[s][:].bitcast(f32), SUB).then_inc(pr_split, 1)
                    ch.leave(KC // 2)

            for t in range(TT):
                pool.wait_ge(m_hi_ready, t + 1)
                pool.tensor_tensor(m_lo[t % 2][:], merged[:, :, t * P:(t + 1) * P], m_hi[t % 2][:].bitcast(f32), SUB).then_inc(m_ready, 1)

            for half in range(2):
                pool.wait_ge(hi_ready["g"], half + 1)
                split_lo(pool, "g", half)

            pool.wait_ge(slots_ready, 1)
            pool.wait_ge(st_zero, 16)
            for k in range(2):
                for t in range(TT):
                    pool.indirect_dma_start(out=d_list, out_offset=bass.IndirectOffsetOnAxis(ap=slot_t[:, k, t:t + 1], axis=0),
                                            in_=tok[:, t:t + 1], in_offset=None).then_inc(st_list, 16)

            nb = pool.value_load(starts[0:1, NE:NE + 1], min_val=NE, max_val=NBLK)
            pool.wait_ge(st_u2, 16 * TT)
            pool.wait_ge(ld_list, 16)
            pool.tensor_copy(tok_cur[:], tokl[:, 0:1]).then_inc(tok_ready, 1)
            pool.wait_ge(tok_ready, 1)
            pool.indirect_dma_start(out=xg[:], out_offset=None, in_=d_u2,
                                    in_offset=bass.IndirectOffsetOnAxis(ap=tok_cur[:], axis=0)).then_inc(ld_xg, 16)
            with pool.Fori(0, nb) as j:
                pool.wait_ge(xg_ps, j + 1)
                hold(pool)
                pool.tensor_copy(tok_cur[:], tokl[:, bass.ds(j + 1, 1)]).then_inc(tok_ready, 1)
                pool.wait_ge(tok_ready, j + 2)
                hold(pool)
                pool.indirect_dma_start(out=xg[:], out_offset=None, in_=d_u2,
                                        in_offset=bass.IndirectOffsetOnAxis(ap=tok_cur[:], axis=0)).then_inc(ld_xg, 16)

            pool.wait_ge(st_y, nb * 16 + 16)
            hold(pool)
            pool.wait_ge(st_pad, 16)
            for t in range(TT):
                if t >= YBUF:
                    pool.wait_ge(fin_ready_x, t - YBUF + 1)
                for k, y in enumerate((y0, y1)):
                    pool.indirect_dma_start(out=y[t % YBUF][:], out_offset=None, in_=d_y,
                                            in_offset=bass.IndirectOffsetOnAxis(ap=pair_s[:, k, t:t + 1], axis=0)).then_inc(ld_y[t % YBUF], 16)

        @block.tensor
        def _(pe):
            for s_, n_ in ((s_ps, PRIME), (pt_ps, PRIME), (o_ps, PRIME), (ot_ps, PRIME), (pr_ps, PR_PRIME), (acc_ps, 1)):
                pe.sem_inc(s_, n_)

            def mod_vector(v):
                for h in range(2):
                    b = 2 * v + h
                    pe.wait_ge(ld_ada[b % 3], 16 * (b // 3 + 1))
                    for kc in range(KC):
                        last = pe.matmul(ps[:, b % 4, :], crep[:, kc, :], ada[b % 3][:, kc, :], start=(kc == 0), stop=(kc == KC - 1))
                    last.then_inc(ada_used, 1)
            pe.wait_ge(crep_ready, 1)
            def x_features(n):
                kc, th = n % KC, n // KC
                pe.wait_ge(xn_ready, 4 * (th + 1))
                if n >= 4:
                    pe.wait_ge(xt_full, n - 3)
                for i in range(4):
                    src = xn[:, 4 * th + i, :].rearrange("p (q c) -> p c q", c=KC)[:, kc, :]
                    last = pe.transpose(ps[:, XBANK[n % 4], i * P:(i + 1) * P], src, ident[:])
                last.then_inc(xt_ps, 1)

            mod_vector(0)
            pe.wait_ge(ld_const, 16 * 5)
            mod_vector(1)
            pe.wait_ge(mod_read, 1)

            def job_half_mms(k, par, h, need_split, need_evac):
                def gen():
                    if h == 0:
                        pe.wait_ge(w_split, need_split)
                    if need_evac is not None:
                        pe.wait_ge(job_evac, need_evac)
                    n = 0
                    for kc in range(KC):
                        for a, b in ((w_hi, u_hi), (w_hi, u_lo), (w_lo, u_hi)):
                            n += 1
                            ins = pe.matmul(ps[:, 5 + h, :], a[par][:, kc, :], b[:, kc, HF[h]], start=(n == 1), stop=(n == MM))
                            if n == MM:
                                ins.then_inc(job_half, 1)
                            yield
                return gen()

            def run(gen, n=10 ** 9):
                for _ in range(n):
                    if next(gen, "end") == "end":
                        return

            def transpose_v(g):
                for i in range(4 * g, min(4 * g + 4, 15)):
                    t0 = i * P if i < 8 else (i - 8) * P + GRID_W
                    last = pe.transpose(ps[:, 1, (i % 4) * P:(i % 4 + 1) * P], vT[:, t0:t0 + P], ident[:])
                last.then_inc(vt_ps, 1)

            first_job = [job_half_mms(0, 0, h, 1, None) for h in range(2)]
            for n in range(2 * KC + 6):
                if n < 2 * KC:
                    x_features(n)
                m = n - 6
                if m >= 0:
                    pe.wait_ge((u_lo_even, u_lo_odd)[m % 2], m // 2 + 1)
                    run(first_job[m // KC], 3)
            for k in range(1, PRO):
                for h in range(2):
                    run(job_half_mms(k, k % 2, h, k + 1, 2 * k + h - 1))
            pe.wait_ge(job_evac, 2 * PRO)
            for g in range(4):
                if g:
                    pe.wait_ge(vt_evac, g)
                transpose_v(g)

            def scores(hp_k, r, u):
                pe.wait_ge(q_staged, done(u))
                pe.wait_ge(s_biased, done(u - 1))
                rs = band(r) * GRID_W
                rhs = kT[:, hp_k, rs:rs + HALF]
                pe.matmul(ps[:, 0, :], q_bd[r % 2][:], rhs, start=True, stop=True).then_inc(s_ps, 1)

            scores(0, 0, 0)

            def pair(hp, n):
                par = hp % 2
                nxt = (hp + 1) % 2
                share = 2 * MM * n // ROWS

                def fill():
                    for i in range(n):
                        k = hp * PER + PRO + i
                        for h in range(2):
                            yield from job_half_mms(k, (PRO + i) % 2, h, k + 1, 2 * k + h - 1)
                fg = fill()
                for r in range(ROWS):
                    u = hp * ROWS + r
                    if r < ROWS - 1:
                        scores(par, r + 1, u + 1)
                    elif n == PER:
                        scores(nxt, 0, u + 1)
                    pe.wait_ge(p_ready, done(u))
                    pe.wait_ge(pt_ready, done(u - 2))
                    for i in range(4):
                        last = pe.transpose(ps[:, 2 + 5 * (r % 2), i * P:(i + 1) * P], prob[r % 2][:, i * P:(i + 1) * P], ident[:])
                    last.then_inc(pt_ps, 1)
                    run(fg, share // 2)
                    pe.wait_ge(pt_ready, done(u))
                    pe.wait_ge(o_ready, done(u - 1))
                    t0 = band(r) // 2 if band(r) % 2 == 0 else 8 + band(r) // 2
                    for i in range(4):
                        rhs = vtok[:, par, t0 + i, :]
                        last = pe.matmul(ps[:, 3, 0:P], probT[r % 2][:, i, :], rhs, start=(i == 0), stop=(i == 3))
                    last.then_inc(o_ps, 1)
                    run(fg, share - share // 2)
                    pe.wait_ge(o_ready, done(u))
                    pe.wait_ge(y_ready, done(u - 1))
                    pe.transpose(ps[:, 4, 0:P], o_bd[r % 2][:], ident[:]).then_inc(ot_ps, 1)
                    if n == PER and VT0 <= r < VT0 + 4:
                        g = r - VT0
                        pe.wait_ge(vt_evac, hp * 4 + 4 + g)
                        if g == 0:
                            pe.wait_ge(job_evac, hp * (2 * PER) + 2 * PRO + 6)
                        transpose_v(g)
                run(fg)

            with pe.Fori(0, PAIRS - 1) as hp:
                pair(hp, PER)
            pair(PAIRS - 1, LAST)

            pe.wait_ge(ld_bd, 16 * 8)
            pe.wait_ge(job_evac, 2 * GATE0)

            def lru_gates(n):
                cc, d = n // 2, n % 2
                pe.wait_ge(xc_ready, cc + 1)
                if n:
                    pe.wait_ge(lru_read, n)
                for g in range(2):
                    for h in range(2):
                        last = pe.matmul(ps[:, 2 * g + h, :], bd[:, (2 * g + d) * BC + cc, :], xc[cc % 2][:, HF[h]], start=True, stop=True)
                last.then_inc(lru_ps, 1)

            def channel_dft(g):
                if g:
                    pe.wait_ge(f_done, g)
                for t in range(TT):
                    last = pe.matmul(ps[:, 4 + t // 2, (t % 2) * 2 * P:(t % 2 + 1) * 2 * P], lx[:, 2, g, t * P:(t + 1) * P], chan[:],
                                     start=True, stop=True)
                last.then_inc(z_ps, 1)

            def position_dft(g):
                pe.wait_ge(z_ready, g + 1)
                for bank, tab, off in ((4, t_cos, 0), (5, t_sin, P)):
                    for odd in range(2):
                        fr = slice(2 * P * odd, 2 * P * (odd + 1))
                        for t in range(TT // 2):
                            pe.matmul(ps[:, bank, fr], z[:, odd, t, off:off + P], tab[:, t, fr], start=(t == 0), stop=(t == TT // 2 - 1))
                for t in range(TT // 2):
                    last = pe.matmul(ps[:, 6, 0:1], z[:, 0, t, 0:P], t_nyq[:, t:t + 1], start=(t == 0), stop=(t == TT // 2 - 1))
                last.then_inc(f_ps, 1)

            lru_gates(0)
            pe.wait_ge(ld_chan, 16 * 2)
            for g in range(GROUPS):
                channel_dft(g)
                lru_gates(2 * g + 1)
                if g == 0:
                    pe.wait_ge(ld_dft, 16 * 2)
                position_dft(g)
                if g < GROUPS - 1:
                    lru_gates(2 * g + 2)

            pe.wait_ge(lru_read, 2 * BC)
            pe.wait_ge(f_done, 4)
            for b in range(3):
                with pe.Fori(0, KC // 2) as two:
                    for s in range(2):
                        it = two * 2 + (b * KC + s)
                        k = it + GATE0
                        for h in range(2):
                            run(job_half_mms(k, s, h, k + 1, 2 * k + (h - 1)))
                        pe.wait_ge(pr_split, it + 2)
                        pe.wait_ge(br_ready, 2 * BC * (b + 1))
                        for h in range(2):
                            pe.wait_ge(gated, 2 * it + (h + GATED_PRIME - 3))
                            n = 0
                            for kc in range(BC):
                                for w, x in ((w_pr_hi, br_hi[b]), (w_pr_hi, br_lo), (w_pr_lo, br_hi[b])):
                                    n += 1
                                    last = pe.matmul(ps[:, 2 * s + h, :], w[s][:, kc, :], x[:, kc, HF[h]], start=(n == 1), stop=(n == 3 * BC))
                            last.then_inc(pr_ps, 1)
                    if b < 2:
                        blk = two + b * (KC // 2)
                        pe.wait_ge(ada_done, blk * 4 + 5)
                        pe.wait_ge(mrow_ready, blk + 1)
                        pe.matmul(ps[0:1, 4, :], ones_f[:], acc[:], start=True, stop=True).then_inc(acc_ps, 1)

            pe.wait_ge(gated, GATED_ALL)
            for t in range(TT + 3):
                if t < TT:
                    for h in range(2):
                        q = 2 * t + h
                        if h == 0:
                            pe.wait_ge(m_ready, t + 1)
                        if q >= 4:
                            pe.wait_ge(x1_half, q - 3)
                        n = 0
                        for kc in range(KC):
                            if t == 0 and kc % 4 == 0:
                                pe.wait_ge(wo_ready, 2 * h + kc // 4 + 1)
                            for a, b in ((m_hi, wo_hi), (m_hi, wo_lo), (m_lo, wo_hi)):
                                n += 1
                                last = pe.matmul(ps[:, q % 4, :], a[t % 2][:, kc, :], b[h][:, kc, :], start=(n == 1), stop=(n == MM))
                        last.then_inc(mo_ps, 1)
                if t >= 3:
                    pe.wait_ge(u2T_ready, t - 2)
                    if t == 3:
                        pe.wait_ge(ld_rows, 16 * 6)
                    for kc in range(KC):
                        last = pe.matmul(ps[:, 6, (t - 3) * NE:(t - 2) * NE], u2T[:, kc, :], wr[:, kc, :], start=(kc == 0), stop=(kc == KC - 1))
                    last.then_inc(ro_ps, 1)
                if 2 <= t <= TT + 1:
                    pe.wait_ge(u2_ready, t - 1)
                    v = u2[:, t - 2, :].rearrange("p (q c) -> p c q", c=KC)
                    for kc in range(KC):
                        last = pe.transpose(ps[:, 4 + kc // 4, (kc % 4) * P:(kc % 4 + 1) * P], v[:, kc, :], ident[:])
                    last.then_inc(x2t_ps, 1)

            pe.wait_ge(hit_ready, 1)
            for t in range(TT):
                for t2 in range(t + 1):
                    pe.matmul(ps[:, 7, t * NE:(t + 1) * NE], (before_b if t2 == t else ones_b)[:], hit_b[:, t2, :], start=(t2 == 0), stop=(t2 == t))
            for t in range(TT):
                last = pe.matmul(ps[:, 7, TT * NE:(TT + 1) * NE], ones_b[:], hit_b[:, t, :], start=(t == 0), stop=(t == TT - 1))
            last.then_inc(rank_ps, 1)

            def rows_to_features(part):
                v = xg[:].rearrange("p (q c) -> p c q", c=KC)
                for kc in range(4 * part, 4 * part + 4):
                    last = pe.transpose(ps[:, kc // 4, (kc % 4) * P:(kc % 4 + 1) * P], v[:, kc, :], ident[:])
                if part:
                    last.then_inc(xg_ps, 1)

            def products(bank, w, e, x_hi, x_lo, cols, x_lo_wait=None):
                _, hi, lo, _ = WT[w]
                n = x_hi.shape[1]
                for kc in range(n):
                    if kc % (n // 2) == 0:
                        pe.wait_ge(lo_ready[w], e * 2 + (2 * kc // n + 1))
                    pe.matmul(ps[:, bank, :], x_hi[:, kc, :], hi[:, kc, cols], start=(kc == 0), stop=False)
                    pe.matmul(ps[:, bank, :], x_hi[:, kc, :], lo[:, kc, cols], start=False, stop=False)
                if x_lo_wait is not None:
                    pe.wait_ge(*x_lo_wait)
                for kc in range(n):
                    last = pe.matmul(ps[:, bank, :], x_lo[:, kc, :], hi[:, kc, cols], start=False, stop=(kc == n - 1))
                return last

            pe.wait_ge(starts_ready, 1)
            pe.wait_ge(ld_xg, 16)
            rows_to_features(0)
            rows_to_features(1)
            hv = act[:].rearrange("p (q c) -> p c q", c=FC)
            with pe.Fori(0, NE) as e:
                first = pe.value_load(starts[0:1, bass.ds(e, 1)], min_val=0, max_val=NBLK)
                end = pe.value_load(starts[0:1, bass.ds(e + 1, 1)], min_val=1, max_val=NBLK)
                with pe.Fori(first, end) as j:
                    pe.wait_ge(xgT_ready, j + 1)
                    products(2, "g", e, xgT_hi, xgT_lo, HF[0]).then_inc(g_ps, 1)
                    products(3, "u", e, xgT_hi, xgT_lo, HF[0]).then_inc(h_ps, 1)
                    pe.wait_ge(ld_xg, j * 16 + 32)
                    rows_to_features(0)
                    pe.wait_ge(h_ready, j + 1)
                    for fc in range(FC):
                        last = pe.transpose(ps[:, 4, fc * P:(fc + 1) * P], hv[:, fc, :], ident[:])
                    last.then_inc(ht_ps, 1)
                    rows_to_features(1)
                    pe.wait_ge(actT_hi_ready, j + 1)
                    pe.wait_ge(y_evac, j + 1)
                    products(5, "d", e, actT_hi, actT_lo, HF[0], (actT_ready, j + 1))
                    products(6, "d", e, actT_hi, actT_lo, HF[1]).then_inc(y_ps, 1)

        @block.scalar
        def _(sc):
            ch = Chain(sc, ch_act)
            for s_, n_ in ((p_ready, PRIME), (pt_ready, PRIME), (y_ready, PRIME), (y_evac, 1), (st_y, 16), (mrow_ready, 1), (st_mod, 16)):
                sc.sem_inc(s_, n_)
            sc.wait_ge(ld_const, 16 * 5)
            sc.activation(cact[:], cvec[:], ACT.Silu).then_inc(cact_ready, 1)
            def squares(t):
                sc.wait_ge(ld_x[t], 16)
                ch(sc.activation(junk[:], xn[:, t, :], ACT.Square, accum_out=ms[:, t:t + 1]))

            def roots(th):
                half = slice(4 * th, 4 * th + 4)
                sc.activation(rstd[:, half], ms[:, half], ACT.Copy).then_inc(ms_ready, 1)
                sc.wait_ge(ms_ready, 2 * th + 2)
                sc.activation(ms[:, half], rstd[:, half], ACT.Sqrt).then_inc(root_ready, 1)

            for t in range(TT // 2):
                squares(t)
            roots(0)
            for n in range(2 * KC):
                kc, th = n % KC, n // KC
                sc.wait_ge(xt_full, n + 1)
                sc.activation(u_hi[:, kc, HF[th]], u_full[n % 4][:], ACT.Copy).then_inc(u_hi_ready, 1)
                if n < 4:
                    squares(4 + n)
                if n == 3:
                    roots(1)
            sc.wait_ge(lam_in, 1)
            sc.activation(lam_t[:, 1], lam_t[:, 0], ACT.Exp, scale=-1.0).then_inc(lam_act, 1)
            sc.wait_ge(lam_in, 2)
            sc.activation(lam_t[:, 3], lam_t[:, 2], ACT.Ln).then_inc(lam_act, 1)

            def evac(k, h, dst, scale=1.0):
                sc.wait_ge(job_half, 2 * k + (h + 1))
                hold(sc)
                sc.activation(dst, ps[:, 5 + h, :], ACT.Copy, scale=scale).then_inc(job_evac, 1)

            for k in range(PRO):
                for h in range(2):
                    evac(k, h, (qT[:, 0, HF[h]], kT[:, 0, HF[h]], vT[:, HF[h]])[k], DH ** -0.5 if k == 0 else 1.0)

            def exps(r, u):
                sc.wait_ge(s_biased, done(u))
                sc.wait_ge(o_ready, done(u - 2))
                sc.activation(prob[r % 2][:], prob[r % 2][:], ACT.Exp, bias=nmax[:, r % 2:r % 2 + 1],
                              accum_out=rsum[:, r % 2:r % 2 + 1]).then_inc(p_ready, 1)

            exps(0, 0)

            def pair(hp, n):
                nxt = (hp + 1) % 2
                for r in range(ROWS):
                    u = hp * ROWS + r
                    sc.wait_ge(pt_ps, done(u))
                    sc.wait_ge(o_ps, done(u - 2))
                    sc.activation(probT[r % 2][:].rearrange("p a b -> p (a b)"), ps[:, 2 + 5 * (r % 2), :], ACT.Copy).then_inc(pt_ready, 1)
                    if r < ROWS - 1:
                        exps(r + 1, u + 1)
                    elif n == PER:
                        exps(0, u + 1)
                    for i in range(n):
                        for h in range(2):
                            if finish_unit(n, i, h) == r:
                                k = hp * PER + PRO + i
                                if n == PER and i < 3:
                                    dst = (qT[:, nxt, HF[h]], kT[:, nxt, HF[h]], vT[:, HF[h]])[i]
                                else:
                                    ii = i - 3 if n == PER else i
                                    dst = lx[:, ii, hp, HF[h]]
                                evac(k, h, dst, DH ** -0.5 if n == PER and i == 0 else 1.0)
                    sc.wait_ge(ot_ps, done(u))
                    hold(sc)
                    for side in range(2):
                        sl = slice(64 * side, 64 * side + 64)
                        dst = y_na[sl, hp, r * GRID_W:(r + 1) * GRID_W]
                        ins = sc.activation(dst, ps[sl, 4, BACK[side]], ACT.Copy)
                        if side:
                            ins.then_inc(y_ready, 1)

            with sc.Fori(0, PAIRS - 1) as hp:
                pair(hp, PER)
            pair(PAIRS - 1, LAST)

            sc.wait_ge(job_evac, 2 * GATE0)
            sc.activation(lx[:, 1], lx[:, 1], ACT.Gelu_apprx_tanh).then_inc(gelu_ready, 1)
            sc.wait_ge(decay_ready, 1)

            flat = lambda a: a.rearrange("p a b -> p (a b)")
            for cc in range(BC):
                for d in range(2):
                    n = 2 * cc + d
                    sc.wait_ge(lru_ps, n + 1)
                    if cc:
                        sc.wait_ge(*((lru_free, n - 1) if d == 0 else (lru_sum, cc)))
                    ch.mark(sc.activation(t_a[d][:], flat(ps[:, 0:2, :]), ACT.Tanh, scale=0.5, bias=lru_b[:, d, cc:cc + 1]))
                    sc.activation(t_b[d][:], flat(ps[:, 2:4, :]), ACT.Tanh, scale=0.5, bias=lru_b[:, 2 + d, cc:cc + 1]).then_inc(lru_read, 1)
                    if d == 0:
                        sc.wait_ge(z_ps, cc + 1)
                        sc.activation(flat(z_first[:]), flat(ps[:, 4:6, :]), ACT.Copy).then_inc(z_copied, 1)
                    ch.sync()
                    dec, dec2 = decay[:, d, cc:cc + 1], decay2[:, d, cc:cc + 1]
                    ch.mark(sc.activation(t_c[d][:], t_a[d][:], ACT.Exp, scale=dec, bias=dec))
                    if n:
                        sc.wait_ge(lru_rad, n)
                    ch(sc.activation(t_d[:], t_a[d][:], ACT.Exp, scale=dec2, bias=dec2))
                    sc.activation(t_a[d][:], t_a[d][:], ACT.Tanh, scale=dec, bias=dec).then_inc(lru_act, 1)
                sc.wait_ge(f_ps, cc + 1)
                if cc:
                    sc.wait_ge(f_done, cc)
                sc.activation(sin_part[:], ps[:, 5, :], ACT.Copy).then_inc(f_sin, 1)
                for d in range(2):
                    sc.wait_ge(lru_rad, 2 * cc + d + 1)
                    sc.activation(t_a[d][:], t_a[d][:], ACT.Sqrt, scale=-1.0).then_inc(lru_root, 1)

            sc.wait_ge(lru_done, 4)
            sc.wait_ge(f_done, 4)
            sc.wait_ge(st_pad, 16)
            for b in range(3):
                if b:
                    sc.wait_ge(gated, 2 * KC * b + GATED_PRIME)
                for i in range(2 * BC):
                    kc, h = i // 2, i % 2
                    if i >= 2:
                        sc.wait_ge(br_ready, 2 * BC * b + i - 1)
                    sc.activation(br_tmp[h][:], (y_na, lx[:, 2], lx[:, 1])[b][:, kc, HF[h]], ACT.Copy).then_inc(br_tmp_ready, 1)
                sc.wait_ge(br_ready, 2 * BC * (b + 1))
                with sc.Fori(0, KC // 2) as two:
                    blk = two + b * (KC // 2)
                    for s in range(2):
                        dc = two * 2 + s
                        it = dc + b * KC
                        for h in range(2):
                            if b < 2:
                                kc = 4 * s + 2 * h
                                sc.wait_ge(ada_done, blk * 4 + (2 * s + h + 1))
                                hold(sc)
                                sc.dma_start(ada_g[:], ada_v[:, kc:kc + 2, bass.ds(blk * HALF + 2 * D, HALF)]).then_inc(ld_mod, 16)
                            sc.wait_ge(job_half, 2 * (it + GATE0) + (h + 1))
                            sc.wait_ge(gated, 2 * it + (h + GATED_PRIME - 1))
                            hold(sc)
                            sc.activation(gate[h][:], ps[:, 5 + h, :], ACT.Sigmoid,
                                          bias=bg[:, bass.ds(dc + BRANCH[b] // P, 1)]).then_inc(job_evac, 1)
                    if b < 2:
                        sc.wait_ge(acc_ps, blk + 2)
                        sc.wait_ge(st_mod, blk * 16 + 16)
                        hold(sc)
                        sc.activation(mrow[:], ps[0:1, 4, :], ACT.Copy).then_inc(mrow_ready, 1)
                        sc.wait_ge(mrow_ready, blk + 2)
                        sc.dma_start(d_mod.rearrange("v n -> (v n)").unsqueeze(0)[:, bass.ds(blk * HALF, HALF)], mrow[:]).then_inc(st_mod, 16)

            def merged_hi(t):
                if t >= 2:
                    sc.wait_ge(mo_ps, 2 * t - 2)
                sc.activation(m_hi[t % 2][:], merged[:, :, t * P:(t + 1) * P], ACT.Copy).then_inc(m_hi_ready, 1)

            sc.wait_ge(gated, GATED_ALL)
            merged_hi(0)
            for i in range(4):
                h, q = i // 2, i % 2
                sc.wait_ge(ld_wo[h], 16)
                sc.activation(half_of(wo_hi[h], q), half_of(wo[h], q), ACT.Copy).then_inc(wo_hi_ready, 1)
            merged_hi(1)

            for t in range(TT):
                if t + 2 < TT:
                    merged_hi(t + 2)
                sc.wait_ge(x1_half, 2 * t + 2)
                sc.activation(u2[:, t, :], x1[:, t, :], ACT.Square, accum_out=ms2[:, t:t + 1]).then_inc(ms2_ready, 1)
                sc.wait_ge(root2, 2 * t + 1)
                sc.activation(ms2[:, t:t + 1], rstd2[:, t:t + 1], ACT.Sqrt).then_inc(root2, 1)
            sc.wait_ge(ro_ps, TT)
            sc.activation(dd["score"][:].rearrange("p a b -> p (a b)"), ps[:, 6, 0:TT * NE], ACT.Sigmoid).then_inc(score_ready, 1)

            sc.wait_ge(st_u2, 16 * TT)
            for w in "gud":
                sc.wait_ge(ld_raw[w], 16)
                for half in range(2):
                    split_hi(w, half)

            def gate_half(j):
                sc.wait_ge(g_ps, j + 1)
                sc.activation(act[:], ps[:, 2, :], ACT.Silu).then_inc(silu_ready, 1)

            def transposed(j):
                sc.wait_ge(ht_ps, j + 1)
                sc.activation(actT_hi[:].rearrange("p a b -> p (a b)"), ps[:, 4, :], ACT.Copy).then_inc(actT_hi_ready, 1)
                next_rows(j + 1)

            def next_rows(j):
                sc.wait_ge(xg_ps, j + 1)
                sc.activation(xgT_hi[:].rearrange("p a b -> p (a b)"), ps[:, 0:2, :].rearrange("p a b -> p (a b)"), ACT.Copy).then_inc(xgT_hi_ready, 1)

            def output(j):
                sc.wait_ge(y_ps, j + 1)
                sc.wait_ge(st_y, j * 16 + 16)
                sc.activation(yb[:], ps[:, 5:7, :].rearrange("p a b -> p (a b)"), ACT.Copy).then_inc(y_evac, 1)
                sc.wait_ge(y_evac, j + 2)
                hold(sc)
                sc.dma_start(d_y[bass.ds(j * CAP, CAP), :], yb[:]).then_inc(st_y, 16)

            def next_hi(w, e, used, end):
                sc.wait_ge(used, end)
                sc.wait_ge(ld_raw[w], e * 16 + 32)
                hold(sc)
                for half in range(2):
                    split_hi(w, half)

            def expert_blocks(e):
                first = sc.value_load(starts[0:1, bass.ds(e, 1)], min_val=0, max_val=NBLK)
                end = sc.value_load(starts[0:1, bass.ds(e + 1, 1)], min_val=1, max_val=NBLK)
                with sc.If(first + 1 < end):
                    with sc.Fori(first, end - 1) as j:
                        gate_half(j)
                        transposed(j)
                        output(j)
                return end

            sc.wait_ge(st_pad, 16)
            sc.wait_ge(starts_ready, 1)
            next_rows(0)
            with sc.Fori(0, NE - 1) as e:
                end = expert_blocks(e)
                gate_half(end - 1)
                next_hi("g", e, g_ps, end)
                transposed(end - 1)
                next_hi("u", e, h_ps, end)
                output(end - 1)
                next_hi("d", e, y_ps, end)
            end = expert_blocks(NE - 1)
            gate_half(end - 1)
            transposed(end - 1)
            output(end - 1)

            for t in range(TT + 1):
                if t < TT:
                    y = y0[t % YBUF]
                    sc.wait_ge(ld_y[t % YBUF], 32 * (t // YBUF + 1))
                    sc.activation(y[:], y[:], ACT.Copy, scale=pair_w[:, 0, t:t + 1]).then_inc(y_scaled, 1)
                if t:
                    m = t - 1
                    sc.wait_ge(fin_ready_x, m + 1)
                    sc.activation(junk2[:], x1[:, m, :], ACT.Square, accum_out=ms2[:, m:m + 1]).then_inc(fin_ms, 1)
                    sc.wait_ge(fin_root, 2 * m + 1)
                    sc.activation(ms2[:, m:m + 1], rstd2[:, m:m + 1], ACT.Sqrt).then_inc(fin_root, 1)

        @block.vector
        def _(dve):
            ch = Chain(dve, ch_dve)
            for s_, n_ in ((s_biased, PRIME), (o_ready, PRIME), (gated, GATED_PRIME), (q_staged, PRIME), (ada_done, 1)):
                dve.sem_inc(s_, n_)
            dve.wait_ge(cact_ready, 1)
            dve.tensor_copy(crep[:], cact[:].unsqueeze(2).to_broadcast([P, KC, P])).then_inc(crep_ready, 1)
            def normalise(th):
                half = slice(4 * th, 4 * th + 4)
                dve.wait_ge(ms_ready, 2 * th + 1)
                dve.tensor_scalar(rstd[:, half], rstd[:, half], 1.0 / D, EPS, MUL, ADD).then_inc(ms_ready, 1)
                dve.wait_ge(root_ready, th + 1)
                ch(dve.reciprocal(rstd[:, half], ms[:, half]))
                for t in range(4 * th, 4 * th + 4):
                    dve.tensor_scalar(xn[:, t, :], xn[:, t, :], rstd[:, t:t + 1], None, MUL).then_inc(xn_ready, 1)

            def mod_vector(v):
                dve.wait_ge(ada_used, 2 * v + 2)
                row = ps[:, 2 * (v % 2):2 * (v % 2) + 2, :].rearrange("p a b -> p (a b)")
                v3 = lambda a: a.rearrange("p (q c) -> p q c", c=KC)
                dve.tensor_tensor(v3(modtmp[:]), v3(row), ident[:].unsqueeze(2).to_broadcast([P, P, KC]), MUL).then_inc(mod_read, 1)
                dve.wait_ge(mod_read, v + 1)
                ch(dve.tensor_reduce(modv[:, v, :], modtmp[:].rearrange("p (q c) -> p c q", c=KC), AX.X, ADD))
                ch(dve.tensor_tensor(modv[:, v, :], modv[:, v, :], mod_b[:, v, :], ADD))
                if v == 1:
                    ch(dve.scalar_tensor_tensor(u_scale[:], modv[:, v, :], 1.0, norm_g[:], ADD, MUL))

            dve.wait_ge(ld_const, 16 * 5)
            mod_vector(0)
            mod_vector(1)
            normalise(0)
            for n in range(2 * KC + 1):
                if n < 2 * KC:
                    kc = n % KC
                    dve.wait_ge(xt_ps, n + 1)
                    if n >= 4:
                        dve.wait_ge((u_lo_even, u_lo_odd)[n % 2], n // 2 - 1)
                    dve.tensor_scalar(u_full[n % 4][:], ps[:, XBANK[n % 4], :], u_scale[:, kc:kc + 1], modv[:, 0, kc:kc + 1], MUL, ADD).then_inc(xt_full, 1)
                if n == 4:
                    normalise(1)
                if n % 2:
                    m = n - 1
                    dst = slice(m // KC * HALF, (m // KC + 1) * HALF)
                    dve.wait_ge(u_hi_ready, m + 1)
                    dve.tensor_tensor(u_lo[:, m % KC, dst], u_full[m % 4][:], u_hi[:, m % KC, dst].bitcast(f32), SUB).then_inc(u_lo_even, 1)

            dve.wait_ge(ld_small, 16 * 12)
            ch(dve.tensor_scalar(decay[:], lam[:], -1.0, None, MUL))
            dve.tensor_tensor(lam_t[:, 0], decay[:], lam[:], ALU.max).then_inc(lam_in, 1)
            dve.wait_ge(lam_act, 1)
            dve.tensor_scalar(lam_t[:, 2], lam_t[:, 1], 1.0, None, ADD).then_inc(lam_in, 1)
            dve.wait_ge(lam_act, 2)
            dve.wait_ge(lam_in, 2)
            ch(dve.tensor_scalar(lam_t[:, 2], lam_t[:, 2], 1.0, None, SUB))
            ch(dve.tensor_scalar(lam_t[:, 0], lam_t[:, 2], 0.0, None, ALU.is_equal))
            ch(dve.tensor_tensor(lam_t[:, 2], lam_t[:, 2], lam_t[:, 0], ADD))
            ch(dve.reciprocal(lam_t[:, 2], lam_t[:, 2]))
            ch(dve.tensor_tensor(lam_t[:, 3], lam_t[:, 3], lam_t[:, 2], MUL))
            ch(dve.tensor_tensor(lam_t[:, 3], lam_t[:, 3], lam_t[:, 0], ADD))
            ch(dve.tensor_tensor(lam_t[:, 3], lam_t[:, 3], lam_t[:, 1], MUL))
            ch(dve.scalar_tensor_tensor(decay[:], decay[:], 0.0, lam_t[:, 3], ALU.max, ADD))
            ch.mark(dve.tensor_scalar(lru_b[:], lru_b[:], 0.5, None, MUL))
            ch(dve.tensor_scalar(decay2[:], decay[:], -8.0, None, MUL))
            ch.mark(dve.memset(ones_f[:], 1.0))
            dve.tensor_scalar(decay[:], decay[:], -4.0, None, MUL).then_inc(decay_ready, 1)

            def v_tiles(g, par):
                n = min(4, 15 - 4 * g)
                dst = vtok[:, par, 4 * g:4 * g + n, :]
                dve.tensor_copy(dst, ps[:, 1, 0:n * P].rearrange("p (a b) -> p a b", b=P)).then_inc(vt_evac, 1)

            def stage_q(r, par):
                for side in range(2):
                    sl = slice(64 * side, 64 * side + 64)
                    ins = dve.tensor_copy(q_bd[r % 2][sl, BACK[side]], qT[sl, par, r * GRID_W:(r + 1) * GRID_W])
                    if side:
                        ins.then_inc(q_staged, 1)

            ch.mark(dve.memset(q_bd[0][:], 0.0))
            ch.mark(dve.memset(q_bd[1][:], 0.0))
            ch.mark(dve.memset(o_bd[0][:], 0.0))
            ch.mark(dve.memset(o_bd[1][:], 0.0))
            for g in range(4):
                dve.wait_ge(vt_ps, g + 1)
                v_tiles(g, 0)
            ch.sync()
            dve.wait_ge(job_evac, 2)
            stage_q(0, 0)
            stage_q(1, 0)
            dve.wait_ge(bias_ready, 1)

            def biased(r, u, par):
                dve.wait_ge(s_ps, done(u))
                dve.wait_ge(pt_ps, done(u - 2))
                d0 = (band(r) - r + WIN_R - 1) * GRID_W
                ch(dve.tensor_tensor(prob[r % 2][:], ps[:, 0, :], bias[:, par, d0:d0 + HALF], ADD))
                dve.tensor_reduce(nmax[:, r % 2:r % 2 + 1], prob[r % 2][:], AX.X, ALU.max, negate=True).then_inc(s_biased, 1)

            biased(0, 0, 0)

            def pair(hp, n):
                par = hp % 2
                nxt = (hp + 1) % 2
                for r in range(ROWS):
                    u = hp * ROWS + r
                    if r < ROWS - 1:
                        biased(r + 1, u + 1, par)
                    elif n == PER:
                        dve.wait_ge(bias_ready, hp + 2)
                        biased(0, u + 1, nxt)
                    if r < ROWS - 2:
                        stage_q(r + 2, par)
                    elif n == PER:
                        if r == ROWS - 2:
                            dve.wait_ge(job_evac, hp * (2 * PER) + 2 * PRO + 2)
                        stage_q(r + 2 - ROWS, nxt)
                    dve.wait_ge(o_ps, done(u))
                    dve.wait_ge(p_ready, done(u))
                    ch(dve.reciprocal(rinv[:, r % 2:r % 2 + 1], rsum[:, r % 2:r % 2 + 1]))
                    dve.wait_ge(ot_ps, done(u - 2))
                    for side in range(2):
                        sl = slice(64 * side, 64 * side + 64)
                        ins = dve.tensor_scalar(o_bd[r % 2][sl, sl], ps[sl, 3, sl], rinv[sl, r % 2:r % 2 + 1], None, MUL)
                        if side:
                            ins.then_inc(o_ready, 1)
                    if n == PER and VT0 <= r < VT0 + 4:
                        g = r - VT0
                        dve.wait_ge(vt_ps, hp * 4 + (g + 5))
                        v_tiles(g, nxt)

            with dve.Fori(0, PAIRS - 1) as hp:
                ch.enter(hp, 2 * ROWS)
                pair(hp, PER)
                ch.leave(PAIRS - 1)
            pair(PAIRS - 1, LAST)

            dve.wait_ge(y_ready, ATT_ALL)
            dve.wait_ge(job_evac, 2 * GATE0)

            def conv(cc):
                xr, o = lx[:, 0, cc, :], xc[cc % 2]
                if cc > 1:
                    dve.wait_ge(lru_ps, 2 * cc - 2)
                ch(dve.tensor_scalar(o[:], xr, conv_w[:, 2, cc:cc + 1], conv_b[:, cc:cc + 1], MUL, ADD))
                ch(dve.scalar_tensor_tensor(o[:, 2:], xr[:, :T - 2], conv_w[:, 0, cc:cc + 1], o[:, 2:], MUL, ADD))
                ch(dve.scalar_tensor_tensor(o[:, 1:], xr[:, :T - 1], conv_w[:, 1, cc:cc + 1], o[:, 1:], MUL, ADD))
                dve.scalar_tensor_tensor(o[:, :T - 1], xr[:, 1:], conv_w[:, 3, cc:cc + 1], o[:, :T - 1], MUL, ADD).then_inc(xc_ready, 1)
                dve.wait_ge(xc_ready, cc + 1)

            conv(0)
            conv(1)
            for cc in range(BC):
                xr = lx[:, 0, cc, :]
                dve.wait_ge(z_copied, cc + 1)
                second = ps[:, 6:8, :].rearrange("p a b -> p (a b)")
                first = z_first[:].rearrange("p a b -> p (a b)")
                ch.mark(dve.tensor_tensor(z[:, 0].rearrange("p a b -> p (a b)"), first, second, ADD))
                dve.tensor_tensor(z[:, 1].rearrange("p a b -> p (a b)"), first, second, SUB).then_inc(z_ready, 1)
                for d in range(2):
                    dve.wait_ge(lru_act, 2 * cc + d + 1)
                    dve.scalar_tensor_tensor(t_a[d][:], t_d[:], 1.0, t_a[d][:], ADD, MUL).then_inc(lru_rad, 1)
                    ch.mark(dve.scalar_tensor_tensor(t_b[d][:], t_b[d][:], 1.0, xc[cc % 2][:], ADD, MUL))
                ch.sync()
                g = cc
                fy = lx[:, 2, g, :]
                dve.wait_ge(f_sin, g + 1)
                cos2, sin2 = ps[:, 4, :].rearrange("p (e m) -> p e m", e=2), sin_part[:].rearrange("p (e m) -> p e m", e=2)
                ch.mark(dve.tensor_tensor(fy[:, 0:HALF].rearrange("p (m e) -> p e m", e=2), cos2, sin2, SUB))
                ch.mark(dve.tensor_tensor(fy[:, T - 2:HALF:-2], cos2[:, 0, 1:], sin2[:, 0, 1:], ADD))
                ch.mark(dve.tensor_tensor(fy[:, T - 1:HALF:-2], cos2[:, 1, :], sin2[:, 1, :], ADD))
                dve.tensor_copy(fy[:, HALF:HALF + 1], ps[:, 6, 0:1]).then_inc(f_done, 1)
                for d in range(2):
                    dve.wait_ge(lru_root, 2 * cc + d + 1)
                    ch(dve.scalar_tensor_tensor(t_a[d][:], t_a[d][:], 0.5, t_b[d][:], MUL, MUL))
                    if d == 0:
                        dve.tensor_tensor_scan(xr, t_c[0][:], t_a[0][:], 0.0, MUL, ADD).then_inc(lru_free, 1)
                    else:
                        dve.tensor_tensor_scan(t_b[1][:, ::-1], t_c[1][:, ::-1], t_a[1][:, ::-1], 0.0, MUL, ADD).then_inc(lru_free, 1)
                if cc + 2 < BC:
                    conv(cc + 2)

            xr, yr = lx[:, 0, BC - 1, :], lx[:, 1, BC - 1, :]
            dve.wait_ge(lru_free, 2 * BC)
            dve.wait_ge(lru_sum, BC - 1)
            dve.tensor_tensor(xr, xr, t_b[1][:], ADD).then_inc(lru_sum, 1)
            dve.wait_ge(lru_sum, BC)
            dve.wait_ge(lru_done, BC - 1)
            dve.tensor_tensor(yr, xr, yr, MUL).then_inc(lru_done, 1)

            for b in range(3):
                if b:
                    dve.wait_ge(pr_ps, 2 * KC * b + PR_PRIME)
                else:
                    dve.wait_ge(lru_done, 4)
                for i in range(2 * BC):
                    kc, h = i // 2, i % 2
                    full = (y_na, lx[:, 2], lx[:, 1])[b][:, kc, HF[h]]
                    dve.wait_ge(br_tmp_ready, 2 * BC * b + i + 1)
                    ch(dve.tensor_tensor(br_lo[:, kc, HF[h]], full, br_tmp[h][:].bitcast(f32), SUB))
                    dve.tensor_copy(br_hi[b][:, kc, HF[h]], br_tmp[h][:]).then_inc(br_ready, 1)
                with dve.Fori(0, KC // 2) as two:
                    blk = two + b * (KC // 2)
                    ch.enter(two, (4, 8, 4)[b])
                    for s in range(2):
                        dc = two * 2 + s
                        it = dc + b * KC
                        if b < 2:
                            for h in range(2):
                                kc, p = 4 * s + 2 * h, 2 * s + h
                                dve.wait_ge(ld_mod, blk * 64 + 16 * (p + 1))
                                if p == 0:
                                    dve.wait_ge(acc_ps, blk + 1)
                                    hold(dve)
                                    ch(dve.tensor_scalar(acc[:], ada_g[:, 0, :], cact[:, 0:1], None, MUL))
                                else:
                                    hold(dve)
                                    ch(dve.scalar_tensor_tensor(acc[:], ada_g[:, 0, :], cact[:, kc:kc + 1], acc[:], MUL, ADD))
                                dve.scalar_tensor_tensor(acc[:], ada_g[:, 1, :], cact[:, kc + 1:kc + 2], acc[:], MUL, ADD).then_inc(ada_done, 1)
                                dve.wait_ge(ada_done, blk * 4 + (p + 2))
                        for h in range(2):
                            dve.wait_ge(job_evac, 2 * (it + GATE0) + (h + 1))
                            dve.wait_ge(pr_ps, 2 * it + (h + 1 + PR_PRIME))
                            dst = merged[:, bass.ds(dc, 1), HF[h]].rearrange("p a n -> p (a n)")
                            proj = ps[:, 2 * s + h, :]
                            hold(dve)
                            if b == 0:
                                dve.tensor_tensor(dst, gate[h][:], proj, MUL).then_inc(gated, 1)
                            else:
                                ch(dve.tensor_tensor(part[:], gate[h][:], proj, MUL))
                                dve.wait_ge(gated, 2 * it + (h + GATED_PRIME))
                                dve.tensor_tensor(dst, dst, part[:], ADD).then_inc(gated, 1)
                                dve.wait_ge(gated, 2 * it + (h + GATED_PRIME + 1))
                    ch.leave(KC // 2)

            for i in range(4):
                h, q = i // 2, i % 2
                dve.wait_ge(wo_hi_ready, i + 1)
                dve.tensor_tensor(half_of(wo_lo[h], q), half_of(wo[h], q), half_of(wo_hi[h], q).bitcast(f32), SUB).then_inc(wo_ready, 1)

            dve.wait_ge(ld_gmix, 32)
            ch(dve.tensor_tensor(gmix[:], gmix[:], gmix_b[:], ADD))
            dve.wait_ge(ld_rows, 16 * 6)
            ch.mark(dve.tensor_tensor(sh_row[:], sh_row[:], sh_b[:], ADD))
            ch(dve.tensor_tensor(sc_row[:], sc_row[:], sc_b[:], ADD))
            ch(dve.scalar_tensor_tensor(sc_row[:], sc_row[:], 1.0, g_row[:], ADD, MUL))
            for t in range(TT + 2):
                if t < TT:
                    dve.wait_ge(ld_x[t], 32)
                    for h in range(2):
                        dve.wait_ge(mo_ps, 2 * t + h + 1)
                        ch(dve.tensor_tensor(mixed[:], ps[:, (2 * t + h) % 4, :], gmix[:, HF[h]], MUL))
                        dve.tensor_tensor(x1[:, t, HF[h]], x1[:, t, HF[h]], mixed[:], ADD).then_inc(x1_half, 1)
                        dve.wait_ge(x1_half, 2 * t + h + 1)
                if 1 <= t <= TT:
                    m = t - 1
                    dve.wait_ge(ms2_ready, m + 1)
                    dve.tensor_scalar(rstd2[:, m:m + 1], ms2[:, m:m + 1], 1.0 / D, EPS, MUL, ADD).then_inc(root2, 1)
                    dve.wait_ge(root2, 2 * m + 2)
                    ch(dve.reciprocal(rstd2[:, m:m + 1], ms2[:, m:m + 1]))
                    ch(dve.scalar_tensor_tensor(u2[:, m, :], x1[:, m, :], rstd2[:, m:m + 1], sc_row[:], MUL, MUL))
                    dve.tensor_tensor(u2[:, m, :], u2[:, m, :], sh_row[:], ADD).then_inc(u2_ready, 1)
                if t >= 2:
                    dve.wait_ge(x2t_ps, t - 1)
                    dve.tensor_copy(u2T[:].rearrange("p a b -> p (a b)"), ps[:, 4:6, :].rearrange("p a b -> p (a b)")).then_inc(u2T_ready, 1)

            t3 = lambda n: dd[n][:]
            g4 = lambda a: a.rearrange("p t (g e) -> p (t g) e", e=EPG)
            dve.wait_ge(mo_ps, 2 * TT)
            ch.mark(dve.memset(ones_b[:], 1.0))
            for g in range(NG):
                ch.mark(dve.memset(gidx[:, g:g + 1], float(g - NG)))
            dve.wait_ge(ld_rt, 32)
            ch(dve.tensor_copy(before_b[:], before[:]))
            dve.wait_ge(score_ready, 1)
            ch(dve.tensor_tensor(t3("sel"), t3("score"), rbias[:].unsqueeze(1).to_broadcast([P, TT, NE]), ADD))
            pt = [pairt[:, i].rearrange("p t g -> p (t g)") for i in range(8)]
            se = [g4(t3("sel"))[:, :, e] for e in range(EPG)]
            tt = lambda o, a, b, op: ch(dve.tensor_tensor(o, a, b, op))
            tt(pt[0], se[0], se[1], ALU.max)
            tt(pt[1], se[0], se[1], ALU.min)
            tt(pt[2], se[2], se[3], ALU.max)
            tt(pt[3], se[2], se[3], ALU.min)
            tt(pt[4], pt[0], pt[2], ALU.max)
            tt(pt[5], pt[0], pt[2], ALU.min)
            tt(pt[1], pt[1], pt[3], ALU.max)
            tt(pt[5], pt[5], pt[1], ALU.max)
            tt(pt[4], pt[4], pt[5], ADD)
            gs = pairt[:, 4]
            top = slot_f[:, 0, :]
            bc8 = lambda a: a.unsqueeze(2).to_broadcast([P, TT, NG])
            gi = gidx[:].unsqueeze(1).to_broadcast([P, TT, NG])
            ch(dve.tensor_reduce(top, gs, AX.X, ALU.max))
            tt(pairt[:, 6], gs, bc8(top), ALU.is_equal)
            tt(pairt[:, 6], pairt[:, 6], gi, MUL)
            ch(dve.tensor_reduce(top, pairt[:, 6], AX.X, ALU.min))
            tt(pairt[:, 7], gi, bc8(top), ALU.is_equal)
            rk = g4(t3("ta"))
            for e in range(EPG):
                ch(dve.memset(rk[:, :, e], float(EPG - 1 - e)))
            for a in range(EPG):
                for b in range(a + 1, EPG):
                    tt(pt[0], se[a], se[b], ALU.is_ge)
                    tt(rk[:, :, b], rk[:, :, b], pt[0], ADD)
                    tt(rk[:, :, a], rk[:, :, a], pt[0], SUB)
            ch(dve.scalar_tensor_tensor(g4(t3("hit")), rk, 1.5, pt[7].unsqueeze(2).to_broadcast([P, TT * NG, EPG]), ALU.is_lt, MUL))
            dve.tensor_copy(hit_b[:], t3("hit")).then_inc(hit_ready, 1)
            bc32 = lambda a: a.unsqueeze(2).to_broadcast([P, TT, NE])
            tt(t3("wgt"), t3("score"), t3("hit"), MUL)
            ch(dve.tensor_reduce(top, t3("wgt"), AX.X, ADD))
            ch(dve.reciprocal(top, top))
            tt(t3("wgt"), t3("wgt"), bc32(top), MUL)
            dve.wait_ge(rank_ps, 1)
            ch(dve.tensor_copy(cnt[:, 0, 0:NE], ps[:, 7, TT * NE:(TT + 1) * NE]))
            ch.mark(dve.memset(cnt[:, 1, :], 1.0))
            ch.mark(dve.memset(cnt[:, 3, :], 1.0))
            ch(dve.memset(cnt[:, 2, :], 0.0))
            for b in range(1, T // CAP):
                ch(dve.scalar_tensor_tensor(cnt[:, 1, 0:NE], cnt[:, 0, 0:NE], float(CAP * b), cnt[:, 1, 0:NE], ALU.is_gt, ADD))
            ch(dve.tensor_tensor_scan(cnt[:, 2, 1:NE + 1], cnt[:, 3, 0:NE], cnt[:, 1, 0:NE], 0.0, MUL, ADD))
            dve.tensor_copy(starts[:], cnt[0:1, 2, :]).then_inc(starts_ready, 1)
            ch(dve.tensor_scalar(cnt[:, 3, 0:NE], cnt[:, 2, 0:NE], float(CAP), 1.0, MUL, ADD))
            tt(t3("slot"), ps[:, 7, 0:TT * NE].rearrange("p (t e) -> p t e", e=NE), cnt[:, 3, 0:NE].unsqueeze(1).to_broadcast([P, TT, NE]), ADD)
            tt(t3("slot"), t3("slot"), t3("hit"), MUL)
            for k in range(2):
                top = slot_f[:, k, :]
                ch(dve.tensor_reduce(top, t3("slot"), AX.X, ALU.max))
                tt(t3("ta"), t3("slot"), bc32(top), ALU.is_equal)
                tt(t3("tb"), t3("ta"), t3("wgt"), MUL)
                ch(dve.tensor_reduce(pair_w[:, k, :], t3("tb"), AX.X, ADD))
                if k == 0:
                    tt(t3("ta"), t3("ta"), t3("slot"), MUL)
                    tt(t3("slot"), t3("slot"), t3("ta"), SUB)
            ch(dve.tensor_scalar(slot_f[:], slot_f[:], 1.0, None, SUB))
            ch(dve.tensor_copy(pair_s[:], slot_f[:]))
            ch(dve.tensor_single_scalar(slot_u[:], pair_s[:], CAP - 1, ALU.bitwise_and))
            ch(dve.tensor_single_scalar(slot_t[:], pair_s[:], 7, ALU.arith_shift_right))
            dve.scalar_tensor_tensor(slot_t[:], slot_u[:], float(LIST), slot_t[:], MUL, ADD).then_inc(slots_ready, 1)

            for w in "ud":
                for half in range(2):
                    dve.wait_ge(hi_ready[w], half + 1)
                    split_lo(dve, w, half)

            def hidden(j):
                dve.wait_ge(silu_ready, j + 1)
                dve.wait_ge(h_ps, j + 1)
                dve.tensor_tensor(act[:], act[:], ps[:, 3, :], MUL).then_inc(h_ready, 1)

            def hidden_rest(j):
                dve.wait_ge(actT_hi_ready, j + 1)
                dve.tensor_tensor(actT_lo[:].rearrange("p a b -> p (a b)"), ps[:, 4, :], actT_hi[:].rearrange("p a b -> p (a b)").bitcast(f32), SUB).then_inc(actT_ready, 1)

            def next_rows(j):
                dve.wait_ge(xgT_hi_ready, j + 1)
                dve.tensor_tensor(xgT_lo[:].rearrange("p a b -> p (a b)"), ps[:, 0:2, :].rearrange("p a b -> p (a b)"),
                                  xgT_hi[:].rearrange("p a b -> p (a b)").bitcast(f32), SUB).then_inc(xgT_ready, 1)

            def next_lo(w, e, half):
                dve.wait_ge(hi_ready[w], e * 2 + (half + 3))
                hold(dve)
                split_lo(dve, w, half)

            def expert_blocks(e):
                first = dve.value_load(starts[0:1, bass.ds(e, 1)], min_val=0, max_val=NBLK)
                end = dve.value_load(starts[0:1, bass.ds(e + 1, 1)], min_val=1, max_val=NBLK)
                with dve.If(first + 1 < end):
                    with dve.Fori(first, end - 1) as j:
                        hidden(j)
                        hidden_rest(j)
                        next_rows(j + 1)
                return end

            dve.wait_ge(starts_ready, 1)
            next_rows(0)
            with dve.Fori(0, NE - 1) as e:
                end = expert_blocks(e)
                hidden(end - 1)
                next_lo("g", e, 0)
                hidden_rest(end - 1)
                next_lo("g", e, 1)
                next_rows(end)
                for w in "ud":
                    next_lo(w, e, 0)
                    next_lo(w, e, 1)
            end = expert_blocks(NE - 1)
            hidden(end - 1)
            hidden_rest(end - 1)
            next_rows(end)

            dve.wait_ge(ld_end, 16 * 3)
            ch(dve.tensor_tensor(gffn[:], gffn[:], gffn_b[:], ADD))
            for t in range(TT + 1):
                if t < TT:
                    y = y0[t % YBUF][:]
                    dve.wait_ge(y_scaled, t + 1)
                    ch(dve.scalar_tensor_tensor(y, y1[t % YBUF][:], pair_w[:, 1, t:t + 1], y, MUL, ADD))
                    ch(dve.tensor_tensor(y, y, gffn[:], MUL))
                    dve.tensor_tensor(x1[:, t, :], x1[:, t, :], y, ADD).then_inc(fin_ready_x, 1)
                if t:
                    m = t - 1
                    dve.wait_ge(fin_ms, m + 1)
                    dve.tensor_scalar(rstd2[:, m:m + 1], ms2[:, m:m + 1], 1.0 / D, EPS, MUL, ADD).then_inc(fin_root, 1)
                    dve.wait_ge(fin_root, 2 * m + 2)
                    ch(dve.reciprocal(rstd2[:, m:m + 1], ms2[:, m:m + 1]))
                    if m >= 2:
                        dve.wait_ge(st_out[m % 2], 16 * (m // 2))
                    dve.scalar_tensor_tensor(res[m % 2][:], x1[:, m, :], rstd2[:, m:m + 1], fing[:], MUL, MUL).then_inc(fin_ready, 1)


_INS = ["x", "c", "ada_w", "ada_b", "norm_mix_g", "norm_ffn_g", "w_in", "w_branch_gate", "b_branch_gate",
        "na_rpb", "lru_conv_w", "lru_conv_b", "lru_w_r", "lru_b_r", "lru_w_i", "lru_b_i", "lru_lambda",
        "w_proj_na", "w_proj_lru", "w_proj_fnet", "w_out", "w_router", "router_bias",
        "w_exp_gate", "w_exp_up", "w_exp_down", "final_g"]


def constants():
    w, cc = np.arange(GRID_W)[:, None], np.arange(GRID_W)[None, :]
    start = np.clip(w - WIN_C // 2, 0, GRID_W - WIN_C)
    window = np.where((cc >= start) & (cc < start + WIN_C), 0.0, NEG)
    j = np.arange(P)
    chan = 2 * np.pi * (np.outer(j, j) % P) / P
    t, k = np.arange(T // 2), np.concatenate([np.arange(0, HALF, 2), np.arange(1, HALF, 2)])
    pos = 2 * np.pi * (np.outer(t, k) % T) / T
    f = lambda a: np.ascontiguousarray(a, dtype=np.float32)
    return {
        "k_ident": f(np.eye(P)),
        "k_window": f(np.concatenate([window[::-1], window[::-1]])),
        "k_before": f(np.triu(np.ones((P, P)), 1)),
        "k_chan": f(np.concatenate([np.cos(chan), np.sin(chan)], 1) / np.sqrt(P)),
        "k_cos": f(np.cos(pos) / np.sqrt(T)),
        "k_sin": f(np.sin(pos) / np.sqrt(T)),
        "k_nyq": f(np.broadcast_to(((-1.0) ** j)[:, None] / np.sqrt(T), (P, TT // 2))),
    }


def kernel(**inputs):
    import numpy as _np
    import concourse.bacc as _bacc
    from concourse import mybir as _mybir
    from concourse.bass_utils import run_bass_kernel_spmd as _run

    nc = _bacc.Bacc("TRN2", target_bir_lowering=False, num_devices=1)
    arrays, args = {}, []
    consts = constants()
    for name in _INS + list(consts):
        a = _np.ascontiguousarray(consts[name] if name in consts else inputs[name])
        arrays[f"in_{name}"] = a
        args.append(nc.dram_tensor(f"in_{name}", a.shape, _mybir.dt.from_np(a.dtype), kind="ExternalInput").ap())
    args.append(nc.dram_tensor("out_0", (1, T, D), _mybir.dt.float32, kind="ExternalOutput").ap())
    build(nc, *args)
    r = _run(nc, [arrays], core_ids=[0])
    return r.results[0]["out_0"]
```
